# Optimizing a Trainium2 kernel written in Bass

```python
import math
import jax, jax.numpy as jnp
from jax import lax
import numpy as np

D_MODEL = 1024
BATCH = 1
SEQ = 512
DEPTH = 2

ATT_HEADS = 8
ATT_HEAD_DIM = 64
ATT_WIDTH = ATT_HEADS * ATT_HEAD_DIM
DILATED_PATTERNS = ((128, 1), (512, 4), (2048, 16))
ATT_BLOCK = 128
ROPE_THETA = 500000.0
ROPE_DIM = ATT_HEAD_DIM // 4

MLSTM_HEADS = 4
MLSTM_HEAD_DIM = 128
MLSTM_WIDTH = MLSTM_HEADS * MLSTM_HEAD_DIM
MLSTM_CHUNK = 64
CONV_WIDTH = 4
FORGET_BIAS = 3.0

D_FF = 4 * D_MODEL
NORM_EPS = 1e-6

COL_AQ = 0
COL_AK = COL_AQ + ATT_WIDTH
COL_AV = COL_AK + ATT_WIDTH
COL_MQ = COL_AV + ATT_WIDTH
COL_MK = COL_MQ + MLSTM_WIDTH
COL_MV = COL_MK + MLSTM_WIDTH
COL_MO = COL_MV + MLSTM_WIDTH
COL_MI = COL_MO + MLSTM_WIDTH
COL_MF = COL_MI + MLSTM_HEADS
COL_GA = COL_MF + MLSTM_HEADS
COL_GB = COL_GA + D_MODEL
D_IN = COL_GB + D_MODEL


def rms_norm(x, w):
    xf = x.astype(jnp.float32)
    y = xf * lax.rsqrt(jnp.mean(xf * xf, axis=-1, keepdims=True) + NORM_EPS)
    return (y * w.astype(jnp.float32)).astype(x.dtype)

def rope_tables(positions):
    inv_freq = ROPE_THETA ** (-jnp.arange(0, ROPE_DIM, 2, dtype=jnp.float32) / ROPE_DIM)
    ang = positions.astype(jnp.float32)[..., None] * inv_freq
    return jnp.cos(ang)[:, :, None, :], jnp.sin(ang)[:, :, None, :]

def apply_partial_rope(t, cos, sin):
    half = ROPE_DIM // 2
    t1 = t[..., :half]
    t2 = t[..., half:ROPE_DIM]
    return jnp.concatenate([t1 * cos - t2 * sin, t2 * cos + t1 * sin, t[..., ROPE_DIM:]], axis=-1)

def dilated_window_attention(q, k, v, window, dilation):
    B, S, H, Dh = q.shape
    span = window // dilation
    L = S // dilation
    nb = -(-L // ATT_BLOCK)
    Lp = nb * ATT_BLOCK
    BD = B * dilation

    def to_sub(t):
        return t.reshape(B, L, dilation, H, Dh).transpose(0, 2, 1, 3, 4).reshape(BD, L, H, Dh)

    qs, ks, vs = to_sub(q), to_sub(k), to_sub(v)
    qb = jnp.pad(qs, ((0, 0), (0, Lp - L), (0, 0), (0, 0))).reshape(BD, nb, ATT_BLOCK, H, Dh)

    def key_blocks(t):
        tp = jnp.pad(t, ((0, 0), (ATT_BLOCK, Lp - L), (0, 0), (0, 0)))
        tp = tp.reshape(BD, nb + 1, ATT_BLOCK, H, Dh)
        return jnp.concatenate([tp[:, :-1], tp[:, 1:]], axis=2)

    kb, vb = key_blocks(ks), key_blocks(vs)
    blk = jnp.arange(nb)[:, None, None]
    qa = jnp.arange(ATT_BLOCK)[None, :, None]
    kc = jnp.arange(2 * ATT_BLOCK)[None, None, :]
    dist = qa + ATT_BLOCK - kc
    key_idx = blk * ATT_BLOCK - ATT_BLOCK + kc
    mask = (dist >= 0) & (dist <= span) & (key_idx >= 0)

    s = jnp.einsum('bnqhd,bnkhd->bnhqk', qb, kb) * (Dh ** -0.5)
    s = jnp.where(mask[None, :, None], s, -jnp.inf)
    m = jnp.max(s, axis=-1, keepdims=True)
    p = jnp.exp(s - m)
    l = jnp.sum(p, axis=-1)
    o = jnp.einsum('bnhqk,bnkhd->bnqhd', p, vb) / jnp.transpose(l, (0, 1, 3, 2))[..., None]
    lse = jnp.transpose(m[..., 0] + jnp.log(l), (0, 1, 3, 2))

    o = o.reshape(BD, Lp, H, Dh)[:, :L].reshape(B, dilation, L, H, Dh)
    o = o.transpose(0, 2, 1, 3, 4).reshape(B, S, H, Dh)
    lse = lse.reshape(BD, Lp, H)[:, :L].reshape(B, dilation, L, H)
    lse = lse.transpose(0, 2, 1, 3).reshape(B, S, H)
    return o, lse

def dilated_mixture_attention(q, k, v):
    outs, lses = [], []
    for window, dilation in DILATED_PATTERNS:
        o, lse = dilated_window_attention(q, k, v, window, dilation)
        outs.append(o)
        lses.append(lse)
    wts = jax.nn.softmax(jnp.stack(lses), axis=0)
    return jnp.einsum('gbsh,gbshd->bshd', wts, jnp.stack(outs))

def causal_short_conv(u, w, b):
    S = u.shape[1]
    up = jnp.pad(u, ((0, 0), (CONV_WIDTH - 1, 0), (0, 0)))
    out = b
    for j in range(CONV_WIDTH):
        out = out + w[j] * up[:, j:j + S]
    return out

def mlstm_chunkwise(q, k, v, ig, fg):
    B, S, H, D = q.shape
    L = MLSTM_CHUNK
    NC = S // L

    def chunks(t):
        return t.reshape(B, NC, L, H, D).transpose(0, 3, 1, 2, 4)

    def gchunks(t):
        return t.reshape(B, NC, L, H).transpose(0, 3, 1, 2)

    q = chunks(q) * (D ** -0.5)
    k = chunks(k)
    v = chunks(v)
    ig = gchunks(ig)
    lf = gchunks(jax.nn.log_sigmoid(fg))
    bcum = jnp.cumsum(lf, axis=-1)
    g = bcum[..., -1]

    a = g[..., None] - bcum + ig
    m_loc = jnp.max(a, axis=-1)
    wk = jnp.exp(a - m_loc[..., None])
    kv_c = jnp.einsum('bhcl,bhclk,bhclv->bhckv', wk, k, v)
    n_c = jnp.einsum('bhcl,bhclk->bhck', wk, k)

    def step(carry, xs):
        C, n, m = carry
        g_c, ml, kv, nn = xs
        m_new = jnp.maximum(g_c + m, ml)
        decay = jnp.exp(g_c + m - m_new)
        inj = jnp.exp(ml - m_new)
        C_new = decay[..., None, None] * C + inj[..., None, None] * kv
        n_new = decay[..., None] * n + inj[..., None] * nn
        return (C_new, n_new, m_new), (C, n, m)

    init = (jnp.zeros((B, H, D, D), jnp.float32), jnp.zeros((B, H, D), jnp.float32),
            jnp.zeros((B, H), jnp.float32))
    xs = (g.transpose(2, 0, 1), m_loc.transpose(2, 0, 1),
          kv_c.transpose(2, 0, 1, 3, 4), n_c.transpose(2, 0, 1, 3))
    _, (C_prev, n_prev, m_prev) = lax.scan(step, init, xs)
    C_prev = C_prev.transpose(1, 2, 0, 3, 4)
    n_prev = n_prev.transpose(1, 2, 0, 3)
    m_prev = m_prev.transpose(1, 2, 0)

    causal = jnp.tril(jnp.ones((L, L), dtype=bool))
    dmat = bcum[..., :, None] - bcum[..., None, :] + ig[..., None, :]
    dmat = jnp.where(causal, dmat, -jnp.inf)
    m_inter = bcum + m_prev[..., None]
    m_t = jnp.maximum(jnp.max(dmat, axis=-1), m_inter)
    p = jnp.exp(dmat - m_t[..., None]) * jnp.einsum('bhcld,bhcsd->bhcls', q, k)
    w_inter = jnp.exp(m_inter - m_t)
    num = (w_inter[..., None] * jnp.einsum('bhcld,bhcdv->bhclv', q, C_prev)
           + jnp.einsum('bhcls,bhcsv->bhclv', p, v))
    den = w_inter * jnp.einsum('bhcld,bhcd->bhcl', q, n_prev) + jnp.sum(p, axis=-1)
    h = num / jnp.maximum(jnp.abs(den), jnp.exp(-m_t))[..., None]
    return h.transpose(0, 2, 3, 1, 4).reshape(B, S, H, D)

def hybrid_layer(x, cos, sin, norm_mix_w, w_in, b_in, conv_w, conv_b, mlstm_norm_w,
                 w_proj_att, w_proj_mlstm, w_out, norm_mlp_w, w_ff1, w_ff2):
    B, S, _ = x.shape
    f32 = jnp.float32
    h = rms_norm(x, norm_mix_w)
    z = h @ w_in + b_in

    aq = z[..., COL_AQ:COL_AK].astype(f32).reshape(B, S, ATT_HEADS, ATT_HEAD_DIM)
    ak = z[..., COL_AK:COL_AV].astype(f32).reshape(B, S, ATT_HEADS, ATT_HEAD_DIM)
    av = z[..., COL_AV:COL_MQ].astype(f32).reshape(B, S, ATT_HEADS, ATT_HEAD_DIM)
    aq = apply_partial_rope(aq, cos, sin)
    ak = apply_partial_rope(ak, cos, sin)
    ya = dilated_mixture_attention(aq, ak, av).reshape(B, S, ATT_WIDTH).astype(x.dtype)

    qk = jax.nn.silu(causal_short_conv(z[..., COL_MQ:COL_MV].astype(f32),
                                       conv_w.astype(f32), conv_b.astype(f32)))
    mq = qk[..., :MLSTM_WIDTH].reshape(B, S, MLSTM_HEADS, MLSTM_HEAD_DIM)
    mk = qk[..., MLSTM_WIDTH:].reshape(B, S, MLSTM_HEADS, MLSTM_HEAD_DIM)
    mv = z[..., COL_MV:COL_MO].astype(f32).reshape(B, S, MLSTM_HEADS, MLSTM_HEAD_DIM)
    mi = z[..., COL_MI:COL_MF].astype(f32)
    mf = z[..., COL_MF:COL_GA].astype(f32)
    hm = mlstm_chunkwise(mq, mk, mv, mi, mf)
    hm = hm * lax.rsqrt(jnp.mean(hm * hm, axis=-1, keepdims=True) + NORM_EPS)
    hm = hm.reshape(B, S, MLSTM_WIDTH) * mlstm_norm_w.astype(f32)
    yb = (jax.nn.sigmoid(z[..., COL_MO:COL_MI].astype(f32)) * hm).astype(x.dtype)

    ga = jax.nn.sigmoid(z[..., COL_GA:COL_GB])
    gb = jax.nn.sigmoid(z[..., COL_GB:D_IN])
    mixed = ga * (ya @ w_proj_att) + gb * (yb @ w_proj_mlstm)
    x = x + mixed @ w_out

    h2 = rms_norm(x, norm_mlp_w)
    x = x + jnp.square(jax.nn.relu(h2 @ w_ff1)) @ w_ff2
    return x

def first_inputs(seed: int = 0) -> dict:
    key = jax.random.key(seed)
    ks = jax.random.split(key, 16)
    nrm = jax.random.normal
    x = nrm(ks[0], (BATCH, SEQ, D_MODEL), jnp.float32)
    offsets = jax.random.randint(ks[1], (BATCH, 1), 0, 1024, dtype=jnp.int32)
    positions = offsets + jnp.arange(SEQ, dtype=jnp.int32)[None, :]
    norm_mix_w = 1.0 + 0.05 * nrm(ks[2], (DEPTH, D_MODEL), jnp.float32)
    w_in = nrm(ks[3], (DEPTH, D_MODEL, D_IN), jnp.float32) * D_MODEL ** -0.5
    b_in = 0.02 * nrm(ks[4], (DEPTH, D_IN), jnp.float32)
    b_in = b_in.at[:, COL_MF:COL_GA].add(FORGET_BIAS)
    conv_w = nrm(ks[5], (DEPTH, CONV_WIDTH, 2 * MLSTM_WIDTH), jnp.float32) * CONV_WIDTH ** -0.5
    conv_b = 0.02 * nrm(ks[6], (DEPTH, 2 * MLSTM_WIDTH), jnp.float32)
    mlstm_norm_w = 1.0 + 0.05 * nrm(ks[7], (DEPTH, MLSTM_WIDTH), jnp.float32)
    w_proj_att = nrm(ks[8], (DEPTH, ATT_WIDTH, D_MODEL), jnp.float32) * ATT_WIDTH ** -0.5
    w_proj_mlstm = nrm(ks[9], (DEPTH, MLSTM_WIDTH, D_MODEL), jnp.float32) * MLSTM_WIDTH ** -0.5
    w_out = nrm(ks[10], (DEPTH, D_MODEL, D_MODEL), jnp.float32) * D_MODEL ** -0.5
    norm_mlp_w = 1.0 + 0.05 * nrm(ks[11], (DEPTH, D_MODEL), jnp.float32)
    w_ff1 = nrm(ks[12], (DEPTH, D_MODEL, D_FF), jnp.float32) * D_MODEL ** -0.5
    w_ff2 = nrm(ks[13], (DEPTH, D_FF, D_MODEL), jnp.float32) * (0.5 * D_FF ** -0.5)
    final_norm_w = 1.0 + 0.05 * nrm(ks[14], (D_MODEL,), jnp.float32)
    return {"x": x, "positions": positions, "norm_mix_w": norm_mix_w, "w_in": w_in,
            "b_in": b_in, "conv_w": conv_w, "conv_b": conv_b, "mlstm_norm_w": mlstm_norm_w,
            "w_proj_att": w_proj_att, "w_proj_mlstm": w_proj_mlstm, "w_out": w_out,
            "norm_mlp_w": norm_mlp_w, "w_ff1": w_ff1, "w_ff2": w_ff2,
            "final_norm_w": final_norm_w}

def first_block(x, positions, norm_mix_w, w_in, b_in, conv_w, conv_b, mlstm_norm_w,
              w_proj_att, w_proj_mlstm, w_out, norm_mlp_w, w_ff1, w_ff2, final_norm_w):
    cos, sin = rope_tables(positions)
    for l in range(DEPTH):
        x = hybrid_layer(x, cos, sin, norm_mix_w[l], w_in[l], b_in[l], conv_w[l], conv_b[l],
                         mlstm_norm_w[l], w_proj_att[l], w_proj_mlstm[l], w_out[l],
                         norm_mlp_w[l], w_ff1[l], w_ff2[l])
    return rms_norm(x, final_norm_w)


GRID_W = 64
CTX_LEN = 256
N_MIXERS = 4
Q_BLOCK = 128
ROPE_BASE = 10000.0
EPS = 1e-6
F32 = jnp.float32

MLA_HEADS = 16
MLA_Q_RANK = 384
MLA_KV_RANK = 256
MLA_NOPE = 64
MLA_ROPE = 32
MLA_V = 64
MLA_WIDTH = MLA_HEADS * MLA_V

GLA_HEADS = 4
GLA_DK = D_MODEL // 2
GLA_DV = D_MODEL
GLA_GATE_RANK = 16
GLA_GATE_NORM = 16.0
GLA_CHUNK = 64

GQA_HEADS = 16
GQA_KV_HEADS = 4
GQA_HEAD_DIM = 64
GQA_WIDTH = GQA_HEADS * GQA_HEAD_DIM

SSD_INNER = 2 * D_MODEL
SSD_HEAD_DIM = 64
SSD_HEADS = SSD_INNER // SSD_HEAD_DIM
SSD_GROUPS = 4
SSD_STATE = 128
SSD_CONV = 5
SSD_CHUNK = 64
SSD_XBC = SSD_INNER + 2 * SSD_GROUPS * SSD_STATE


def _n_layers_of(kind):
    return len(range(kind, DEPTH, N_MIXERS))

def split_last(t, sizes):
    idx = [int(v) for v in np.cumsum(sizes)[:-1]]
    return jnp.split(t, idx, axis=-1)

def rms_norm_2(x, g, eps=EPS):
    xf = x.astype(F32)
    y = xf * lax.rsqrt(jnp.mean(xf * xf, axis=-1, keepdims=True) + eps)
    return (y * g.astype(F32)).astype(x.dtype)

def grid_positions(n):
    rows = n // GRID_W
    row = jnp.repeat(jnp.arange(rows, dtype=jnp.int32), GRID_W)
    col = jnp.tile(jnp.arange(GRID_W, dtype=jnp.int32), rows)
    return row, col

def _rope_1d(x, pos):
    half = x.shape[-1] // 2
    inv = ROPE_BASE ** (-jnp.arange(half, dtype=F32) / half)
    ang = pos.astype(F32)[:, None] * inv[None, :]
    cos = jnp.cos(ang)[:, None, :]
    sin = jnp.sin(ang)[:, None, :]
    xf = x.astype(F32)
    x1, x2 = xf[..., :half], xf[..., half:]
    return jnp.concatenate([x1 * cos - x2 * sin, x2 * cos + x1 * sin], axis=-1).astype(x.dtype)

def axial_rope(x, row, col):
    d = x.shape[-1] // 2
    return jnp.concatenate([_rope_1d(x[..., :d], row), _rope_1d(x[..., d:], col)], axis=-1)

def attention_blocks(q, k, v):
    b, lq, h, dk = q.shape
    hkv = k.shape[2]
    rep = h // hkv
    dv = v.shape[-1]
    scale = dk ** -0.5
    blk = min(Q_BLOCK, lq)
    nb = lq // blk
    qb = jnp.moveaxis(q.reshape(b, nb, blk, hkv, rep, dk), 1, 0)

    def one_block(qi):
        s = jnp.einsum('bqhrd,bkhd->bhrqk', qi, k, preferred_element_type=F32) * scale
        p = jax.nn.softmax(s, axis=-1).astype(v.dtype)
        return jnp.einsum('bhrqk,bkhe->bqhre', p, v)

    o = lax.map(one_block, qb)
    return jnp.moveaxis(o, 0, 1).reshape(b, lq, h, dv)

def modulation(cond, w, bias):
    m = jax.nn.silu(cond) @ w + bias
    return jnp.split(m, 3, axis=-1)

def mla_mixer(hc, hx, row, col, w_in, q_norm_g, w_uq, kv_norm_g, w_ukv, w_out):
    def project(h, rotate):
        b, n, _ = h.shape
        cq, ckv, kr, gate = split_last(h @ w_in, (MLA_Q_RANK, MLA_KV_RANK, MLA_ROPE, MLA_WIDTH))
        q = (rms_norm_2(cq, q_norm_g) @ w_uq).reshape(b, n, MLA_HEADS, MLA_NOPE + MLA_ROPE)
        kv = (rms_norm_2(ckv, kv_norm_g) @ w_ukv).reshape(b, n, MLA_HEADS, MLA_NOPE + MLA_V)
        q_nope, q_rope = q[..., :MLA_NOPE], q[..., MLA_NOPE:]
        k_nope, v = kv[..., :MLA_NOPE], kv[..., MLA_NOPE:]
        kr = kr[:, :, None, :]
        if rotate:
            q_rope = axial_rope(q_rope, row, col)
            kr = axial_rope(kr, row, col)
        k = jnp.concatenate([k_nope, jnp.broadcast_to(kr, (b, n, MLA_HEADS, MLA_ROPE))], axis=-1)
        q = jnp.concatenate([q_nope, q_rope], axis=-1)
        return q, k, v, gate

    qc, kc, vc, gc = project(hc, False)
    qx, kx, vx, gx = project(hx, True)
    oc = attention_blocks(qc, kc, vc)
    ox = attention_blocks(qx, jnp.concatenate([kc, kx], axis=1), jnp.concatenate([vc, vx], axis=1))

    def out(o, gate):
        b, n = gate.shape[:2]
        return (o.reshape(b, n, MLA_WIDTH) * jax.nn.silu(gate)) @ w_out

    return out(oc, gc), out(ox, gx)

def gla_chunk_scan(q, k, v, g, s0):
    b, l, h, dk = q.shape
    dv = v.shape[-1]
    c = GLA_CHUNK
    nc = l // c
    causal = jnp.tril(jnp.ones((c, c), dtype=bool))

    def to_chunks(t):
        return t.astype(F32).reshape(b, nc, c, h, t.shape[-1]).transpose(1, 0, 3, 2, 4)

    def step(s, inp):
        qc, kc, vc, gc = inp
        bc = jnp.cumsum(gc, axis=2)
        o_inter = jnp.einsum('bhcd,bhde->bhce', qc * jnp.exp(bc), s)
        diff = bc[:, :, :, None, :] - bc[:, :, None, :, :]
        decay = jnp.exp(jnp.where(causal[:, :, None], diff, -jnp.inf))
        a = jnp.einsum('bhid,bhijd->bhij', qc, kc[:, :, None, :, :] * decay)
        o = o_inter + jnp.einsum('bhij,bhje->bhie', a, vc)
        blast = bc[:, :, -1:, :]
        s_new = jnp.exp(blast[:, :, 0, :])[..., None] * s + jnp.einsum('bhcd,bhce->bhde', kc * jnp.exp(blast - bc), vc)
        return s_new, o

    s, o = lax.scan(step, s0, (to_chunks(q), to_chunks(k), to_chunks(v), to_chunks(g)))
    o = o.transpose(1, 0, 3, 2, 4).reshape(b, l, h, dv)
    return o, s

def gla_bidirectional(q, k, v, gf, gb, s0f, s0b):
    flip = lambda t: t[:, ::-1]
    of, sf = gla_chunk_scan(q, k, v, gf, s0f)
    ob, sb = gla_chunk_scan(flip(q), flip(k), flip(v), flip(gb), s0b)
    return of + flip(ob), sf, sb

def gla_mixer(hc, hx, w_in, w_gf, b_gf, w_gb, b_gb, o_norm_g, w_out):
    dk = GLA_DK // GLA_HEADS
    dv = GLA_DV // GLA_HEADS
    sizes = (GLA_DK, GLA_DK, GLA_DV, GLA_DV, GLA_GATE_RANK, GLA_GATE_RANK)

    def project(h):
        b, n, _ = h.shape
        q, k, v, gate, rf, rb = split_last(h @ w_in, sizes)
        heads = lambda t, d: t.reshape(b, n, GLA_HEADS, d)
        gf = jax.nn.log_sigmoid((rf @ w_gf + b_gf).astype(F32)) / GLA_GATE_NORM
        gb = jax.nn.log_sigmoid((rb @ w_gb + b_gb).astype(F32)) / GLA_GATE_NORM
        return heads(q, dk) * (dk ** -0.5), heads(k, dk), heads(v, dv), heads(gf, dk), heads(gb, dk), gate

    qc, kc, vc, gfc, gbc, gatec = project(hc)
    qx, kx, vx, gfx, gbx, gatex = project(hx)
    s0 = jnp.zeros((hc.shape[0], GLA_HEADS, dk, dv), F32)
    oc, sf, sb = gla_bidirectional(qc, kc, vc, gfc, gbc, s0, s0)
    ox, _, _ = gla_bidirectional(qx, kx, vx, gfx, gbx, sf, sb)

    def out(o, gate):
        b, n = gate.shape[:2]
        o = rms_norm_2(o.astype(gate.dtype), o_norm_g).reshape(b, n, GLA_DV)
        return (o * jax.nn.silu(gate)) @ w_out

    return out(oc, gatec), out(ox, gatex)

def gqa_mixer(hc, hx, row, col, w_in, q_norm_g, k_norm_g, w_out):
    kvw = GQA_KV_HEADS * GQA_HEAD_DIM

    def project(h, rotate):
        b, n, _ = h.shape
        q, k, v, gate = split_last(h @ w_in, (GQA_WIDTH, kvw, kvw, GQA_WIDTH))
        q = rms_norm_2(q.reshape(b, n, GQA_HEADS, GQA_HEAD_DIM), q_norm_g)
        k = rms_norm_2(k.reshape(b, n, GQA_KV_HEADS, GQA_HEAD_DIM), k_norm_g)
        v = v.reshape(b, n, GQA_KV_HEADS, GQA_HEAD_DIM)
        if rotate:
            q = axial_rope(q, row, col)
            k = axial_rope(k, row, col)
        return q, k, v, gate

    qc, kc, vc, gc = project(hc, False)
    qx, kx, vx, gx = project(hx, True)
    oc = attention_blocks(qc, kc, vc)
    ox = attention_blocks(qx, jnp.concatenate([kc, kx], axis=1), jnp.concatenate([vc, vx], axis=1))

    def out(o, gate):
        b, n = gate.shape[:2]
        return (o.reshape(b, n, GQA_WIDTH) * jax.nn.silu(gate)) @ w_out

    return out(oc, gc), out(ox, gx)

def dwconv_centred(u, w, bias):
    kw = w.shape[0]
    pad = kw // 2
    out = lax.conv_general_dilated(u, w[:, None, :], window_strides=(1,), padding=[(pad, kw - 1 - pad)],
                                   dimension_numbers=('NWC', 'WIO', 'NWC'), feature_group_count=u.shape[-1])
    return out + bias

def ssd_chunk_scan(x, dt, a, bm, cm, h0):
    b, l, h, p = x.shape
    g, n = bm.shape[2], bm.shape[3]
    rep = h // g
    c = SSD_CHUNK
    nc = l // c
    causal = jnp.tril(jnp.ones((c, c), dtype=bool))

    def to_chunks(t):
        return jnp.swapaxes(t.astype(F32).reshape(b, nc, c, *t.shape[2:]), 0, 1)

    def step(hs, inp):
        xc, dtc, bc, cc = inp
        la = jnp.cumsum(dtc * a, axis=1)
        xg = (xc * dtc[..., None]).reshape(b, c, g, rep, p)
        hg = hs.reshape(b, g, rep, p, n)
        y_inter = jnp.einsum('bcgn,bgrpn->bcgrp', cc, hg) * jnp.exp(la).reshape(b, c, g, rep)[..., None]
        diff = la[:, :, None, :] - la[:, None, :, :]
        lmat = jnp.exp(jnp.where(causal[None, :, :, None], diff, -jnp.inf)).reshape(b, c, c, g, rep)
        cb = jnp.einsum('bign,bjgn->bijg', cc, bc)
        y_intra = jnp.einsum('bijgr,bjgrp->bigrp', cb[..., None] * lmat, xg)
        dlast = jnp.exp(la[:, -1:, :] - la).reshape(b, c, g, rep)
        h_new = jnp.exp(la[:, -1, :]).reshape(b, g, rep)[..., None, None] * hg + \
            jnp.einsum('bcgrp,bcgn->bgrpn', dlast[..., None] * xg, bc)
        return h_new.reshape(b, h, p, n), (y_inter + y_intra).reshape(b, c, h, p)

    hs, y = lax.scan(step, h0, (to_chunks(x), to_chunks(dt), to_chunks(bm), to_chunks(cm)))
    return jnp.swapaxes(y, 0, 1).reshape(b, l, h, p), hs

def ssd_bidirectional(x, dtf, dtb, af, ab, bm, cm, h0f, h0b):
    flip = lambda t: t[:, ::-1]
    yf, hf = ssd_chunk_scan(x, dtf, af, bm, cm, h0f)
    yb, hb = ssd_chunk_scan(flip(x), flip(dtb), ab, flip(bm), flip(cm), h0b)
    return yf + flip(yb), hf, hb

def ssd_mixer(hc, hx, w_in, conv_w, conv_b, dt_bias_f, dt_bias_b, a_log_f, a_log_b, d_skip, gnorm_g, w_out):
    af = -jnp.exp(a_log_f.astype(F32))
    ab = -jnp.exp(a_log_b.astype(F32))
    gw = SSD_GROUPS * SSD_STATE

    def project(h):
        b, n, _ = h.shape
        z, xbc, dtf, dtb = split_last(h @ w_in, (SSD_INNER, SSD_XBC, SSD_HEADS, SSD_HEADS))
        xbc = jax.nn.silu(dwconv_centred(xbc, conv_w, conv_b))
        xs, bm, cm = split_last(xbc, (SSD_INNER, gw, gw))
        xs = xs.reshape(b, n, SSD_HEADS, SSD_HEAD_DIM)
        bm = bm.reshape(b, n, SSD_GROUPS, SSD_STATE)
        cm = cm.reshape(b, n, SSD_GROUPS, SSD_STATE)
        dtf = jax.nn.softplus(dtf.astype(F32) + dt_bias_f.astype(F32))
        dtb = jax.nn.softplus(dtb.astype(F32) + dt_bias_b.astype(F32))
        return z, xs, bm, cm, dtf, dtb

    zc, xsc, bmc, cmc, dtfc, dtbc = project(hc)
    zx, xsx, bmx, cmx, dtfx, dtbx = project(hx)
    h0 = jnp.zeros((hc.shape[0], SSD_HEADS, SSD_HEAD_DIM, SSD_STATE), F32)
    yc, hf, hb = ssd_bidirectional(xsc, dtfc, dtbc, af, ab, bmc, cmc, h0, h0)
    yx, _, _ = ssd_bidirectional(xsx, dtfx, dtbx, af, ab, bmx, cmx, hf, hb)

    def out(y, xs, z):
        b, n = z.shape[:2]
        y = y.astype(z.dtype) + xs * d_skip[:, None]
        y = y.reshape(b, n, SSD_INNER) * jax.nn.silu(z)
        y = rms_norm_2(y.reshape(b, n, SSD_GROUPS, SSD_INNER // SSD_GROUPS),
                     gnorm_g.reshape(SSD_GROUPS, SSD_INNER // SSD_GROUPS)).reshape(b, n, SSD_INNER)
        return y @ w_out

    return out(yc, xsc, zc), out(yx, xsx, zx)

def second_inputs(seed: int = 0) -> dict:
    key = jax.random.key(seed)
    ks = iter(jax.random.split(key, 64))
    nA, nB, nC, nD = (_n_layers_of(t) for t in range(N_MIXERS))

    def nrm(shape, fan_in, scale=1.0):
        return jax.random.normal(next(ks), shape, F32) * (scale * fan_in ** -0.5)

    def gain(shape):
        return 1.0 + 0.05 * jax.random.normal(next(ks), shape, F32)

    def small(shape, s=0.02):
        return s * jax.random.normal(next(ks), shape, F32)

    def dt_bias(shape):
        u = jax.random.uniform(next(ks), shape, F32)
        dt = jnp.exp(u * (math.log(0.1) - math.log(0.001)) + math.log(0.001))
        dt = jnp.maximum(dt, 1e-4)
        return dt + jnp.log(-jnp.expm1(-dt))

    def a_log(shape):
        return jnp.log(jax.random.uniform(next(ks), shape, F32, 1.0, 16.0))

    D = D_MODEL
    mla_in = MLA_Q_RANK + MLA_KV_RANK + MLA_ROPE + MLA_WIDTH
    gla_in = 2 * GLA_DK + 2 * GLA_DV + 2 * GLA_GATE_RANK
    gqa_in = 2 * GQA_WIDTH + 2 * GQA_KV_HEADS * GQA_HEAD_DIM
    ssd_in = SSD_INNER + SSD_XBC + 2 * SSD_HEADS
    return {
        "x": jax.random.normal(next(ks), (BATCH, SEQ, D), F32),
        "c": jax.random.normal(next(ks), (BATCH, D), F32),
        "ctx": jax.random.normal(next(ks), (BATCH, CTX_LEN, D), F32),
        "c_ctx": jax.random.normal(next(ks), (D,), F32),
        "ada_w": nrm((DEPTH, D, 3 * D), D, 0.5),
        "ada_b": small((DEPTH, 3 * D)),
        "norm_g": gain((DEPTH, D)),
        "final_g": gain((D,)),
        "mla_w_in": nrm((nA, D, mla_in), D),
        "mla_q_norm": gain((nA, MLA_Q_RANK)),
        "mla_w_uq": nrm((nA, MLA_Q_RANK, MLA_HEADS * (MLA_NOPE + MLA_ROPE)), MLA_Q_RANK),
        "mla_kv_norm": gain((nA, MLA_KV_RANK)),
        "mla_w_ukv": nrm((nA, MLA_KV_RANK, MLA_HEADS * (MLA_NOPE + MLA_V)), MLA_KV_RANK),
        "mla_w_out": nrm((nA, MLA_WIDTH, D), MLA_WIDTH),
        "gla_w_in": nrm((nB, D, gla_in), D),
        "gla_w_gf": nrm((nB, GLA_GATE_RANK, GLA_DK), GLA_GATE_RANK),
        "gla_b_gf": small((nB, GLA_DK), 0.1),
        "gla_w_gb": nrm((nB, GLA_GATE_RANK, GLA_DK), GLA_GATE_RANK),
        "gla_b_gb": small((nB, GLA_DK), 0.1),
        "gla_o_norm": gain((nB, GLA_DV // GLA_HEADS)),
        "gla_w_out": nrm((nB, GLA_DV, D), GLA_DV),
        "gqa_w_in": nrm((nC, D, gqa_in), D),
        "gqa_q_norm": gain((nC, GQA_HEAD_DIM)),
        "gqa_k_norm": gain((nC, GQA_HEAD_DIM)),
        "gqa_w_out": nrm((nC, GQA_WIDTH, D), GQA_WIDTH),
        "ssd_w_in": nrm((nD, D, ssd_in), D),
        "ssd_conv_w": nrm((nD, SSD_CONV, SSD_XBC), SSD_CONV),
        "ssd_conv_b": small((nD, SSD_XBC)),
        "ssd_dt_bias_f": dt_bias((nD, SSD_HEADS)),
        "ssd_dt_bias_b": dt_bias((nD, SSD_HEADS)),
        "ssd_a_log_f": a_log((nD, SSD_HEADS)),
        "ssd_a_log_b": a_log((nD, SSD_HEADS)),
        "ssd_d": gain((nD, SSD_HEADS)),
        "ssd_norm": gain((nD, SSD_INNER)),
        "ssd_w_out": nrm((nD, SSD_INNER, D), SSD_INNER),
    }

def second_block(x, c, ctx, c_ctx, ada_w, ada_b, norm_g, final_g,
              mla_w_in, mla_q_norm, mla_w_uq, mla_kv_norm, mla_w_ukv, mla_w_out,
              gla_w_in, gla_w_gf, gla_b_gf, gla_w_gb, gla_b_gb, gla_o_norm, gla_w_out,
              gqa_w_in, gqa_q_norm, gqa_k_norm, gqa_w_out,
              ssd_w_in, ssd_conv_w, ssd_conv_b, ssd_dt_bias_f, ssd_dt_bias_b,
              ssd_a_log_f, ssd_a_log_b, ssd_d, ssd_norm, ssd_w_out):
    row, col = grid_positions(x.shape[1])
    for i in range(DEPTH):
        kind, j = i % N_MIXERS, i // N_MIXERS
        sx, scx, gx = (m[:, None, :] for m in modulation(c, ada_w[i], ada_b[i]))
        sc, scc, gc = modulation(c_ctx, ada_w[i], ada_b[i])
        hx = rms_norm_2(x, norm_g[i]) * (1 + scx) + sx
        hc = rms_norm_2(ctx, norm_g[i]) * (1 + scc) + sc
        if kind == 0:
            yc, yx = mla_mixer(hc, hx, row, col, mla_w_in[j], mla_q_norm[j], mla_w_uq[j],
                               mla_kv_norm[j], mla_w_ukv[j], mla_w_out[j])
        elif kind == 1:
            yc, yx = gla_mixer(hc, hx, gla_w_in[j], gla_w_gf[j], gla_b_gf[j], gla_w_gb[j], gla_b_gb[j],
                               gla_o_norm[j], gla_w_out[j])
        elif kind == 2:
            yc, yx = gqa_mixer(hc, hx, row, col, gqa_w_in[j], gqa_q_norm[j], gqa_k_norm[j], gqa_w_out[j])
        else:
            yc, yx = ssd_mixer(hc, hx, ssd_w_in[j], ssd_conv_w[j], ssd_conv_b[j], ssd_dt_bias_f[j],
                               ssd_dt_bias_b[j], ssd_a_log_f[j], ssd_a_log_b[j], ssd_d[j], ssd_norm[j],
                               ssd_w_out[j])
        x = x + gx * yx
        if i < DEPTH - 1:
            ctx = ctx + gc * yc
    return rms_norm_2(x, final_g)


def setup_inputs(seed=0):
    out = dict(first_inputs(seed))
    for name, value in second_inputs(seed + 1).items():
        if name != "x":
            out[name + "_2"] = value
    return out


def reference(
    x, positions, norm_mix_w, w_in, b_in, conv_w, conv_b, mlstm_norm_w, w_proj_att,
    w_proj_mlstm, w_out, norm_mlp_w, w_ff1, w_ff2, final_norm_w, c_2, ctx_2, c_ctx_2, ada_w_2,
    ada_b_2, norm_g_2, final_g_2, mla_w_in_2, mla_q_norm_2, mla_w_uq_2, mla_kv_norm_2,
    mla_w_ukv_2, mla_w_out_2, gla_w_in_2, gla_w_gf_2, gla_b_gf_2, gla_w_gb_2, gla_b_gb_2,
    gla_o_norm_2, gla_w_out_2, gqa_w_in_2, gqa_q_norm_2, gqa_k_norm_2, gqa_w_out_2, ssd_w_in_2,
    ssd_conv_w_2, ssd_conv_b_2, ssd_dt_bias_f_2, ssd_dt_bias_b_2, ssd_a_log_f_2, ssd_a_log_b_2,
    ssd_d_2, ssd_norm_2, ssd_w_out_2,
):
    x = first_block(
        x, positions, norm_mix_w, w_in, b_in, conv_w, conv_b, mlstm_norm_w, w_proj_att,
        w_proj_mlstm, w_out, norm_mlp_w, w_ff1, w_ff2, final_norm_w,
    )
    return second_block(
        x, c_2, ctx_2, c_ctx_2, ada_w_2, ada_b_2, norm_g_2, final_g_2, mla_w_in_2, mla_q_norm_2,
        mla_w_uq_2, mla_kv_norm_2, mla_w_ukv_2, mla_w_out_2, gla_w_in_2, gla_w_gf_2, gla_b_gf_2,
        gla_w_gb_2, gla_b_gb_2, gla_o_norm_2, gla_w_out_2, gqa_w_in_2, gqa_q_norm_2,
        gqa_k_norm_2, gqa_w_out_2, ssd_w_in_2, ssd_conv_w_2, ssd_conv_b_2, ssd_dt_bias_f_2,
        ssd_dt_bias_b_2, ssd_a_log_f_2, ssd_a_log_b_2, ssd_d_2, ssd_norm_2, ssd_w_out_2,
    )


_drawn_inputs = setup_inputs


def setup_inputs(seed=0):
    import zlib

    import numpy as np

    out = dict(_drawn_inputs(seed))
    spreads = {}
    factors = {'conv_b': 5.617,
     'mlstm_norm_w': 2.667,
     'ada_b_2': 2.739,
     'mla_q_norm_2': 8.0,
     'mla_w_uq_2': 3.212,
     'mla_kv_norm_2': 8.0,
     'gla_b_gf_2': 6.236,
     'gla_b_gb_2': 7.545,
     'gla_o_norm_2': 5.84}
    for name, (base, spread) in spreads.items():
        noise = np.random.default_rng([zlib.crc32(name.encode()), seed]).standard_normal(out[name].shape)
        drawn = base * np.exp(spread * noise) if base else spread * noise
        out[name] = __import__('jax').numpy.asarray(drawn.astype(out[name].dtype))
    for name, factor in factors.items():
        out[name] = (out[name] * factor).astype(out[name].dtype)
    return out
```

```python
from contextlib import ExitStack

import numpy as np

import concourse.bass as bass
from concourse import mybir

P = 128
F32 = mybir.dt.float32
F32R = mybir.dt.float32r
I32 = mybir.dt.int32
ALU = mybir.AluOpType
ACT = mybir.ActivationFunctionType
AX_X = mybir.AxisListType.X

SEQ, CTX, DM = 512, 256, 1024
XT, CT, KT = SEQ // P, CTX // P, DM // P
DEPTH = 2
EPS = 1e-6
NEG = -1e30

AH, AHD = 8, 64
MH, MHD = 4, 128
ROPE_HALF = 8
CONV = 4
COL_AQ, COL_AK, COL_AV, COL_MQ, COL_MV, COL_MO, COL_MI, COL_GA, COL_GB, D_IN = (
    0, 512, 1024, 1536, 2560, 3072, 3584, 3592, 4616, 5640)
D_FF = 4096
PATTERNS = ((128, 1), (512, 4), (2048, 16))
ROPE_THETA = 500000.0

LH, NOPE, LROPE, LV = 16, 64, 32, 64
QR, KVR = 384, 256
LAT = QR + KVR + LROPE
GH, GDK, GDV, GRANK = 4, 128, 256, 16
GC = 128
GB = 32
GATE_NORM = 16.0

UNIT = 2048

C_ID, C_ATT, C_TRI, C_UP, C_ONES, C_NSEL, C_SEL2, C_AX, C_INV, C_LOW, C_END = (
    0, 128, 640, 768, 896, 1024, 1536, 1792, 2048, 2056, 2184)


def constants():
    c = np.zeros((P, C_END), np.float32)
    p = np.arange(P)
    c[:, C_ID:C_ID + P] = np.eye(P)
    d = p[:, None] + 3 * P - np.arange(4 * P)[None, :]
    n = sum(((d >= 0) & (d <= w) & (d % s == 0)).astype(np.float64) for w, s in PATTERNS)
    c[:, C_ATT:C_ATT + 512] = np.where(n > 0, np.log(np.maximum(n, 1)) * AHD ** 0.5, NEG)
    c[:, C_TRI:C_TRI + P] = np.where(p[:, None] <= p[None, :], 0.0, NEG)
    c[:, C_UP:C_UP + P] = p[:, None] <= p[None, :]
    c[:, C_LOW:C_LOW + P] = p[:, None] >= p[None, :]
    c[:, C_ONES:C_ONES + P] = 1.0
    for h in range(MH):
        c[h, C_NSEL + h * P:C_NSEL + (h + 1) * P] = -1.0
    for r in range(2):
        c[r, C_SEL2 + r * P:C_SEL2 + (r + 1) * P] = 1.0
    inv = (10000.0 ** (-np.arange(8, dtype=np.float32) / 8)).astype(np.float32)
    tok = np.arange(SEQ)
    for t in range(XT):
        at = C_AX + t * 64
        for half, pos in enumerate((tok // 64, tok % 64)):
            ang = (pos[t * P:(t + 1) * P, None].astype(np.float32) * inv).astype(np.float32)
            co, si = np.cos(ang), np.sin(ang)
            c[:, at + half * 16:at + half * 16 + 16] = np.concatenate([co, co], 1)
            c[:, at + 32 + half * 16:at + 48 + half * 16] = np.concatenate([-si, si], 1)
    c[:, C_INV:C_INV + 8] = (np.float32(ROPE_THETA) ** (-np.arange(0, 16, 2, dtype=np.float32) / 16))
    return c


def _queued(call):
    def queue(self, *args, **kwargs):
        self.calls.append((call, args, kwargs))
    return queue


class Calls:

    def __init__(self):
        self.calls = []

    matmul = _queued(lambda e, a, k: e.matmul(*a, **k))
    transpose = _queued(lambda e, a, k: e.transpose(*a, **k))
    activation = _queued(lambda e, a, k: e.activation(*a, **k))
    tensor_tensor = _queued(lambda e, a, k: e.tensor_tensor(*a, **k))
    tensor_scalar = _queued(lambda e, a, k: e.tensor_scalar(*a, **k))
    scalar_tensor_tensor = _queued(lambda e, a, k: e.scalar_tensor_tensor(*a, **k))
    tensor_tensor_reduce = _queued(lambda e, a, k: e.tensor_tensor_reduce(*a, **k))
    tensor_tensor_scan = _queued(lambda e, a, k: e.tensor_tensor_scan(*a, **k))
    tensor_reduce = _queued(lambda e, a, k: e.tensor_reduce(*a, **k))
    tensor_copy = _queued(lambda e, a, k: e.tensor_copy(*a, **k))
    copy_predicated = _queued(lambda e, a, k: e.copy_predicated(*a, **k))
    reciprocal = _queued(lambda e, a, k: e.reciprocal(*a, **k))
    dma_start = _queued(lambda e, a, k: e.dma_start(*a, **k))
    memset = _queued(lambda e, a, k: e.memset(*a, **k))


def emit(e, queue):
    reached = {}
    for waits, calls, sem, increment in queue:
        for w, value in waits:
            if value > reached.get(w.name, 0):
                e.wait_ge(w, value)
                reached[w.name] = value
        for call, args, kwargs in calls:
            last = call(e, args, kwargs)
        last.then_inc(sem, increment)


class Engine:

    def __init__(self, done, in_order=False):
        self.done, self.in_order = done, in_order
        self.count, self.queue, self.pending = 0, [], []

    def now(self):
        return (self.done, self.count)

    def step(self, issue, after=()):
        waits = list(after) + self.pending
        self.pending = []
        if not self.in_order:
            waits.append(self.now())
        most = {}
        for sem, value in waits:
            if value > most.get(sem.name, (sem, 0))[1]:
                most[sem.name] = (sem, value)
        self.count += 1
        step = Calls()
        issue(step)
        self.queue.append((list(most.values()), step.calls, self.done, 1))
        return (self.done, self.count)


class Loads:

    def __init__(self, sems, queue):
        self.sems, self.counts, self.n, self.queue = sems, [0] * len(sems), 0, queue

    def load(self, out, in_, after=(), strided=False):
        i = self.n % len(self.sems)
        self.n += 1
        waits = list(after)
        if self.counts[i]:
            waits.append((self.sems[i], self.counts[i]))
        self.counts[i] += 16
        step = Calls()
        step.dma_start(out, in_, allow_slow_non_contiguous=strided)
        self.queue.append((waits, step.calls, self.sems[i], 16))
        return (self.sems[i], self.counts[i])


class Slot:

    def __init__(self, buf):
        self.buf, self.free = buf, []


class Ring:
    def __init__(self, bufs):
        self.slots, self.n = [Slot(b) for b in bufs], 0

    def take(self):
        self.n += 1
        return self.slots[(self.n - 1) % len(self.slots)]


class Split:

    def __init__(self, hi, lo):
        self.hi, self.lo = hi, lo


def interleave(*streams):
    live = list(streams)
    while live:
        for s in list(live):
            if next(s, live) is live:
                live.remove(s)


class Program:
    def __init__(self, nc, ins, out, ctx):
        self.nc, self.ins, self.out, self.ctx = nc, ins, out, ctx
        sem = lambda n: ctx.enter_context(nc.semaphore(n))
        self.pe = Engine(sem("pe_done"), in_order=True)
        self.dve = Engine(sem("dve_done"))
        self.act = Engine(sem("act_done"))
        self.pool = Engine(sem("pool_done"))
        self.sp_queue = []
        self.sp = Loads([sem(f"sp_load{i}") for i in range(4)], self.sp_queue)
        self.small = Loads([sem(f"small_load{i}") for i in range(8)], self.pool.queue)
        self.out_sem = sem("out_stored")
        self.high = 0
        self.at = 16512
        self.names = self.bank_turn = 0
        self.ps = ctx.enter_context(nc.psum_tensor("ps", [P, 8, 512], F32))
        self.banks = [Slot(self.ps[:, i, :]) for i in range(8)]
        self.fixed()

    def place(self, name, shape, dt=F32):
        size = int(np.prod(shape[1:])) * 4
        self.at = (self.at + 31) // 32 * 32
        t = self.nc.alloc_sbuf_tensor_at(f"{name}_{self.names}", list(shape), dt, offset=self.at)
        self.names += 1
        self.at += size
        assert self.at <= 229344, (name, self.at)
        self.high = max(self.high, self.at)
        return t

    def fixed(self):
        self.cst = self.place("constant_columns", [P, C_END])
        self.cols = self.place("feature_columns", [P, 256])
        self.rope = self.place("rope_tables", [P, XT, 32])
        self.tiny = self.place("tiny", [P, 256])
        self.x = self.place("x_residual", [P, XT, DM])
        self.stage = Ring([self.place(f"w_stage{i}", [P, UNIT]) for i in range(2)])
        self.w_split = Ring([Split(self.place(f"w_hi{i}", [P, UNIT], F32R), self.place(f"w_lo{i}", [P, UNIT], F32R))
                             for i in range(2)])
        self.at = (self.at + 31) // 32 * 32
        self.hx_at = self.at
        self.hx = Split(self.place("hx_hi", [P, KT, SEQ], F32R), self.place("hx_lo", [P, KT, SEQ], F32R))
        self.hc_at = self.at
        self.negsel = self.cst[0:MH, C_NSEL:C_NSEL + MH * P].rearrange("p (h n) -> p h n", h=MH)
        self.ident = self.cst[:, C_ID:C_ID + P]
        self.area = None

    def fence(self):
        marks = [e.now() for e in (self.pe, self.dve, self.act, self.pool)]
        marks = [m for m in marks if m[1]]
        for e in (self.pe, self.dve, self.act, self.pool):
            e.pending = list(marks)
        return marks

    def plan_weights(self, plan):
        self.plan, self.loaded, self.prepared, self.taken = plan, 0, 0, 0
        self.staged, self.ready, self.released = {}, {}, set()

    def refill(self):
        while self.loaded < len(self.plan) and (self.loaded < 2 or self.loaded - 2 in self.released):
            name, src, k, n, raw = self.plan[self.loaded]
            slot = self.stage.take()
            dst = slot.buf[:, 0:k * n].rearrange("p (k n) -> p k n", k=k)
            self.staged[self.loaded] = (slot, dst, self.sp.load(dst, src, after=slot.free))
            self.loaded += 1

    def prepare(self):
        self.refill()
        i = self.prepared
        name, src, k, n, raw = self.plan[i]
        slot, staged, landed = self.staged.pop(i)
        if raw:
            self.ready[i] = (staged, slot, [landed])
        else:
            w = self.w_split.take()
            hi = w.buf.hi[:, 0:k * n].rearrange("p (k n) -> p k n", k=k)
            lo = w.buf.lo[:, 0:k * n].rearrange("p (k n) -> p k n", k=k)
            a = self.act.step(lambda e: e.activation(hi, staged, ACT.Copy), [landed] + w.free)
            b = self.dve.step(lambda e: e.tensor_tensor(lo, staged, hi.bitcast(F32), ALU.subtract), [a, landed] + w.free)
            slot.free = [a, b]
            self.released.add(i)
            self.ready[i] = (Split(hi, lo), w, [a, b])
        self.prepared += 1
        self.refill()

    def take(self, name):
        i = self.taken
        assert self.plan[i][0] == name, (self.plan[i][0], name)
        while self.prepared <= i:
            self.prepare()
        self.taken += 1
        if not self.plan[i][4] and i + 1 < len(self.plan) and not self.plan[i + 1][4]:
            self.prepare()
        return self.ready.pop(i)

    def raw_done(self, slot, ticket):
        slot.free = [ticket]
        self.released.add(self.taken - 1)
        self.refill()

    @staticmethod
    def mm3(e, out, a, b, start, stop):
        e.matmul(out, a[0], b[0], start=start, stop=False)
        e.matmul(out, a[0], b[1], start=False, stop=False)
        return e.matmul(out, a[1], b[0], start=False, stop=stop)

    def to_tokens(self, halves, srcs, nc_, banks, evac, ready=()):
        last = None
        for u, (uname, k0, kn) in enumerate(halves):
            w, slot, rdy = self.take(uname)
            for j, (src, t) in enumerate(srcs):
                bank = banks[j]

                def issue(e, src=src, t=t, bank=bank, w=w, k0=k0, kn=kn, u=u):
                    for k in range(kn):
                        l = self.mm3(e, bank.buf[:, 0:nc_],
                                     (src.hi[:, k0 + k, t * P:(t + 1) * P], src.lo[:, k0 + k, t * P:(t + 1) * P]),
                                     (w.hi[:, k, :], w.lo[:, k, :]),
                                     u == 0 and k == 0, u == len(halves) - 1 and k == kn - 1)
                    return l
                last = self.pe.step(issue, rdy + (bank.free if u == 0 else []) + list(ready))
                if u == len(halves) - 1:
                    bank.free = evac(j, bank.buf[:, 0:nc_], last)
                yield
            slot.free = [last]

    def to_features(self, halves, src, ntok, banks, evac, ready=(), m_tiles=4):
        last = None
        for u, (uname, k0, kn) in enumerate(halves):
            w, slot, rdy = self.take(uname)
            for m in range(m_tiles):
                bank = banks[m]

                def issue(e, m=m, bank=bank, w=w, k0=k0, kn=kn, u=u):
                    for k in range(kn):
                        l = self.mm3(e, bank.buf[:, 0:ntok],
                                     (w.hi[:, k, m * P:(m + 1) * P], w.lo[:, k, m * P:(m + 1) * P]),
                                     (src.hi[:, k0 + k, 0:ntok], src.lo[:, k0 + k, 0:ntok]),
                                     u == 0 and k == 0, u == len(halves) - 1 and k == kn - 1)
                    return l
                last = self.pe.step(issue, rdy + (bank.free if u == 0 else []) + list(ready))
                if u == len(halves) - 1:
                    bank.free = evac(m, bank.buf[:, 0:ntok], last)
                yield
            slot.free = [last]

    def put_split(self, dst, at, src, after, scale=1.0):
        hi, lo = dst.hi[at], dst.lo[at]
        a = self.act.step(lambda e: e.activation(hi, src, ACT.Identity, scale=scale), after)
        b = self.dve.step(lambda e: e.scalar_tensor_tensor(lo, src, scale, hi.bitcast(F32), ALU.mult, ALU.subtract), [a])
        return [a, b]

    def some_banks(self, n):
        self.bank_turn += n
        return [self.banks[(self.bank_turn - n + i) % 8] for i in range(n)]

    def to_both(self, halves, src, banks, evac, ready=(), m_tiles=4):
        for u, (uname, k0, kn) in enumerate(halves):
            w, slot, rdy = self.take(uname)
            for m in range(m_tiles):
                for c, n in ((0, SEQ), (1, CTX)):
                    bank = banks[2 * m + c]

                    def issue(e):
                        for k in range(kn):
                            self.mm3(e, bank.buf[:, 0:n],
                                     (w.hi[:, k, m * P:(m + 1) * P], w.lo[:, k, m * P:(m + 1) * P]),
                                     (src[c].hi[:, k0 + k, 0:n], src[c].lo[:, k0 + k, 0:n]),
                                     u == 0 and k == 0, u == len(halves) - 1 and k == kn - 1)
                    last = self.pe.step(issue, rdy + (bank.free if u == 0 else []) + list(ready))
                    if u == len(halves) - 1:
                        bank.free = evac(m, c, bank.buf[:, 0:n], last)
            slot.free = [last]

    def rstd(self, srcs, width, out, after):
        n = len(srcs)
        last = None
        for i, s in enumerate(srcs):
            last = self.act.step(lambda e, s=s, i=i: e.activation(self.junk[:, 0:width], s, ACT.Square,
                                                                  accum_out=out[:, i:i + 1]), after)
        a = self.dve.step(lambda e: e.tensor_scalar(out[:, 0:n], out[:, 0:n], 1.0 / width, EPS, ALU.mult, ALU.add), [last])
        b = self.act.step(lambda e: e.activation(out[:, 0:n], out[:, 0:n], ACT.Sqrt), [a])
        return self.dve.step(lambda e: e.reciprocal(out[:, 0:n], out[:, 0:n]), [b])

    def norm_features(self, tiles, width, dst, gain, after, bias=None):
        nt, kt = len(tiles), width // P
        r = self.tiny[:, 0:nt]
        ready = self.rstd(tiles, width, r, after)
        for i in range(nt):
            last = self.dve.step(lambda e, i=i: e.tensor_scalar(self.diag[:, i, :], self.ident, r[:, i:i + 1], None, ALU.mult), [ready])
        groups = []
        for lo in range(0, nt, 4):
            groups.append(list(range(lo, min(lo + 4, nt))))
        out = []
        n = 0
        for k in range(kt):
            for g in groups:
                bank = self.banks[n % 8]
                n += 1

                def issue(e, k=k, g=g, bank=bank):
                    for j, i in enumerate(g):
                        l = e.matmul(bank.buf[:, j * P:(j + 1) * P], tiles[i][:, k * P:(k + 1) * P],
                                     self.diag[:, i, :], start=True, stop=True)
                    return l
                t = self.pe.step(issue, [last] + bank.free)
                src = bank.buf[:, 0:len(g) * P]
                d, tok = dst[g[0]]
                at = (slice(None), k, slice(tok, tok + len(g) * P))
                if bias is None:
                    bank.free = self.put_split(d, at, src, [t], gain[:, k:k + 1])
                else:
                    tmp = self.nrm_tmp.take()
                    full = tmp.buf[:, 0:len(g) * P]
                    hi, lo = d.hi[at], d.lo[at]
                    gk, bk = gain[:, k:k + 1], bias[:, k:k + 1]
                    a = self.act.step(lambda e, full=full, src=src, gk=gk, bk=bk: e.activation(full, src, ACT.Identity, scale=gk, bias=bk), [t] + tmp.free)
                    b = self.act.step(lambda e, hi=hi, full=full: e.activation(hi, full, ACT.Copy), [a])
                    c = self.dve.step(lambda e, lo=lo, full=full, hi=hi: e.tensor_tensor(lo, full, hi.bitcast(F32), ALU.subtract), [b])
                    bank.free, tmp.free = [a], [c]
                    out.append(c)
                out += bank.free
        return [self.act.now(), self.dve.now()]

    def load_rows_as_columns(self, rows, at):
        n, loads = 0, []
        slab = self.row_slab
        for src in rows:
            r = src.shape[0]
            loads.append(self.small.load(slab[n:n + r, :], src, after=self.slab_free))
            n += r
        bank = self.banks[7]
        t = self.pe.step(lambda e: e.transpose(bank.buf[:, 0:n], slab[0:n, :], self.ident[0:n, 0:n]),
                         loads + [self.cst_ready] + bank.free)
        c = self.dve.step(lambda e: e.tensor_copy(self.cols[:, at:at + n], bank.buf[:, 0:n]), [t])
        bank.free, self.slab_free = [c], [t]
        return at + n

    def rows(self, name, *index):
        a = self.ins[name]
        for i in index:
            a = a[i]
        if len(a.shape) == 2:
            a = a.rearrange("a b -> (a b)")
        return a.rearrange("(r c) -> r c", c=P)

    def setup(self):
        base = self.at
        self.row_slab = self.place("row_slab", [P, P])
        self.slab_free = []
        self.junk = self.place("setup_junk", [P, DM])
        work = self.place("rope_work", [P, 6, XT, 8])
        pos_i = self.place("positions", [P, XT], I32)
        pos_f = self.place("positions_f", [P, XT])
        self.cst_ready = self.small.load(self.cst[:, :], self.ins["constants"])
        xload = self.small.load(self.x[:, :, :], self.ins["x"][0].rearrange("(t p) d -> p t d", p=P))
        pl = self.small.load(pos_i[:, :], self.ins["positions"][0].rearrange("(t p) -> p t", p=P), strided=True)
        D = self.rows
        c = {}
        at = 0
        c["norm_mix"], c["conv_w"], c["conv_b"], c["norm_mlp"] = 0, 16, 80, 96
        at = self.load_rows_as_columns(
            [D("norm_mix_w", slice(0, DEPTH)), self.ins["conv_w"].rearrange("l j (r c) -> (l j r) c", c=P),
             D("conv_b", slice(0, DEPTH)), D("norm_mlp_w", slice(0, DEPTH))], at)
        assert at == 112
        c["b_gate"], c["norm_g"], c["q_norm"], c["kv_norm"], c["cond"], c["ada_b"] = at, at + 32, at + 48, at + 51, at + 53, at + 69
        at = self.load_rows_as_columns(
            [D("b_in", 0, slice(COL_GA, D_IN)), D("b_in", 1, slice(COL_GA, D_IN)), D("norm_g_2", slice(0, DEPTH)),
             D("mla_q_norm_2", 0), D("mla_kv_norm_2", 0), D("c_2", 0), D("c_ctx_2"), D("ada_b_2", slice(0, DEPTH))], at)
        assert at == c["ada_b"] + 48
        c["gla_b"], c["b_mqk"] = at, at + 8
        at = self.load_rows_as_columns(
            [D("gla_b_gf_2", 0), D("gla_b_gb_2", 0), D("b_in", 0, slice(COL_MQ, COL_MV)), D("b_in", 1, slice(COL_MQ, COL_MV))], at)
        self.c = c
        f = self.dve.step(lambda e: e.tensor_copy(pos_f[:, :], pos_i[:, :]), [pl])
        ang, turn, k, r = (work[:, i, :, :] for i in range(4))
        inv = self.cst[:, C_INV:C_INV + 8]
        for t in range(XT):
            self.dve.step(lambda e, t=t: e.tensor_scalar(ang[:, t, :], inv, pos_f[:, t:t + 1], None, ALU.mult), [f, self.cst_ready])
        magic = 1.5 * 2.0 ** 23
        c1, c2 = 6.28125, float(np.float32(np.round((2 * np.pi - 6.28125) * 2 ** 22) / 2 ** 22))
        c3 = float(2 * np.pi - c1 - c2)
        for i, quarter in enumerate((0.25, 0.0)):
            self.dve.step(lambda e, quarter=quarter: e.tensor_scalar(turn, ang, 1 / (2 * np.pi), quarter, ALU.mult, ALU.add))
            self.dve.step(lambda e: e.tensor_scalar(k, turn, magic, None, ALU.add))
            self.dve.step(lambda e: e.tensor_scalar(k, k, -magic, None, ALU.add))
            self.dve.step(lambda e: e.scalar_tensor_tensor(r, k, -c1, ang, ALU.mult, ALU.add))
            self.dve.step(lambda e: e.scalar_tensor_tensor(r, k, -c2, r, ALU.mult, ALU.add))
            self.dve.step(lambda e: e.scalar_tensor_tensor(r, k, -c3, r, ALU.mult, ALU.add))
            self.dve.step(lambda e, quarter=quarter: e.tensor_scalar(r, r, quarter * 2 * np.pi, float(np.float32(3.1415925)), ALU.add, ALU.min))
            d = self.dve.step(lambda e: e.tensor_scalar(r, r, float(-np.float32(3.1415925)), None, ALU.max))
            s = self.act.step(lambda e, i=i: e.activation(work[:, 4 + i, :, :], r, ACT.Sin), [d])
            self.dve.pending = [s]
        cos, sin = work[:, 4, :, :], work[:, 5, :, :]
        for o in (0, 8):
            self.dve.step(lambda e, o=o: e.tensor_copy(self.rope[:, :, o:o + 8], cos), [s])
        self.dve.step(lambda e: e.tensor_scalar(self.rope[:, :, 16:24], sin, -1.0, None, ALU.mult))
        self.dve.step(lambda e: e.tensor_copy(self.rope[:, :, 24:32], sin))
        self.at = base
        self.x_ready = [xload]
        self.fence()

    def layer(self, l):
        c, cols, cst, ins = self.c, self.cols, self.cst, self.ins
        pe, dve, act, pool = self.pe, self.dve, self.act, self.pool
        fence = self.fence()
        base = self.at = self.hc_at
        mqk = self.place("mlstm_qk", [P, 8, SEQ])
        mv = self.place("mlstm_v", [P, XT, MH, MHD + 1])
        mo = self.place("mlstm_out_gate", [P, XT, 512])
        qk_end = self.at
        y_att = Split(self.place("y_att_hi", [P, 4, SEQ], F32R), self.place("y_att_lo", [P, 4, SEQ], F32R))
        gates = self.place("gates", [P, 8, 16])
        mrow = self.place("running_max_row", [MH, SEQ])
        zrow = self.place("zero_row", [MH, SEQ])
        self.rope_tmp = self.place("rope_swapped", [P, P])
        att_at = self.at
        qT = self.place("att_qT", [P, 4, SEQ])
        kT = self.place("att_kT", [P, 4, SEQ])
        av = self.place("att_v", [P, XT, 512])
        conv_in = Ring([self.place(f"conv_in{i}", [P, CONV - 1 + SEQ]) for i in range(2)])
        conv_acc = self.place("conv_acc", [P, SEQ])
        tok = Ring([self.place(f"token_tile{i}", [P, 512]) for i in range(2)])
        bias_row = Ring([self.place(f"bias_row{i}", [P, 512]) for i in range(1)])
        tmp_at = self.at
        prob = Ring([self.place(f"prob{i}", [P, 512]) for i in range(2)])
        probT = Ring([self.place(f"probT{i}", [P, 512]) for i in range(2)])
        y_tok = Ring([self.place(f"y_tok{i}", [P, 512]) for i in range(1)])
        self.junk = self.nc.alloc_sbuf_tensor_at(f"junk_l{l}", [P, DM], F32, offset=(tmp_at + 31) // 32 * 32)
        self.diag = self.nc.alloc_sbuf_tensor_at(f"diag_l{l}", [P, 4, P], F32, offset=(tmp_at + 31) // 32 * 32 + 4096)
        tiny = self.tiny

        h_ready = self.norm_features([self.x[:, t, :] for t in range(XT)], DM, [(self.hx, t * P) for t in range(XT)],
                                     self.cols[:, c["norm_mix"] + 8 * l:c["norm_mix"] + 8 * l + 8], self.x_ready)
        marks_of_phase = self.fence()
        for s in conv_in.slots:
            s.free = [pool.step(lambda e, s=s: e.memset(s.buf[:, 0:CONV - 1], 0.0))]
        ones = [pool.step(lambda e: e.memset(mv[:, :, :, MHD:MHD + 1], 1.0)), pool.step(lambda e: e.memset(zrow[:, :], 0.0))]
        X = [(self.hx, t) for t in range(XT)]
        main, side = self.banks[0:4], self.banks[4:8]

        def bias_load(lo, n):
            b = bias_row.take()
            t = self.small.load(b.buf[:, 0:n], ins["b_in"][l, lo:lo + n].partition_broadcast(P), after=b.free + marks_of_phase)
            return b, t

        def u(name):
            return [(f"{name}.{l}.{i}", 4 * i, 4) for i in range(2)]

        done = {}
        for name, lo, dst in (("aq", COL_AQ, qT), ("ak", COL_AK, kT)):
            b, bt = bias_load(lo, 512)

            def evac(t, bank, made, dst=dst, b=b, bt=bt, name=name):
                z = tok.take()
                first = dve.step(lambda e: e.tensor_tensor(z.buf[:, :], bank, b.buf[:, :], ALU.add), [made, bt] + z.free)
                zh = z.buf[:, :].rearrange("p (h d) -> p h d", h=AH)
                swap = self.rope_tmp[:, 0:128].rearrange("p (h d) -> p h d", h=AH)
                table = self.rope[:, t, :]
                cc = table[:, 0:16].unsqueeze(1).broadcast_to([P, AH, 16])
                dve.step(lambda e: e.tensor_tensor(swap[:, :, 0:8], zh[:, :, 8:16], table[:, 16:24].unsqueeze(1).broadcast_to([P, AH, 8]), ALU.mult))
                dve.step(lambda e: e.tensor_tensor(swap[:, :, 8:16], zh[:, :, 0:8], table[:, 24:32].unsqueeze(1).broadcast_to([P, AH, 8]), ALU.mult))
                dve.step(lambda e: e.tensor_tensor(zh[:, :, 0:16], zh[:, :, 0:16], cc, ALU.mult))
                r = dve.step(lambda e: e.tensor_tensor(zh[:, :, 0:16], zh[:, :, 0:16], swap, ALU.add))
                sb = side[t]

                def tr(e):
                    for g in range(4):
                        last = e.transpose(sb.buf[:, g * P:(g + 1) * P], z.buf[:, g * P:(g + 1) * P], self.ident)
                    return last
                tt = pe.step(tr, [r] + sb.free)
                o = act.step(lambda e: e.activation(dst[:, :, t * P:(t + 1) * P], sb.buf[:, :].rearrange("p (g t) -> p g t", g=4), ACT.Copy), [tt])
                sb.free, z.free, b.free = [o], [tt], [first]
                done[name, t] = o
                return [first]
            for _ in self.to_tokens(u(name), X, 512, main, evac, h_ready):
                pass
        b, bt = bias_load(COL_AV, 512)

        def evac_v(t, bank, made):
            a = dve.step(lambda e: e.tensor_tensor(av[:, t, :], bank, b.buf[:, :], ALU.add), [made, bt])
            b.free = [a]
            done["av", t] = a
            return [a]
        for _ in self.to_tokens(u("av"), X, 512, main, evac_v, h_ready):
            pass

        def mlstm_inputs():
            for g in range(2):
                for _ in self.to_features(u(f"mqk{g}"), self.hx, SEQ, main, lambda m, bank, made, g=g: conv(g * 4 + m, bank, made)):
                    yield
            b, bt = bias_load(COL_MV, 512)

            def evac_mv(t, bank, made):
                a = dve.step(lambda e: e.tensor_tensor(mv[:, t, :, 0:MHD], bank.rearrange("p (h d) -> p h d", h=MH),
                                                       b.buf[:, :].rearrange("p (h d) -> p h d", h=MH), ALU.add), [made, bt] + ones)
                b.free = [a]
                done["mv", t] = a
                return [a]
            for _ in self.to_tokens(u("mv"), X, 512, main, evac_mv):
                yield
            b2, bt2 = bias_load(COL_MO, 512)

            def evac_mo(t, bank, made):
                a = dve.step(lambda e: e.tensor_tensor(mo[:, t, :], bank, b2.buf[:, :], ALU.add), [made, bt2])
                b2.free = [a]
                done["mo", t] = a
                return [a]
            for _ in self.to_tokens(u("mo"), X, 512, main, evac_mo):
                yield
            b3, bt3 = bias_load(COL_MI, 8)

            def evac_if(t, bank, made):
                a = dve.step(lambda e: e.tensor_tensor(gates[:, 0:2, 4 * t:4 * t + 4], bank.rearrange("p (g h) -> p g h", g=2),
                                                       b3.buf[:, 0:8].rearrange("p (g h) -> p g h", g=2), ALU.add), [made, bt3])
                b3.free = [a]
                done["if", t] = a
                return [a]
            for _ in self.to_tokens([(f"mif.{l}", 0, 8)], X, 8, main, evac_if):
                yield

        def conv(m, bank, made):
            s = conv_in.take()
            bcol = cols[:, c["b_mqk"] + 8 * l + m:c["b_mqk"] + 8 * l + m + 1]
            a = act.step(lambda e: e.activation(s.buf[:, CONV - 1:], bank, ACT.Identity, bias=bcol), [made] + s.free)
            w = lambda j: cols[:, c["conv_w"] + (l * CONV + j) * 8 + m:c["conv_w"] + (l * CONV + j) * 8 + m + 1]
            cb = cols[:, c["conv_b"] + 8 * l + m:c["conv_b"] + 8 * l + m + 1]
            d = dve.step(lambda e: e.tensor_scalar(conv_acc[:, :], s.buf[:, 0:SEQ], w(0), cb, ALU.mult, ALU.add), [a] + self.acc_free)
            for j in range(1, CONV):
                d = dve.step(lambda e, j=j: e.scalar_tensor_tensor(conv_acc[:, :], s.buf[:, j:j + SEQ], w(j), conv_acc[:, :], ALU.mult, ALU.add))
            s.free = [d]
            sg = act.step(lambda e: e.activation(mqk[:, m, :], conv_acc[:, :], ACT.Silu), [d])
            self.acc_free = [sg]
            done["mqk", m] = sg
            return [a]
        self.acc_free = []

        def attention():
            s_banks, t_bank, o_bank = Ring(side[0:2]), side[2], side[3]
            s_banks.slots = side[0:2]
            units = [(i, h) for i in range(XT) for h in range(AH)]
            state = {}

            def scores(i, h):
                n = (i + 1) * P
                bank = s_banks.take()
                hp = (h % 2) * AHD
                t = pe.step(lambda e: e.matmul(bank.buf[:, 0:n], qT[hp:hp + AHD, h // 2, i * P:(i + 1) * P], kT[hp:hp + AHD, h // 2, 0:n],
                                               start=True, stop=True), [done["aq", i], done["ak", i]] + bank.free)
                p = prob.take()
                mn, ls = tiny[:, 64 + h:65 + h], tiny[:, 72 + h:73 + h]
                d = dve.step(lambda e: e.tensor_tensor_reduce(out=p.buf[:, 0:n], in0=bank.buf[:, 0:n], in1=cst[:, C_ATT + 512 - n:C_ATT + 512],
                                                              scale=-AHD ** -0.5, scalar=3e38, op0=ALU.add, op1=ALU.min, accum_out=mn), [t] + p.free)
                bank.free = [d]
                a = act.step(lambda e: e.activation(p.buf[:, 0:n], p.buf[:, 0:n], ACT.Exp, bias=mn, scale=-1.0, accum_out=ls), [d])
                state[i, h] = (p, n, ls, a)

            def turn(i, h):
                p, n, ls, a = state[i, h]

                def tr(e):
                    for j in range(i + 1):
                        last = e.transpose(t_bank.buf[:, j * P:(j + 1) * P], p.buf[:, j * P:(j + 1) * P], self.ident)
                    return last
                t = pe.step(tr, [a] + t_bank.free)
                p.free = [t]
                q = probT.take()
                if h % 2:
                    cp = dve.step(lambda e: e.tensor_copy(q.buf[:, 0:n], t_bank.buf[:, 0:n]), [t] + q.free)
                else:
                    cp = act.step(lambda e: e.activation(q.buf[:, 0:n], t_bank.buf[:, 0:n], ACT.Copy), [t] + q.free)
                t_bank.free = [cp]
                state[i, h] = (q, ls, cp, a)

            def values(i, h):
                q, ls, cp, a = state[i, h]

                def pv(e):
                    for j in range(i + 1):
                        last = e.matmul(o_bank.buf[:, 0:AHD], q.buf[:, j * P:(j + 1) * P], av[:, j, h * AHD:(h + 1) * AHD],
                                        start=(j == 0), stop=(j == i))
                    return last
                t = pe.step(pv, [cp, done["av", i]] + o_bank.free)
                q.free = [t]
                if h == 0:
                    state["y", i] = y_tok.take()
                y = state["y", i]
                dve.step(lambda e: e.reciprocal(ls, ls), [a])
                d = dve.step(lambda e: e.tensor_scalar(y.buf[:, h * AHD:(h + 1) * AHD], o_bank.buf[:, 0:AHD], ls, None, ALU.mult), [t] + y.free)
                o_bank.free = [d]
                if h == AH - 1:
                    def tr(e):
                        for g in range(4):
                            last = e.transpose(t_bank.buf[:, g * P:(g + 1) * P], y.buf[:, g * P:(g + 1) * P], self.ident)
                        return last
                    tt = pe.step(tr, [d] + t_bank.free)
                    y.free = [tt]
                    t_bank.free = self.put_split(y_att, (slice(None), slice(0, 4), slice(i * P, (i + 1) * P)),
                                                 t_bank.buf[:, :].rearrange("p (g t) -> p g t", g=4), [tt])
                    done["y", i] = t_bank.free
            for s in range(len(units) + 2):
                if s < len(units):
                    scores(*units[s])
                    yield
                if 1 <= s <= len(units):
                    turn(*units[s - 1])
                    yield
                if s >= 2:
                    values(*units[s - 2])
                    yield

        interleave(attention(), mlstm_inputs())

        self.fence()
        self.at = att_at
        mix_a = self.place("mixed_att", [P, 8, SEQ])
        y_m = Split(self.place("y_mlstm_hi", [P, 4, SEQ], F32R), self.place("y_mlstm_lo", [P, 4, SEQ], F32R))
        E = Ring([self.place(f"decay{i}", [P, 512]) for i in range(2)])
        Pm = Ring([self.place("mlstm_prob", [P, 1280])])
        p_at = (0, 512, 896, 1152)
        nrow = self.place("mlstm_norm_row", [P, 512])
        bl = self.small.load(nrow[:, 0:512], ins["mlstm_norm_w"][l, :].partition_broadcast(P), after=self.fence())
        G = lambda j: gates[:, j, :]
        gr = [done["if", t] for t in range(XT)]
        act.step(lambda e: e.activation(G(2), G(1), ACT.Abs), gr)
        act.step(lambda e: e.activation(G(2), G(2), ACT.Exp, scale=-1.0))
        a = act.step(lambda e: e.activation(G(2), G(2), ACT.Ln, bias=1.0))
        d = dve.step(lambda e: e.scalar_tensor_tensor(G(3), G(1), 0.0, G(2), ALU.min, ALU.subtract), [a])
        dve.step(lambda e: e.memset(gates[:, 4, 0:4], 0.0))
        for t in range(1, XT):
            d = dve.step(lambda e, t=t: e.tensor_tensor(gates[:, 4, 4 * t:4 * t + 4], gates[:, 4, 4 * t - 4:4 * t], gates[:, 3, 4 * t - 4:4 * t], ALU.add))
        bk = self.banks[4]

        def cum(e):
            e.matmul(bk.buf[:, 0:16], cst[:, C_UP:C_UP + P], G(3), start=True, stop=False)
            return e.matmul(bk.buf[:, 0:16], cst[:, C_ONES:C_ONES + P], G(4), start=False, stop=True)
        t = pe.step(cum, [d] + bk.free)
        dve.step(lambda e: e.tensor_copy(G(5), bk.buf[:, 0:16]), [t])
        d = dve.step(lambda e: e.tensor_tensor(G(6), G(0), G(5), ALU.subtract))
        bk.free = [d]
        bk2 = self.banks[5]

        def rows_(e):
            for t in range(XT):
                last = e.transpose(bk2.buf[0:MH, t * P:(t + 1) * P], gates[:, 6, 4 * t:4 * t + 4], self.ident)
            return last
        t = pe.step(rows_, [d] + bk2.free)
        m_row = dve.step(lambda e: e.tensor_tensor_scan(mrow[:, :], bk2.buf[0:MH, :], zrow[:, :], 0.0, ALU.max, ALU.max), [t])
        bk2.free = [m_row]

        def back(e):
            for t in range(XT):
                last = e.transpose(bk.buf[:, 4 * t:4 * t + 4], mrow[:, t * P:(t + 1) * P], self.ident[0:MH, 0:MH])
            return last
        t = pe.step(back, [m_row] + bk.free)
        d = dve.step(lambda e: e.tensor_tensor(G(7), bk.buf[:, 0:16], G(5), ALU.add), [t])
        bk.free = [d]
        floor_ready = act.step(lambda e: e.activation(G(7), G(7), ACT.Exp, scale=-1.0), [d])

        def mlstm():
            m_bank, s_bank, o_banks = side[0], side[1], side[2:4]
            for h in range(MH):
                t = pe.step(lambda e, h=h: e.matmul(m_bank.buf[:, :], self.negsel[:, h, :], mrow[:, :], start=True, stop=True), [m_row] + m_bank.free)
                pm = Pm.take()
                last = None
                yield
                for j in range(XT):
                    n = (XT - j) * P
                    w = E.take()
                    d = dve.step(lambda e, j=j, n=n, w=w, h=h: e.tensor_scalar(w.buf[:, 0:n], m_bank.buf[:, j * P:], gates[:, 6, 4 * j + h:4 * j + h + 1], None, ALU.add), [t] + w.free)
                    d = dve.step(lambda e, w=w: e.tensor_tensor(w.buf[:, 0:P], w.buf[:, 0:P], cst[:, C_TRI:C_TRI + P], ALU.add))
                    a = act.step(lambda e, n=n, w=w: e.activation(w.buf[:, 0:n], w.buf[:, 0:n], ACT.Exp), [d])
                    s = pe.step(lambda e, j=j, n=n, h=h: e.matmul(s_bank.buf[:, 0:n], mqk[:, 4 + h, j * P:(j + 1) * P], mqk[:, h, j * P:], start=True, stop=True),
                                [done["mqk", h], done["mqk", 4 + h]] + s_bank.free)
                    last = dve.step(lambda e, j=j, n=n, w=w, pm=pm: e.scalar_tensor_tensor(pm.buf[:, p_at[j]:p_at[j] + n], s_bank.buf[:, 0:n], MHD ** -0.5, w.buf[:, 0:n], ALU.mult, ALU.mult),
                                    [s, a] + pm.free)
                    s_bank.free, w.free = [last], [last]
                    if j == XT - 1:
                        m_bank.free = [d]
                    yield
                for half in range(2):
                    ob = o_banks[half]

                    def pv(e):
                        for ii in range(2):
                            i = 2 * half + ii
                            for j in range(i + 1):
                                e.matmul(ob.buf[:, ii * 129:ii * 129 + 129], pm.buf[:, p_at[j] + (i - j) * P:p_at[j] + (i - j + 1) * P],
                                         mv[:, j, h, :], start=(j == 0), stop=(j == i))
                    t2 = pe.step(pv, [last] + [done["mv", j] for j in range(XT)] + ob.free)
                pm.free = [t2]
                yield
                for half in range(2):
                    ob = o_banks[half]
                    o2 = ob.buf[:, 0:258].rearrange("p (i d) -> p i d", i=2)
                    den = tiny[:, 96:98]
                    fl = gates[:, 7, :].rearrange("p (t h) -> p t h", h=MH)[:, 2 * half:2 * half + 2, h]
                    dve.step(lambda e: e.tensor_scalar(den, o2[:, :, MHD], -1.0, None, ALU.mult), [t2])
                    dve.step(lambda e: e.tensor_tensor(den, o2[:, :, MHD], den, ALU.max))
                    dve.step(lambda e: e.tensor_tensor(den, den, fl, ALU.max), [floor_ready])
                    dve.step(lambda e: e.reciprocal(den, den))
                    for ii in range(2):
                        d = dve.step(lambda e: e.tensor_scalar(mv[:, 2 * half + ii, h, 0:MHD], o2[:, ii, 0:MHD], den[:, ii:ii + 1], None, ALU.mult))
                    ob.free = [d]
                    yield
            done["hm"] = d

        def att_projection():
            for g in range(2):
                ga = {}

                def evac_g(m, bank, made, g=g):
                    bcol = cols[:, c["b_gate"] + 16 * l + 4 * g + m:c["b_gate"] + 16 * l + 4 * g + m + 1]
                    a = dve.step(lambda e: e.tensor_scalar(mix_a[:, 4 * g + m, :], bank, bcol, None, ALU.add), [made])
                    return [a]
                for _ in self.to_features(u(f"ga{g}"), self.hx, SEQ, main, evac_g):
                    yield
                a = act.step(lambda e, g=g: e.activation(mix_a[:, 4 * g:4 * g + 4, :], mix_a[:, 4 * g:4 * g + 4, :], ACT.Sigmoid), [dve.now()])

                def evac_p(m, bank, made, g=g, a=a):
                    return [dve.step(lambda e: e.tensor_tensor(mix_a[:, 4 * g + m, :], bank, mix_a[:, 4 * g + m, :], ALU.mult), [made, a])]
                for _ in self.to_features([(f"pa{g}.{l}", 0, 4)], y_att, SEQ, main, evac_p, done["y", 3]):
                    yield
        interleave(mlstm(), att_projection())

        rs = self.tiny[:, 100:116]
        for t in range(XT):
            w = E.take()
            d = dve.step(lambda e, t=t, w=w: e.tensor_tensor(w.buf[:, :].rearrange("p (h d) -> p h d", h=MH), mv[:, t, :, 0:MHD], mv[:, t, :, 0:MHD], ALU.mult), [done["hm"]] + w.free)
            d = dve.step(lambda e, t=t, w=w: e.tensor_reduce(rs[:, 4 * t:4 * t + 4], w.buf[:, :].rearrange("p (h d) -> p h d", h=MH), AX_X, ALU.add))
            w.free = [d]
        d = dve.step(lambda e: e.tensor_scalar(rs, rs, 1.0 / MHD, EPS, ALU.mult, ALU.add))
        a = act.step(lambda e: e.activation(rs, rs, ACT.Sqrt), [d])
        dve.step(lambda e: e.reciprocal(rs, rs), [a])
        sg = act.step(lambda e: e.activation(mo[:, :, :], mo[:, :, :], ACT.Sigmoid), [done["mo", t] for t in range(XT)])
        for t in range(XT):
            dve.step(lambda e, t=t: e.tensor_tensor(mo[:, t, :], mo[:, t, :], nrow[:, 0:512], ALU.mult), [sg, bl])
            for h in range(MH):
                sl = slice(h * MHD, (h + 1) * MHD)
                d = dve.step(lambda e, t=t, h=h, sl=sl: e.scalar_tensor_tensor(mv[:, t, h, 0:MHD], mv[:, t, h, 0:MHD], rs[:, 4 * t + h:4 * t + h + 1], mo[:, t, sl], ALU.mult, ALU.mult))
            sb = side[t]

            def tr(e, t=t, sb=sb):
                for g in range(4):
                    last = e.transpose(sb.buf[:, g * P:(g + 1) * P], mv[:, t, g, 0:MHD], self.ident)
                return last
            tt = pe.step(tr, [d] + sb.free)
            sb.free = self.put_split(y_m, (slice(None), slice(0, 4), slice(t * P, (t + 1) * P)),
                                     sb.buf[:, :].rearrange("p (g t) -> p g t", g=4), [tt])
            y_ready = sb.free
        self.fence()
        self.at = base
        mixed = Split(self.place("mixed_hi", [P, 8, SEQ], F32R), self.place("mixed_lo", [P, 8, SEQ], F32R))
        assert self.at <= qk_end
        self.at = qk_end
        gbt = self.place("gated", [P, 4, SEQ])
        assert self.at <= att_at
        for g in range(2):
            def evac_g(m, bank, made, g=g):
                bcol = cols[:, c["b_gate"] + 16 * l + 8 + 4 * g + m:c["b_gate"] + 16 * l + 8 + 4 * g + m + 1]
                return [act.step(lambda e: e.activation(gbt[:, m, :], bank, ACT.Sigmoid, bias=bcol), [made, dve.now()])]
            for _ in self.to_features(u(f"gb{g}"), self.hx, SEQ, self.banks[0:4], evac_g):
                pass

            def evac_p(m, bank, made, g=g):
                k = 4 * g + m
                dve.step(lambda e: e.tensor_tensor(gbt[:, m, :], bank, gbt[:, m, :], ALU.mult), [made, act.now()])
                d = dve.step(lambda e: e.tensor_tensor(gbt[:, m, :], gbt[:, m, :], mix_a[:, k, :], ALU.add))
                a = act.step(lambda e: e.activation(mixed.hi[:, k, :], gbt[:, m, :], ACT.Copy), [d])
                dve.step(lambda e: e.tensor_tensor(mixed.lo[:, k, :], gbt[:, m, :], mixed.hi[:, k, :].bitcast(F32), ALU.subtract), [a])
                return [d]
            for _ in self.to_features([(f"pm{g}.{l}", 0, 4)], y_m, SEQ, self.banks[4:8], evac_p):
                pass
        ready = [act.now(), dve.now()]
        for g in range(2):
            def evac_o(t, bank, made, g=g):
                sl = slice(g * 512, (g + 1) * 512)
                return [dve.step(lambda e: e.tensor_tensor(self.x[:, t, sl], bank, self.x[:, t, sl], ALU.add), [made])]
            for _ in self.to_tokens([(f"wo{g}.{l}.{i}", 4 * i, 4) for i in range(2)], [(mixed, t) for t in range(XT)], 512,
                                    self.banks[4 * g:4 * g + 4], evac_o, ready):
                pass

        self.fence()
        self.at = base
        up = [Split(self.place(f"hidden_hi{i}", [P, 8, SEQ], F32R), self.place(f"hidden_lo{i}", [P, 8, SEQ], F32R)) for i in range(1)]
        relu = Ring([self.place(f"relu{i}", [P, SEQ]) for i in range(2)])
        sq = Ring([self.place(f"relu_sq{i}", [P, SEQ]) for i in range(2)])
        self.junk = self.place("mlp_junk", [P, DM])
        self.diag = self.place("mlp_diag", [P, 4, P])
        self.norm_features([self.x[:, t, :] for t in range(XT)], DM, [(self.hx, t * P) for t in range(XT)],
                           self.cols[:, c["norm_mlp"] + 8 * l:c["norm_mlp"] + 8 * l + 8], [dve.now()])
        h_ready = [act.now(), dve.now()]
        up_free = [[]]
        for q in range(4):
            U = up[0]
            for g in range(2):
                def evac_u(m, bank, made, g=g):
                    k = 4 * g + m
                    r, s = relu.take(), sq.take()
                    a = act.step(lambda e: e.activation(r.buf[:, :], bank, ACT.Relu), [made] + r.free)
                    b = act.step(lambda e: e.activation(U.hi[:, k, :], r.buf[:, :], ACT.Square), up_free[0])
                    d = dve.step(lambda e: e.tensor_tensor(s.buf[:, :], r.buf[:, :], r.buf[:, :], ALU.mult), [a] + s.free)
                    d = dve.step(lambda e: e.tensor_tensor(U.lo[:, k, :], s.buf[:, :], U.hi[:, k, :].bitcast(F32), ALU.subtract), [b] + up_free[0])
                    r.free, s.free = [b, d], [d]
                    return [a]
                for _ in self.to_features([(f"f1.{l}.{q}.{g}.{i}", 4 * i, 4) for i in range(2)], self.hx, SEQ, self.banks[0:4], evac_u, h_ready):
                    pass
            ready = [act.now(), dve.now()]
            for g in range(2):
                def evac_d(t, bank, made, g=g):
                    sl = slice(g * 512, (g + 1) * 512)
                    return [dve.step(lambda e: e.tensor_tensor(self.x[:, t, sl], bank, self.x[:, t, sl], ALU.add), [made])]
                for _ in self.to_tokens([(f"f2.{l}.{q}.{g}.{i}", 4 * i, 4) for i in range(2)], [(U, t) for t in range(XT)], 512,
                                        self.banks[4:8], evac_d, ready):
                    pass
            up_free[0] = [pe.now()]
        self.x_ready = [dve.now()]

    def layer_plan(self, l):
        w = {n: self.ins[n][l] for n in ("w_in", "w_proj_att", "w_proj_mlstm", "w_out", "w_ff1", "w_ff2")}

        units = self.units
        plan = []
        for n, c0 in (("aq", COL_AQ), ("ak", COL_AK), ("av", COL_AV), ("mqk0", COL_MQ), ("mqk1", COL_MQ + 512), ("mv", COL_MV), ("mo", COL_MO)):
            plan += units(f"{n}.{l}", w["w_in"], c0)
        plan += units(f"mif.{l}", w["w_in"], COL_MI, 8, per=8)
        for n, c0, pn, pw in (("ga", COL_GA, "pa", "w_proj_att"), ("gb", COL_GB, "pm", "w_proj_mlstm")):
            for g in range(2):
                plan += units(f"{n}{g}.{l}", w["w_in"], c0 + 512 * g)
                plan += units(f"{pn}{g}.{l}", w[pw], 512 * g, kn=4)
        for g in range(2):
            plan += units(f"wo{g}.{l}", w["w_out"], 512 * g)
        for q in range(4):
            for g in range(2):
                plan += units(f"f1.{l}.{q}.{g}", w["w_ff1"], q * 1024 + g * 512)
            for g in range(2):
                plan += units(f"f2.{l}.{q}.{g}", w["w_ff2"], g * 512, k0=q * 8)
        return plan

    def final_norm(self, name, dst_dram=None):
        marks = self.fence()
        row = self.place("final_gain_row", [P, DM])
        self.junk = self.place("final_junk", [P, DM])
        rl = self.small.load(row[:, :], self.ins[name].partition_broadcast(P), after=marks)
        r = self.tiny[:, 0:XT]
        ready = self.rstd([self.x[:, t, :] for t in range(XT)], DM, r, self.x_ready)
        for t in range(XT):
            self.x_ready = [self.dve.step(lambda e: e.scalar_tensor_tensor(self.x[:, t, :], self.x[:, t, :], r[:, t:t + 1], row[:, :], ALU.mult, ALU.mult), [ready, rl])]

    def modulation(self, i, gate_bc, gain, shift, work):
        pe, dve, act, cols, c = self.pe, self.dve, self.act, self.cols, self.c
        cond = work("cond", [P, KT, 2])
        row = Ring([work(f"mod_row{j}", [2, 512]) for j in range(2)])
        brow = Ring([work(f"mod_bias_row{j}", [P, 512]) for j in range(1)])
        mod = work("mod_cols", [P, 2, 16])
        marks = self.fence()
        s = act.step(lambda e: e.activation(cond[:, :, :], cols[:, c["cond"]:c["cond"] + 16].rearrange("p (c k) -> p k c", c=2), ACT.Silu))
        for g in range(6):
            bank, = self.some_banks(1)
            for u in range(2):
                w, slot, rdy = self.take(f"ada{i}.{g}.{u}")

                def issue(e):
                    for k in range(4):
                        e.matmul(bank.buf[0:2, :], cond[:, 4 * u + k, :], w[:, k, :], start=(u == 0 and k == 0), stop=(u == 1 and k == 3))
                t = pe.step(issue, rdy + [s] + (bank.free if u == 0 else []))
                self.raw_done(slot, t)
            r = row.take()
            a = act.step(lambda e: e.activation(r.buf[:, :], bank.buf[0:2, :], ACT.Copy), [t] + r.free)
            bank.free = [a]
            if g < 4:
                b2, = self.some_banks(1)

                def tr(e):
                    for m in range(4):
                        e.transpose(b2.buf[:, 2 * m:2 * m + 2], r.buf[:, m * P:(m + 1) * P], self.ident[0:2, 0:2])
                t = pe.step(tr, [a] + b2.free)
                ab = cols[:, c["ada_b"] + 24 * i + 4 * g:c["ada_b"] + 24 * i + 4 * g + 4]
                d = dve.step(lambda e: e.tensor_tensor(mod[:, :, 4 * g:4 * g + 4], b2.buf[:, 0:8].rearrange("p (m c) -> p c m", m=4),
                                                       ab.unsqueeze(1).broadcast_to([P, 2, 4]), ALU.add), [t])
                b2.free, r.free = [d], [t]
            else:
                b = brow.take()
                lo = 512 * g
                bt = self.small.load(b.buf[:, :], self.ins["ada_b_2"][i, lo:lo + 512].partition_broadcast(P), after=b.free + marks)
                for q, gate in enumerate(gate_bc):
                    b2, = self.some_banks(1)
                    t = pe.step(lambda e: e.matmul(b2.buf[:, :], self.cst[0:2, C_SEL2 + q * P:C_SEL2 + (q + 1) * P], r.buf[:, :], start=True, stop=True), [a] + b2.free)
                    d = dve.step(lambda e: e.tensor_tensor(gate[:, (g - 4) * 512:(g - 3) * 512], b2.buf[:, :], b.buf[:, :], ALU.add), [t, bt])
                    b2.free, b.free, r.free = [d], [d], [t]
        ng = cols[:, c["norm_g"] + 8 * i:c["norm_g"] + 8 * i + 8]
        dve.step(lambda e: e.tensor_copy(shift[:, :, :], mod[:, :, 0:8]))
        dve.step(lambda e: e.tensor_scalar(gain[:, :, :], mod[:, :, 8:16], 1.0, None, ALU.add))
        return dve.step(lambda e: e.tensor_tensor(gain[:, :, :], gain[:, :, :], ng.unsqueeze(1).broadcast_to([P, 2, 8]), ALU.mult))

    def modulated_norm(self, gain, shift, ready):
        self.junk = self.place("norm_junk", [P, DM])
        self.diag = self.place("norm_diag", [P, 4, P])
        self.nrm_tmp = Ring([self.place(f"norm_tmp{j}", [P, 512]) for j in range(2)])
        self.norm_features([self.x[:, t, :] for t in range(XT)], DM, [(self.hx, t * P) for t in range(XT)],
                           gain[:, 0, :], ready + self.x_ready, shift[:, 0, :])
        self.norm_features([self.ctx_res[:, t, :] for t in range(CT)], DM, [(self.hc, t * P) for t in range(CT)],
                           gain[:, 1, :], ready, shift[:, 1, :])
        return [self.act.now(), self.dve.now()]

    def mla(self):
        pe, dve, act, c, cols, cst = self.pe, self.dve, self.act, self.c, self.cols, self.cst
        T = XT + CT
        marks = self.fence()
        self.at = self.hc_at
        self.hc = Split(self.place("hc_hi", [P, KT, CTX], F32R), self.place("hc_lo", [P, KT, CTX], F32R))
        self.after_hc = self.at
        self.ctx_res = self.place("context_residual", [P, CT, DM])
        after_ctx = self.at
        cl = self.small.load(self.ctx_res[:, :, :], self.ins["ctx_2"][0].rearrange("(t p) d -> p t d", p=P), after=marks)
        gate_bc = [self.place("mod_gate_x", [P, DM]), self.place("mod_gate_ctx", [P, DM])]
        gate = self.place("mla_gate", [P, T, DM])
        krot = self.place("mla_rope_key", [P, T, LROPE])
        gain, shift = self.place("mod_gain", [P, 2, 8]), self.place("mod_shift", [P, 2, 8])
        self.rope_tmp = self.place("axial_swapped", [P, P])
        body = self.at
        mod = self.modulation(0, gate_bc, gain, shift, self.place)
        self.at = body
        self.fence()
        ready = self.modulated_norm(gain, shift, [mod, cl])
        self.fence()
        self.at = body
        lat = self.place("mla_latents", [P, T, LAT])
        srcs = [(self.hx, t) for t in range(XT)] + [(self.hc, t) for t in range(CT)]
        for n, lo, w in (("l0", 0, 512), ("l1", 512, 160), ("g0", LAT, 512), ("g1", LAT + 512, 512)):
            def evac(t, bank, made):
                if n[0] == "l":
                    return [act.step(lambda e: e.activation(lat[:, t, lo:lo + w], bank, ACT.Copy), [made])]
                return [act.step(lambda e: e.activation(gate[:, t, lo - LAT:lo - LAT + w], bank, ACT.Silu), [made])]
            for _ in self.to_tokens([(f"mla_{n}.{i}", 4 * i, 4) for i in range(2)], srcs, w, self.some_banks(T), evac, ready):
                pass
        r0 = QR + KVR
        dve.pending.append(act.now())
        for t in range(T):
            k = lat[:, t, r0:r0 + LROPE]
            if t < XT:
                self.axial(k.unsqueeze(1), krot[:, t, :].unsqueeze(1), t, 1)
            else:
                dve.step(lambda e: e.tensor_copy(krot[:, t, :], k))
        self.fence()
        lat_end = self.at
        self.at = self.hx_at
        cq = Split(self.place("cq_hi", [P, 3, 768], F32R), self.place("cq_lo", [P, 3, 768], F32R))
        ckv = Split(self.place("ckv_hi", [P, 2, 768], F32R), self.place("ckv_lo", [P, 2, 768], F32R))
        prob = Ring([self.place(f"mla_prob{j}", [P, 768]) for j in range(2)])
        probT = Ring([self.place(f"mla_probT{j}", [P, 768]) for j in range(2)])
        assert self.at <= self.after_hc, self.at - self.after_hc
        self.at = lat_end
        self.junk = self.place("latent_junk", [P, QR])
        self.diag = self.place("latent_diag", [P, T, P])
        for lo, w, dst, gn in ((0, QR, cq, c["q_norm"]), (QR, KVR, ckv, c["kv_norm"])):
            self.norm_features([lat[:, t, lo:lo + w] for t in range(T)], w, [(dst, t * P) for t in range(T)],
                               cols[:, gn:gn + w // P], [])
            self.fence()
        self.at = body
        qT = self.place("mla_qT", [NOPE + LROPE, 4, 768])
        kT = self.place("mla_kT", [NOPE + LROPE, 4, 768])
        v = self.place("mla_v", [P, T, 4, LV])
        tok = Ring([self.place(f"mla_token_tile{j}", [P, 4, NOPE + LROPE]) for j in range(3)])
        scale = float((NOPE + LROPE) ** -0.5)
        tiny = self.tiny
        sizes = tiny[:, 128:256]
        stat = Ring([(sizes[:, 2 * j:2 * j + 1], sizes[:, 2 * j + 1:2 * j + 2]) for j in range(4)])
        proj_ready = [act.now(), dve.now()]
        last_use = []

        for g in range(4):
            heads = {}

            def turned(z, r, t, dst, what):
                b, = self.some_banks(1)

                def tr(e):
                    for h in range(4):
                        e.transpose(b.buf[0:96, h * P:(h + 1) * P], z.buf[:, h, :], self.ident)
                tt = pe.step(tr, [r] + b.free)
                o = act.step(lambda e: e.activation(dst[:, :, t * P:(t + 1) * P], b.buf[0:96, :].rearrange("p (h t) -> p h t", h=4), ACT.Copy), [tt] + last_use)
                b.free, z.free = [o], [tt]
                heads[what, t] = o

            def evac_q(t, bank, made):
                z = tok.take()
                a = act.step(lambda e: e.activation(z.buf[:, :, :], bank.rearrange("p (h d) -> p h d", h=4), ACT.Copy), [made] + z.free)
                r = a
                if t < XT:
                    dve.pending.append(a)
                    r = self.axial(z.buf[:, :, NOPE:], z.buf[:, :, NOPE:], t, 4)
                turned(z, r, t, qT, "q")
                return [a]

            def evac_kv(t, bank, made):
                z = tok.take()
                b4 = bank.rearrange("p (h d) -> p h d", h=4)
                a = act.step(lambda e: e.activation(z.buf[:, :, 0:NOPE], b4[:, :, 0:NOPE], ACT.Copy), [made] + z.free)
                d = dve.step(lambda e: e.tensor_copy(z.buf[:, :, NOPE:], krot[:, t, :].unsqueeze(1).broadcast_to([P, 4, LROPE])), z.free)
                d2 = dve.step(lambda e: e.tensor_copy(v[:, t, :, :], b4[:, :, NOPE:]), [a] + last_use)
                heads["v", t] = d2
                pe.pending.append(a)
                turned(z, d2, t, kT, "k")
                return [d2]
            for name, src, kn, w, ev in (("uq", cq, 3, 384, evac_q), ("ukv", ckv, 2, 512, evac_kv)):
                for _ in self.to_tokens([(f"{name}.{g}", 0, kn)], [(src, t) for t in range(T)], w, self.some_banks(T), ev, proj_ready):
                    pass
            banks = self.banks
            pair = lambda b: self.ps[:, b:b + 2, :].rearrange("p b n -> p (b n)")
            s_turn = [0]
            state = {}

            def scores(u):
                h, t = units[u]
                b = 2 * (u % 2)
                s = pair(b)
                n, k0 = (768, 0) if t < XT else (CTX, SEQ)
                need = [heads["q", t]] + [heads["k", j] for j in range(k0 // P, T)] + banks[b].free + banks[b + 1].free

                def mm(e):
                    for lo in range(0, n, 512):
                        w = min(512, n - lo)
                        e.matmul(s[:, lo:lo + w], qT[:, h, t * P:(t + 1) * P], kT[:, h, k0 + lo:k0 + lo + w], start=True, stop=True)
                m = pe.step(mm, need)
                st = stat.take()
                mx, ls = st.buf
                dve.step(lambda e: e.tensor_reduce(mx, s[:, 0:n], AX_X, ALU.max), [m] + st.free)
                d = dve.step(lambda e: e.tensor_scalar(mx, mx, -scale, None, ALU.mult))
                p = prob.take()
                a = act.step(lambda e: e.activation(p.buf[:, 0:n], s[:, 0:n], ACT.Exp, bias=mx, scale=scale, accum_out=ls), [d] + p.free)
                banks[b].free = banks[b + 1].free = [a]
                state[u] = (p, n, k0, st, a)

            def turn(u):
                p, n, k0, st, a = state[u]
                s = pair(4)

                def tr(e):
                    for j in range(n // P):
                        e.transpose(s[:, j * P:(j + 1) * P], p.buf[:, j * P:(j + 1) * P], self.ident)
                t = pe.step(tr, [a] + banks[4].free + banks[5].free)
                p.free = [t]
                q = probT.take()
                w = min(n, 512)
                d = dve.step(lambda e: e.tensor_copy(q.buf[:, 0:w], s[:, 0:w]), [t] + q.free)
                copied = [d]
                if n > 512:
                    a2 = act.step(lambda e: e.activation(q.buf[:, 512:n], s[:, 512:n], ACT.Copy), [t] + q.free)
                    copied.append(a2)
                    banks[5].free = [a2]
                banks[4].free = [d]
                state[u] = (q, n, k0, st, a, copied)

            def values(u):
                h, t = units[u]
                q, n, k0, st, a, copied = state[u]
                ob = banks[6 + u % 2]

                def pv(e):
                    for j in range(n // P):
                        e.matmul(ob.buf[:, 0:LV], q.buf[:, j * P:(j + 1) * P], v[:, k0 // P + j, h, :], start=(j == 0), stop=(j == n // P - 1))
                m = pe.step(pv, copied + [heads["v", j] for j in range(k0 // P, T)] + ob.free)
                q.free = [m]
                ls = st.buf[1]
                dve.step(lambda e: e.reciprocal(ls, ls), [a])
                col = slice((4 * g + h) * LV, (4 * g + h + 1) * LV)
                d = dve.step(lambda e: e.scalar_tensor_tensor(gate[:, t, col], ob.buf[:, 0:LV], ls, gate[:, t, col], ALU.mult, ALU.mult), [m])
                ob.free, st.free = [d], [d]
            units = [(h, t) for h in range(4) for t in range(T)]
            for s in range(len(units) + 2):
                if s < len(units):
                    scores(s)
                if 1 <= s <= len(units):
                    turn(s - 1)
                if s >= 2:
                    values(s - 2)
            last_use = [pe.now()]

        self.fence()
        self.at = self.hx_at
        oT = Split(self.place("mla_oT_hi", [P, KT, 768], F32R), self.place("mla_oT_lo", [P, KT, 768], F32R))
        assert self.at <= self.after_hc
        ready = self.to_feature_major([gate[:, t, :] for t in range(T)], oT)
        self.fence()
        self.at = body
        gated = Ring([self.place(f"gated_out{j}", [P, 512]) for j in range(2)])
        for g in range(2):
            def evac_o(t, bank, made):
                sl = slice(g * 512, (g + 1) * 512)
                z = gated.take()
                res = self.x[:, t, sl] if t < XT else self.ctx_res[:, t - XT, sl]
                gb = gate_bc[0 if t < XT else 1]
                d = dve.step(lambda e: e.tensor_tensor(z.buf[:, :], bank, gb[:, sl], ALU.mult), [made] + z.free)
                d2 = dve.step(lambda e: e.tensor_tensor(res, res, z.buf[:, :], ALU.add))
                z.free = [d2]
                return [d]
            for _ in self.to_tokens([(f"mla_o{g}.{i}", 4 * i, 4) for i in range(2)], [(oT, t) for t in range(T)], 512, self.some_banks(T), evac_o, ready):
                pass
        self.x_ready = [dve.now()]

    def axial(self, src, dst, t, heads):
        dve = self.dve
        at = C_AX + t * 64
        co = self.cst[:, at:at + 32].unsqueeze(1).broadcast_to([P, heads, 32])
        si = self.cst[:, at + 32:at + 64].rearrange("p (f c d) -> p f c d", f=2, c=2)
        tmp = self.rope_tmp[:, 0:heads * 32].rearrange("p (h d) -> p h d", h=heads)
        for f in range(2):
            for half in range(2):
                a, b = f * 16 + 8 * half, f * 16 + 8 * (1 - half)
                dve.step(lambda e: e.tensor_tensor(tmp[:, :, a:a + 8], src[:, :, b:b + 8], si[:, f, half, :].unsqueeze(1).broadcast_to([P, heads, 8]), ALU.mult))
        dve.step(lambda e: e.tensor_tensor(dst, src, co, ALU.mult))
        return dve.step(lambda e: e.tensor_tensor(dst, dst, tmp, ALU.add))

    def to_feature_major(self, tiles, dst):
        n = len(tiles)
        for k in range(KT):
            for lo in range(0, n, 4):
                m = min(4, n - lo)
                b, = self.some_banks(1)

                def tr(e):
                    for j in range(m):
                        e.transpose(b.buf[:, j * P:(j + 1) * P], tiles[lo + j][:, k * P:(k + 1) * P], self.ident)
                t = self.pe.step(tr, b.free)
                b.free = self.put_split(dst, (slice(None), k, slice(lo * P, (lo + m) * P)), b.buf[:, 0:m * P], [t])
        return [self.act.now(), self.dve.now()]

    def gla(self):
        pe, dve, act, pool, c, cols, cst = self.pe, self.dve, self.act, self.pool, self.c, self.cols, self.cst
        T = XT + CT
        marks = self.fence()
        self.at = self.after_hc
        self.place("context_residual_kept", [P, CT, DM])
        hc_at = self.hc_at
        self.hc = Split(self.nc.alloc_sbuf_tensor_at("gla_hc_hi", [P, KT, CTX], F32R, offset=hc_at),
                        self.nc.alloc_sbuf_tensor_at("gla_hc_lo", [P, KT, CTX], F32R, offset=hc_at + KT * CTX * 4))
        self.at = self.after_hc
        v = self.place("gla_v", [P, T, DM])
        body = self.at
        gate_bc = self.place("gla_mod_gate", [P, DM])
        gain, shift = self.place("gla_mod_gain", [P, 2, 8]), self.place("gla_mod_shift", [P, 2, 8])
        q = self.place("gla_q", [P, GH, SEQ])
        kept = self.at
        mod = self.modulation(1, [gate_bc], gain, shift, self.place)
        self.at = kept
        self.fence()
        ready = self.modulated_norm(gain, shift, [mod])
        self.at = kept
        k = self.place("gla_k", [P, GH, 768])
        cum = [self.place("gla_decay_fwd", [P, GH, T, GC + 1]), self.place("gla_decay_bwd", [P, GH, T, GC + 1])]
        end = self.at
        self.at = self.after_hc
        rtok = self.place("gla_rank_tok", [P, T, 32])
        rT = self.place("gla_rankT", [32, 768])
        wg = self.place("gla_gate_w", [32, 2, 512])
        lin = Ring([self.place(f"gla_gate_lin{j}", [P, 512]) for j in range(2)])
        lg = Ring([self.place(f"gla_gate_log{j}", [P, 512]) for j in range(2)])
        ones = self.place("gla_ones", [P, P])
        marks = self.fence()
        z = pool.step(lambda e: e.memset(wg[:, :, :], 0.0))
        z1 = pool.step(lambda e: e.memset(ones[:, :], 1.0))
        z2 = pool.step(lambda e: e.memset(cum[0][:, :, :, 0:1], 0.0))
        z3 = pool.step(lambda e: e.memset(cum[1][:, :, :, 0:1], 0.0))
        w1 = self.small.load(wg[0:GRANK, 0, :], self.ins["gla_w_gf_2"][0], after=[z])
        w2 = self.small.load(wg[GRANK:2 * GRANK, 1, :], self.ins["gla_w_gb_2"][0], after=[z])
        srcs = [(self.hx, t) for t in range(XT)] + [(self.hc, t) for t in range(CT)]
        for _ in self.to_tokens([("gla_r", 0, 8)], srcs, 32, self.some_banks(T),
                                lambda t, bank, made: [act.step(lambda e: e.activation(rtok[:, t, :], bank, ACT.Copy), [made])], ready):
            pass
        for lo in (0, 4):
            m = min(4, T - lo)
            b, = self.some_banks(1)

            def tr(e):
                for j in range(m):
                    e.transpose(b.buf[0:32, j * P:(j + 1) * P], rtok[:, lo + j, :], self.ident)
            t = pe.step(tr, [act.now()] + b.free)
            b.free = [act.step(lambda e: e.activation(rT[:, lo * P:(lo + m) * P], b.buf[0:32, 0:m * P], ACT.Copy), [t])]
        r_ready = act.now()
        for d_ in range(2):
            for m in range(GH):
                for lo, n in ((0, SEQ), (SEQ, CTX)):
                    b, = self.some_banks(1)
                    t = pe.step(lambda e: e.matmul(b.buf[:, 0:n], wg[:, d_, m * P:(m + 1) * P], rT[:, lo:lo + n], start=True, stop=True), [r_ready, w1, w2] + b.free)
                    x_, l_ = lin.take(), lg.take()
                    bc = cols[:, c["gla_b"] + 4 * d_ + m:c["gla_b"] + 4 * d_ + m + 1]
                    a = act.step(lambda e: e.activation(x_.buf[:, 0:n], b.buf[:, 0:n], ACT.Identity, bias=bc), [t] + x_.free)
                    b.free = [a]
                    act.step(lambda e: e.activation(l_.buf[:, 0:n], x_.buf[:, 0:n], ACT.Abs), l_.free)
                    act.step(lambda e: e.activation(l_.buf[:, 0:n], l_.buf[:, 0:n], ACT.Exp, scale=-1.0))
                    a = act.step(lambda e: e.activation(l_.buf[:, 0:n], l_.buf[:, 0:n], ACT.Ln, bias=1.0))
                    d = dve.step(lambda e: e.scalar_tensor_tensor(l_.buf[:, 0:n], x_.buf[:, 0:n], 0.0, l_.buf[:, 0:n], ALU.min, ALU.subtract), [a])
                    x_.free = [d]
                    for ch in range(n // P):
                        d = dve.step(lambda e: e.tensor_tensor_scan(cum[d_][:, m, lo // P + ch, 1:GC + 1], ones[:, :], l_.buf[:, ch * P:(ch + 1) * P], 0.0, ALU.mult, ALU.add), [z1])
                    l_.free = [d]

        def evac_k(m, cx, bank, made):
            n0 = 0 if cx == 0 else SEQ
            return [act.step(lambda e: e.activation(k[:, m, n0:n0 + bank.shape[1]], bank, ACT.Copy), [made])]
        self.to_both([(f"gla_k.{i}", 4 * i, 4) for i in range(2)], (self.hx, self.hc), self.some_banks(8), evac_k, ready)
        for _ in self.to_features([(f"gla_q.{i}", 4 * i, 4) for i in range(2)], self.hx, SEQ, self.some_banks(4),
                                  lambda m, bank, made: [act.step(lambda e: e.activation(q[:, m, :], bank, ACT.Copy, scale=GDK ** -0.5), [made])], ready):
            pass
        self.fence()
        for g in range(2):
            for _ in self.to_tokens([(f"gla_v{g}.{i}", 4 * i, 4) for i in range(2)], srcs, 512, self.some_banks(T),
                                    lambda t, bank, made: [act.step(lambda e: e.activation(v[:, t, g * 512:(g + 1) * 512], bank, ACT.Copy), [made])], ready):
                pass
        self.fence()
        self.at = self.hc_at
        gate = self.place("gla_gate", [P, XT, DM])
        assert self.at <= self.after_hc
        for g in range(2):
            for _ in self.to_tokens([(f"gla_g{g}.{i}", 4 * i, 4) for i in range(2)], srcs[0:XT], 512, self.some_banks(XT),
                                    lambda t, bank, made: [act.step(lambda e: e.activation(gate[:, t, g * 512:(g + 1) * 512], bank, ACT.Silu), [made])], ready):
                pass

        self.fence()
        self.at = self.hx_at
        o = self.place("gla_o", [P, XT, DM])
        S = [self.place("gla_state_fwd", [P, GH, GDV]), self.place("gla_state_bwd", [P, GH, GDV])]
        tot, etot = self.place("gla_total", [P, 2, GH * T]), self.place("gla_total_decay", [P, 2, GH * T])
        small4 = lambda n: Ring([self.place(f"{n}{j}", [P, P]) for j in range(2)])
        Qt, Qh, Kd, KdT = small4("gla_Qt"), small4("gla_Qh"), small4("gla_Kd"), small4("gla_KdT")
        A = [small4("gla_A_fwd"), small4("gla_A_bwd")]
        assert self.at <= self.hc_at
        self.at = end
        D = Ring([self.place(f"gla_D{j}", [P, 640]) for j in range(2)])
        Kt = Ring([self.place(f"gla_Kt{j}", [P, 4, P]) for j in range(2)])
        for d_ in range(2):
            dve.step(lambda e: e.tensor_scalar(tot[:, d_, :].rearrange("p (h t) -> p h t", h=GH), cum[d_][:, :, :, GC], 1.0 / GATE_NORM, None, ALU.mult))
            for s in A[d_].slots:
                s.free = [pool.step(lambda e: e.memset(s.buf[:, :], 0.0))]
        act.step(lambda e: e.activation(etot[:, :, :], tot[:, :, :], ACT.Exp), [dve.now()])
        dve.pending.append(act.now())
        masks = [cst[:, C_UP:C_UP + P].bitcast(I32), cst[:, C_LOW:C_LOW + P].bitcast(I32)]
        o_written = {}
        inv = 1.0 / GATE_NORM

        def scan(d_, h):
            fwd = d_ == 0
            chunks = [4, 5, 0, 1, 2, 3] if fwd else [5, 4, 3, 2, 1, 0]
            s_state = S[d_][:, h, :]
            state_ready, state_read = [], []
            for step, ch in enumerate(chunks):
                cc = cum[d_][:, h, ch, :]
                sh = 1 if fwd else 0
                tcol = tot[:, d_, h * T + ch:h * T + ch + 1]
                kk = k[:, h, ch * P:(ch + 1) * P]
                if ch < XT:
                    qq = q[:, h, ch * P:(ch + 1) * P]
                    Dd, kt, qt, qh = D.take(), Kt.take(), Qt.take(), Qh.take()

                    def diffs(e):
                        for I in range(GC // GB):
                            r = cc[:, I * GB + GB // 2:I * GB + GB // 2 + 1]
                            e.tensor_scalar(Dd.buf[:, I * P:(I + 1) * P], cc[:, sh:sh + P], r, (-80.0 if fwd else 80.0) * GATE_NORM,
                                            ALU.subtract, ALU.max if fwd else ALU.min)
                    dd = dve.step(diffs, Dd.free)
                    yield
                    a = act.step(lambda e: e.activation(kt.buf[:, :, :], Dd.buf[:, 0:512].rearrange("p (b n) -> p b n", b=4), ACT.Exp, scale=-inv if fwd else inv), [dd] + kt.free)
                    diag = Dd.buf[:, :].rearrange("p (b n) -> p b n", n=P + GB)[:, :, 0:GB]
                    a2 = act.step(lambda e: e.activation(qt.buf[:, :].rearrange("p (b n) -> p b n", b=4), diag, ACT.Exp, scale=inv if fwd else -inv), qt.free)
                    Dd.free = [a2]
                    if fwd:
                        a3 = act.step(lambda e: e.activation(qh.buf[:, :], cc[:, 1:P + 1], ACT.Exp, scale=inv), qh.free)
                    else:
                        a3 = act.step(lambda e: e.activation(qh.buf[:, :], cc[:, 0:P], ACT.Exp, scale=-inv, bias=tcol), qh.free)
                    d1 = dve.step(lambda e: e.tensor_tensor(kt.buf[:, :, :], kt.buf[:, :, :], kk.unsqueeze(1).broadcast_to([P, 4, P]), ALU.mult), [a])
                    d2 = dve.step(lambda e: e.tensor_tensor(qt.buf[:, :], qt.buf[:, :], qq, ALU.mult), [a2])
                    d3 = pool.step(lambda e: e.tensor_tensor(qh.buf[:, :], qh.buf[:, :], qq, ALU.mult), [a3])
                    yield
                    b, = self.some_banks(1)

                    def am(e):
                        for I in range(4):
                            e.matmul(b.buf[:, I * GB:(I + 1) * GB], kt.buf[:, I, :], qt.buf[:, I * GB:(I + 1) * GB], start=True, stop=True)
                    t = pe.step(am, [d1, d2] + b.free)
                    kt.free, qt.free = [t], [t]
                    at_ = A[d_].take()
                    d4 = dve.step(lambda e: e.copy_predicated(at_.buf[:, :], masks[d_], b.buf[:, 0:P]), [t] + at_.free)
                    b.free = [d4]
                    yield
                    ob, = self.some_banks(1)

                    def om(e):
                        e.matmul(ob.buf[:, 0:GDV], qh.buf[:, :], s_state, start=True, stop=False)
                        e.matmul(ob.buf[:, 0:GDV], at_.buf[:, :], v[:, ch, h * GDV:(h + 1) * GDV], start=False, stop=True)
                    t = pe.step(om, [d3, d4] + state_ready + ob.free)
                    qh.free, at_.free, state_read = [t], [t], [t]
                    oc = o[:, ch, h * GDV:(h + 1) * GDV]
                    if (ch, h) in o_written:
                        ob.free = [dve.step(lambda e: e.tensor_tensor(oc, ob.buf[:, 0:GDV], oc, ALU.add), [t, o_written[ch, h]])]
                    else:
                        ob.free = [act.step(lambda e: e.activation(oc, ob.buf[:, 0:GDV], ACT.Copy), [t])]
                    o_written[ch, h] = ob.free[0]
                    yield
                if step < len(chunks) - 1:
                    kd, kdt = Kd.take(), KdT.take()
                    if fwd:
                        a = act.step(lambda e: e.activation(kd.buf[:, :], cc[:, 1:P + 1], ACT.Exp, scale=-inv, bias=tcol), kd.free)
                    else:
                        a = act.step(lambda e: e.activation(kd.buf[:, :], cc[:, 0:P], ACT.Exp, scale=inv), kd.free)
                    m_ = pool.step(lambda e: e.tensor_tensor(kd.buf[:, :], kd.buf[:, :], kk, ALU.mult), [a])
                    b, = self.some_banks(1)
                    t = pe.step(lambda e: e.transpose(b.buf[:, 0:P], kd.buf[:, :], self.ident), [m_] + b.free)
                    kd.free = [t]
                    a = act.step(lambda e: e.activation(kdt.buf[:, :], b.buf[:, 0:P], ACT.Copy), [t] + kdt.free)
                    b.free = [a]
                    yield
                    b, = self.some_banks(1)
                    t = pe.step(lambda e: e.matmul(b.buf[:, 0:GDV], kdt.buf[:, :], v[:, ch, h * GDV:(h + 1) * GDV], start=True, stop=True), [a] + b.free)
                    kdt.free = [t]
                    if step == 0:
                        s2 = dve.step(lambda e: e.tensor_copy(s_state, b.buf[:, 0:GDV]), [t])
                    else:
                        et = etot[:, d_, h * T + ch:h * T + ch + 1]
                        s2 = dve.step(lambda e: e.scalar_tensor_tensor(s_state, s_state, et, b.buf[:, 0:GDV], ALU.mult, ALU.add), [t] + state_read)
                    b.free, state_ready = [s2], [s2]
                    yield
        def run_heads(hs):
            for h in hs:
                for d_ in range(2):
                    yield from scan(d_, h)
        interleave(run_heads([0, 1]), run_heads([2, 3]))

        self.fence()
        self.at = end
        orow = self.place("gla_norm_row", [P, GDV])
        sq = self.place("gla_square", [P, DM])
        gated = Ring([self.place(f"gla_gated_out{j}", [P, 512]) for j in range(2)])
        rl = self.small.load(orow[:, :], self.ins["gla_o_norm_2"][0].partition_broadcast(P), after=self.fence())
        rs = self.tiny[:, 0:16]
        H = lambda ap: ap.rearrange("p (h d) -> p h d", h=GH)
        for t in range(XT):
            dve.step(lambda e: e.tensor_tensor(sq[:, :], o[:, t, :], o[:, t, :], ALU.mult))
            dve.step(lambda e: e.tensor_reduce(rs[:, 4 * t:4 * t + 4], H(sq[:, :]), AX_X, ALU.add))
        d = dve.step(lambda e: e.tensor_scalar(rs, rs, 1.0 / GDV, EPS, ALU.mult, ALU.add))
        a = act.step(lambda e: e.activation(rs, rs, ACT.Sqrt), [d])
        dve.step(lambda e: e.reciprocal(rs, rs), [a])
        for t in range(XT):
            dve.step(lambda e: e.tensor_tensor(H(gate[:, t, :]), H(gate[:, t, :]), orow[:, :].unsqueeze(1).broadcast_to([P, GH, GDV]), ALU.mult), [rl])
            for h in range(GH):
                sl = slice(h * GDV, (h + 1) * GDV)
                dve.step(lambda e: e.scalar_tensor_tensor(gate[:, t, sl], o[:, t, sl], rs[:, 4 * t + h:4 * t + h + 1], gate[:, t, sl], ALU.mult, ALU.mult))
        self.fence()
        self.hx = Split(self.nc.alloc_sbuf_tensor_at("gla_oT_hi", [P, KT, SEQ], F32R, offset=self.hx_at),
                        self.nc.alloc_sbuf_tensor_at("gla_oT_lo", [P, KT, SEQ], F32R, offset=self.hx_at + KT * SEQ * 4))
        ready = self.to_feature_major([gate[:, t, :] for t in range(XT)], self.hx)
        for g in range(2):
            def evac_o(t, bank, made):
                sl = slice(g * 512, (g + 1) * 512)
                z = gated.take()
                d = dve.step(lambda e: e.tensor_tensor(z.buf[:, :], bank, gate_bc[:, sl], ALU.mult), [made] + z.free)
                z.free = [dve.step(lambda e: e.tensor_tensor(self.x[:, t, sl], self.x[:, t, sl], z.buf[:, :], ALU.add))]
                return [d]
            for _ in self.to_tokens([(f"gla_o{g}.{i}", 4 * i, 4) for i in range(2)], [(self.hx, t) for t in range(XT)], 512, self.some_banks(XT), evac_o, ready):
                pass
        self.x_ready = [dve.now()]
        self.at = self.hc_at

    def units(self, name, a, c0, n=512, k0=0, kn=8, per=4, raw=False):
        v = a.rearrange("(k p) n -> p k n", p=P)
        if kn <= per:
            return [(name, v[:, k0:k0 + kn, c0:c0 + n], kn, n, raw)]
        return [(f"{name}.{i}", v[:, k0 + i * per:k0 + (i + 1) * per, c0:c0 + n], per, n, raw) for i in range(kn // per)]

    def second_plan(self, mla=True, gla=True):
        ins, plan = self.ins, []
        ada = lambda i: [u for g in range(6) for u in self.units(f"ada{i}.{g}", ins["ada_w_2"][i], 512 * g, raw=True)]
        if mla:
            plan += ada(0)
            w = ins["mla_w_in_2"][0]
            for n, c0, cn in (("l0", 0, 512), ("l1", 512, 160), ("g0", LAT, 512), ("g1", LAT + 512, 512)):
                plan += self.units(f"mla_{n}", w, c0, cn)
            for g in range(4):
                plan += self.units(f"uq.{g}", ins["mla_w_uq_2"][0], 384 * g, 384, kn=3)
                plan += self.units(f"ukv.{g}", ins["mla_w_ukv_2"][0], 512 * g, kn=2)
            for g in range(2):
                plan += self.units(f"mla_o{g}", ins["mla_w_out_2"][0], 512 * g)
        if gla:
            plan += ada(1)
            w = ins["gla_w_in_2"][0]
            plan += self.units("gla_r", w, 3072, 32, per=8)
            plan += self.units("gla_k", w, 512)
            plan += self.units("gla_q", w, 0)
            for n, c0 in (("v", 1024), ("g", 2048)):
                for g in range(2):
                    plan += self.units(f"gla_{n}{g}", w, c0 + 512 * g)
            for g in range(2):
                plan += self.units(f"gla_o{g}", ins["gla_w_out_2"][0], 512 * g)
        return plan


def build(nc, ins, out):
    with ExitStack() as ctx:
        p = Program(nc, ins, out, ctx)
        p.setup()
        plan = []
        for l in range(DEPTH):
            plan += p.layer_plan(l)
        plan += p.second_plan()
        p.plan_weights(plan)
        for l in range(DEPTH):
            p.layer(l)
        p.at = p.hc_at
        p.final_norm("final_norm_w")
        p.mla()
        p.gla()
        p.final_norm("final_g_2")
        xs = out.rearrange("(t p) d -> p t d", p=P)
        p.finish = (xs, p.x_ready)
        block = ctx.enter_context(nc.Block())

        @block.sync
        def _(e):
            emit(e, p.sp_queue)
            for s, v in p.finish[1]:
                e.wait_ge(s, v)
            e.dma_start(p.finish[0], p.x[:, :, :]).then_inc(p.out_sem, 16)
            e.wait_ge(p.out_sem, 16)

        @block.gpsimd
        def _(e):
            emit(e, p.pool.queue)

        @block.scalar
        def _(e):
            emit(e, p.act.queue)

        @block.vector
        def _(e):
            emit(e, p.dve.queue)

        @block.tensor
        def _(e):
            emit(e, p.pe.queue)


_INS = ['x', 'positions', 'norm_mix_w', 'w_in', 'b_in', 'conv_w', 'conv_b', 'mlstm_norm_w', 'w_proj_att',
        'w_proj_mlstm', 'w_out', 'norm_mlp_w', 'w_ff1', 'w_ff2', 'final_norm_w', 'c_2', 'ctx_2', 'c_ctx_2', 'ada_w_2',
        'ada_b_2', 'norm_g_2', 'final_g_2', 'mla_w_in_2', 'mla_q_norm_2', 'mla_w_uq_2', 'mla_kv_norm_2',
        'mla_w_ukv_2', 'mla_w_out_2', 'gla_w_in_2', 'gla_w_gf_2', 'gla_b_gf_2', 'gla_w_gb_2', 'gla_b_gb_2',
        'gla_o_norm_2', 'gla_w_out_2']


def kernel(**inputs):
    import numpy as _np
    import concourse.bacc as _bacc
    from concourse import mybir as _mybir
    from concourse.bass_utils import run_bass_kernel_spmd as _run

    nc = _bacc.Bacc("TRN2", target_bir_lowering=False, num_devices=1)
    arrays, ins = {}, {}
    for name in _INS:
        arrays[f"in_{name}"] = _np.ascontiguousarray(inputs[name])
    arrays["in_constants"] = constants()
    for name, a in arrays.items():
        ins[name[3:]] = nc.dram_tensor(name, a.shape, _mybir.dt.from_np(a.dtype), kind="ExternalInput").ap()
    out = nc.dram_tensor("out_x", (SEQ, DM), _mybir.dt.float32, kind="ExternalOutput").ap()
    build(nc, ins, out)
    r = _run(nc, [arrays], core_ids=[0])
    return r.results[0]["out_x"].reshape(1, SEQ, DM)
```

```python
from contextlib import ExitStack

import numpy as np

import concourse.bass as bass
from concourse import mybir

P = 128
F32 = mybir.dt.float32
F32R = mybir.dt.float32r
I32 = mybir.dt.int32
ALU = mybir.AluOpType
ACT = mybir.ActivationFunctionType
AX_X = mybir.AxisListType.X

SEQ, CTX, DM = 512, 256, 1024
XT, CT, KT = SEQ // P, CTX // P, DM // P
DEPTH = 2
EPS = 1e-6
NEG = -1e30

AH, AHD = 8, 64
MH, MHD = 4, 128
ROPE_HALF = 8
CONV = 4
COL_AQ, COL_AK, COL_AV, COL_MQ, COL_MV, COL_MO, COL_MI, COL_GA, COL_GB, D_IN = (
    0, 512, 1024, 1536, 2560, 3072, 3584, 3592, 4616, 5640)
D_FF = 4096
PATTERNS = ((128, 1), (512, 4), (2048, 16))
ROPE_THETA = 500000.0

LH, NOPE, LROPE, LV = 16, 64, 32, 64
QR, KVR = 384, 256
LAT = QR + KVR + LROPE
GH, GDK, GDV, GRANK = 4, 128, 256, 16
GC = 128
GB = 32
GATE_NORM = 16.0

UNIT = 2048

C_ID, C_ATT, C_TRI, C_UP, C_ONES, C_NSEL, C_SEL2, C_AX, C_INV, C_LOW, C_END = (
    0, 128, 640, 768, 896, 1024, 1536, 1792, 2048, 2056, 2184)


def constants():
    c = np.zeros((P, C_END), np.float32)
    p = np.arange(P)
    c[:, C_ID:C_ID + P] = np.eye(P)
    d = p[:, None] + 3 * P - np.arange(4 * P)[None, :]
    n = sum(((d >= 0) & (d <= w) & (d % s == 0)).astype(np.float64) for w, s in PATTERNS)
    c[:, C_ATT:C_ATT + 512] = np.where(n > 0, np.log(np.maximum(n, 1)) * AHD ** 0.5, NEG)
    c[:, C_TRI:C_TRI + P] = np.where(p[:, None] <= p[None, :], 0.0, NEG)
    c[:, C_UP:C_UP + P] = p[:, None] <= p[None, :]
    c[:, C_LOW:C_LOW + P] = p[:, None] >= p[None, :]
    c[:, C_ONES:C_ONES + P] = 1.0
    for h in range(MH):
        c[h, C_NSEL + h * P:C_NSEL + (h + 1) * P] = -1.0
    for r in range(2):
        c[r, C_SEL2 + r * P:C_SEL2 + (r + 1) * P] = 1.0
    inv = (10000.0 ** (-np.arange(8, dtype=np.float32) / 8)).astype(np.float32)
    tok = np.arange(SEQ)
    for t in range(XT):
        at = C_AX + t * 64
        for half, pos in enumerate((tok // 64, tok % 64)):
            ang = (pos[t * P:(t + 1) * P, None].astype(np.float32) * inv).astype(np.float32)
            co, si = np.cos(ang), np.sin(ang)
            c[:, at + half * 16:at + half * 16 + 16] = np.concatenate([co, co], 1)
            c[:, at + 32 + half * 16:at + 48 + half * 16] = np.concatenate([-si, si], 1)
    c[:, C_INV:C_INV + 8] = (np.float32(ROPE_THETA) ** (-np.arange(0, 16, 2, dtype=np.float32) / 16))
    return c


def _queued(call):
    def queue(self, *args, **kwargs):
        self.calls.append((call, args, kwargs))
    return queue


class Calls:

    def __init__(self):
        self.calls = []

    matmul = _queued(lambda e, a, k: e.matmul(*a, **k))
    transpose = _queued(lambda e, a, k: e.transpose(*a, **k))
    activation = _queued(lambda e, a, k: e.activation(*a, **k))
    tensor_tensor = _queued(lambda e, a, k: e.tensor_tensor(*a, **k))
    tensor_scalar = _queued(lambda e, a, k: e.tensor_scalar(*a, **k))
    scalar_tensor_tensor = _queued(lambda e, a, k: e.scalar_tensor_tensor(*a, **k))
    tensor_tensor_reduce = _queued(lambda e, a, k: e.tensor_tensor_reduce(*a, **k))
    tensor_tensor_scan = _queued(lambda e, a, k: e.tensor_tensor_scan(*a, **k))
    tensor_reduce = _queued(lambda e, a, k: e.tensor_reduce(*a, **k))
    tensor_copy = _queued(lambda e, a, k: e.tensor_copy(*a, **k))
    copy_predicated = _queued(lambda e, a, k: e.copy_predicated(*a, **k))
    reciprocal = _queued(lambda e, a, k: e.reciprocal(*a, **k))
    dma_start = _queued(lambda e, a, k: e.dma_start(*a, **k))
    memset = _queued(lambda e, a, k: e.memset(*a, **k))


def emit(e, queue):
    reached = {}
    for waits, calls, sem, increment in queue:
        for w, value in waits:
            if value > reached.get(w.name, 0):
                e.wait_ge(w, value)
                reached[w.name] = value
        for call, args, kwargs in calls:
            last = call(e, args, kwargs)
        last.then_inc(sem, increment)


class Engine:

    def __init__(self, done, in_order=False):
        self.done, self.in_order = done, in_order
        self.count, self.queue, self.pending = 0, [], []

    def now(self):
        return (self.done, self.count)

    def step(self, issue, after=()):
        waits = list(after) + self.pending
        self.pending = []
        if not self.in_order:
            waits.append(self.now())
        most = {}
        for sem, value in waits:
            if value > most.get(sem.name, (sem, 0))[1]:
                most[sem.name] = (sem, value)
        self.count += 1
        step = Calls()
        issue(step)
        self.queue.append((list(most.values()), step.calls, self.done, 1))
        return (self.done, self.count)


class Loads:

    def __init__(self, sems, queue):
        self.sems, self.counts, self.n, self.queue = sems, [0] * len(sems), 0, queue

    def load(self, out, in_, after=(), strided=False):
        i = self.n % len(self.sems)
        self.n += 1
        waits = list(after)
        if self.counts[i]:
            waits.append((self.sems[i], self.counts[i]))
        self.counts[i] += 16
        step = Calls()
        step.dma_start(out, in_, allow_slow_non_contiguous=strided)
        self.queue.append((waits, step.calls, self.sems[i], 16))
        return (self.sems[i], self.counts[i])


class Slot:

    def __init__(self, buf):
        self.buf, self.free = buf, []


class Ring:
    def __init__(self, bufs):
        self.slots, self.n = [Slot(b) for b in bufs], 0

    def take(self):
        self.n += 1
        return self.slots[(self.n - 1) % len(self.slots)]


class Split:

    def __init__(self, hi, lo):
        self.hi, self.lo = hi, lo


def interleave(*streams):
    live = list(streams)
    while live:
        for entry in list(live):
            for _ in range(entry[1]):
                if next(entry[0], live) is live:
                    live.remove(entry)
                    break


class Program:
    def __init__(self, nc, ins, out, ctx):
        self.nc, self.ins, self.out, self.ctx = nc, ins, out, ctx
        sem = lambda n: ctx.enter_context(nc.semaphore(n))
        self.pe = Engine(sem("pe_done"), in_order=True)
        self.dve = Engine(sem("dve_done"))
        self.act = Engine(sem("act_done"))
        self.pool = Engine(sem("pool_done"))
        self.sp_queue = []
        self.sp = Loads([sem(f"sp_load{i}") for i in range(4)], self.sp_queue)
        self.small = Loads([sem(f"small_load{i}") for i in range(8)], self.pool.queue)
        self.out_sem = sem("out_stored")
        self.gate_rows = nc.dram_tensor("mod_gate_rows", (DEPTH, 2, DM), F32, kind="Internal").ap()
        self.high = 0
        self.high_end = 229344 - 2048
        self.at = 16512
        self.names = self.bank_turn = 0
        self.ps = ctx.enter_context(nc.psum_tensor("ps", [P, 8, 512], F32))
        self.gate_stored = []
        self.banks = [Slot(self.ps[:, i, :]) for i in range(8)]
        self.fixed()

    def place(self, name, shape, dt=F32):
        size = int(np.prod(shape[1:])) * 4
        self.at = (self.at + 31) // 32 * 32
        t = self.nc.alloc_sbuf_tensor_at(f"{name}_{self.names}", list(shape), dt, offset=self.at)
        self.names += 1
        self.at += size
        assert self.at <= 229344, (name, self.at)
        self.high = max(self.high, self.at)
        return t

    def fixed(self):
        self.cst = self.place("constant_columns", [P, C_END])
        self.cols = self.place("feature_columns", [P, 256])
        self.rope = self.place("rope_tables", [P, XT, 32])
        self.tiny = self.place("tiny", [P, 256])
        self.x = self.place("x_residual", [P, XT, DM])
        self.stage = Ring([self.place(f"w_stage{i}", [P, UNIT]) for i in range(2)])
        self.w_split = Ring([Split(self.place(f"w_hi{i}", [P, UNIT], F32R), self.place(f"w_lo{i}", [P, UNIT], F32R))
                             for i in range(2)])
        self.at = (self.at + 31) // 32 * 32
        self.hx_at = self.at
        self.hx = Split(self.place("hx_hi", [P, KT, SEQ], F32R), self.place("hx_lo", [P, KT, SEQ], F32R))
        self.hc_at = self.at
        self.negsel = self.cst[0:MH, C_NSEL:C_NSEL + MH * P].rearrange("p (h n) -> p h n", h=MH)
        self.ident = self.cst[:, C_ID:C_ID + P]
        self.area = None

    def fence(self):
        marks = [e.now() for e in (self.pe, self.dve, self.act, self.pool)] + self.gate_stored
        marks = [m for m in marks if m[1]]
        for e in (self.pe, self.dve, self.act, self.pool):
            e.pending = list(marks)
        return marks

    def plan_weights(self, plan):
        self.plan, self.loaded, self.prepared, self.taken = plan, 0, 0, 0
        self.staged, self.ready, self.released, self.deferred = {}, {}, set(), []

    def refill(self):
        while self.loaded < len(self.plan) and (self.loaded < 2 or self.loaded - 2 in self.released):
            name, src, k, n, raw = self.plan[self.loaded]
            slot = self.stage.take()
            dst = slot.buf[:, 0:k * n].rearrange("p (k n) -> p k n", k=k)
            self.staged[self.loaded] = (slot, dst, self.sp.load(dst, src, after=slot.free))
            self.loaded += 1

    def prepare(self):
        self.refill()
        i = self.prepared
        name, src, k, n, raw = self.plan[i]
        slot, staged, landed = self.staged.pop(i)
        if raw:
            self.ready[i] = (staged, slot, [landed])
        else:
            w = self.w_split.take()
            hi = w.buf.hi[:, 0:k * n].rearrange("p (k n) -> p k n", k=k)
            lo = w.buf.lo[:, 0:k * n].rearrange("p (k n) -> p k n", k=k)
            a = self.act.step(lambda e: e.activation(hi, staged, ACT.Copy), [landed] + w.free)
            b = self.dve.step(lambda e: e.tensor_tensor(lo, staged, hi.bitcast(F32), ALU.subtract), [a, landed] + w.free)
            slot.free = [a, b]
            self.released.add(i)
            self.ready[i] = (Split(hi, lo), w, [a, b])
        self.prepared += 1
        self.refill()

    def take(self, name):
        i = self.taken
        assert self.plan[i][0] == name, (self.plan[i][0], name)
        while self.prepared <= i:
            self.prepare()
        self.taken += 1
        return self.ready.pop(i)

    def prepare_ahead(self):
        if self.prepared == self.taken < len(self.plan) and not self.plan[self.taken][4]:
            self.prepare()

    def defer(self, task):
        self.deferred.append(task)

    def flush(self):
        tasks, self.deferred = self.deferred, []
        for task in tasks:
            task()

    def raw_done(self, slot, ticket):
        slot.free = [ticket]
        self.released.add(self.taken - 1)
        self.refill()

    @staticmethod
    def mm3(e, out, a, b, start, stop):
        e.matmul(out, a[0], b[0], start=start, stop=False)
        e.matmul(out, a[0], b[1], start=False, stop=False)
        return e.matmul(out, a[1], b[0], start=False, stop=stop)

    def to_tokens(self, halves, srcs, nc_, banks, evac, ready=()):
        last = None
        for u, (uname, k0, kn) in enumerate(halves):
            w, slot, rdy = self.take(uname)
            for j, (src, t) in enumerate(srcs):
                bank = banks[j]

                def issue(e, src=src, t=t, bank=bank, w=w, k0=k0, kn=kn, u=u):
                    for k in range(kn):
                        l = self.mm3(e, bank.buf[:, 0:nc_],
                                     (src.hi[:, k0 + k, t * P:(t + 1) * P], src.lo[:, k0 + k, t * P:(t + 1) * P]),
                                     (w.hi[:, k, :], w.lo[:, k, :]),
                                     u == 0 and k == 0, u == len(halves) - 1 and k == kn - 1)
                    return l
                last = self.pe.step(issue, rdy + (bank.free if u == 0 else []) + list(ready))
                if j == 0:
                    self.prepare_ahead()
                tasks, self.deferred = self.deferred, []
                if u == len(halves) - 1:
                    bank.free = evac(j, bank.buf[:, 0:nc_], last)
                for task in tasks:
                    task()
                yield
            slot.free = [last]

    def to_features(self, halves, src, ntok, banks, evac, ready=(), m_tiles=4):
        last = None
        for u, (uname, k0, kn) in enumerate(halves):
            w, slot, rdy = self.take(uname)
            for m in range(m_tiles):
                bank = banks[m]

                def issue(e, m=m, bank=bank, w=w, k0=k0, kn=kn, u=u):
                    for k in range(kn):
                        l = self.mm3(e, bank.buf[:, 0:ntok],
                                     (w.hi[:, k, m * P:(m + 1) * P], w.lo[:, k, m * P:(m + 1) * P]),
                                     (src.hi[:, k0 + k, 0:ntok], src.lo[:, k0 + k, 0:ntok]),
                                     u == 0 and k == 0, u == len(halves) - 1 and k == kn - 1)
                    return l
                last = self.pe.step(issue, rdy + (bank.free if u == 0 else []) + list(ready))
                if m == 0:
                    self.prepare_ahead()
                self.flush()
                if u == len(halves) - 1:
                    bank.free = evac(m, bank.buf[:, 0:ntok], last)
                yield
            slot.free = [last]

    def put_split(self, dst, at, src, after, scale=1.0):
        hi, lo = dst.hi[at], dst.lo[at]
        a = self.act.step(lambda e: e.activation(hi, src, ACT.Identity, scale=scale), after)
        b = self.dve.step(lambda e: e.scalar_tensor_tensor(lo, src, scale, hi.bitcast(F32), ALU.mult, ALU.subtract), [a])
        return [a, b]

    def some_banks(self, n):
        self.bank_turn += n
        return [self.banks[(self.bank_turn - n + i) % 8] for i in range(n)]

    def to_both(self, halves, src, banks, evac, ready=(), m_tiles=4):
        for u, (uname, k0, kn) in enumerate(halves):
            w, slot, rdy = self.take(uname)
            for m in range(m_tiles):
                for c, n in ((0, SEQ), (1, CTX)):
                    bank = banks[2 * m + c]

                    def issue(e):
                        for k in range(kn):
                            self.mm3(e, bank.buf[:, 0:n],
                                     (w.hi[:, k, m * P:(m + 1) * P], w.lo[:, k, m * P:(m + 1) * P]),
                                     (src[c].hi[:, k0 + k, 0:n], src[c].lo[:, k0 + k, 0:n]),
                                     u == 0 and k == 0, u == len(halves) - 1 and k == kn - 1)
                    last = self.pe.step(issue, rdy + (bank.free if u == 0 else []) + list(ready))
                    if m == c == 0:
                        self.prepare_ahead()
                    if u == len(halves) - 1:
                        bank.free = evac(m, c, bank.buf[:, 0:n], last)
            slot.free = [last]

    def rstd(self, srcs, width, out, after):
        n = len(srcs)
        for i, s in enumerate(srcs):
            if i % 2:
                self.dve.step(lambda e: e.tensor_tensor_reduce(out=self.junk2[:, 0:width], in0=s, in1=s, scale=1.0, scalar=0.0,
                                                               op0=ALU.mult, op1=ALU.add, accum_out=out[:, i:i + 1]), after)
            else:
                last = self.act.step(lambda e: e.activation(self.junk[:, 0:width], s, ACT.Square, accum_out=out[:, i:i + 1]), after)
        a = self.dve.step(lambda e: e.tensor_scalar(out[:, 0:n], out[:, 0:n], 1.0 / width, EPS, ALU.mult, ALU.add), [last])
        b = self.act.step(lambda e: e.activation(out[:, 0:n], out[:, 0:n], ACT.Sqrt), [a])
        return self.dve.step(lambda e: e.reciprocal(out[:, 0:n], out[:, 0:n]), [b])

    def norm_features(self, tiles, width, dst, gain, after, bias=None):
        nt, kt = len(tiles), width // P
        r = self.tiny[:, 0:nt]
        ready = self.rstd(tiles, width, r, after)
        for i in range(nt):
            last = self.dve.step(lambda e, i=i: e.tensor_scalar(self.diag[:, i, :], self.ident, r[:, i:i + 1], None, ALU.mult), [ready])
        groups = []
        for lo in range(0, nt, 4):
            groups.append(list(range(lo, min(lo + 4, nt))))
        out = []
        n = 0
        for k in range(kt):
            for g in groups:
                bank = self.banks[n % 8]
                n += 1

                def issue(e, k=k, g=g, bank=bank):
                    for j, i in enumerate(g):
                        l = e.matmul(bank.buf[:, j * P:(j + 1) * P], tiles[i][:, k * P:(k + 1) * P],
                                     self.diag[:, i, :], start=True, stop=True)
                    return l
                t = self.pe.step(issue, [last] + bank.free)
                src = bank.buf[:, 0:len(g) * P]
                d, tok = dst[g[0]]
                at = (slice(None), k, slice(tok, tok + len(g) * P))
                if bias is None:
                    bank.free = self.put_split(d, at, src, [t], gain[:, k:k + 1])
                else:
                    cond = 0 if g[0] < XT else 1
                    tmp = self.nrm_tmp.take()
                    full = tmp.buf[:, 0:len(g) * P]
                    hi, lo = d.hi[at], d.lo[at]
                    gk, bk = gain[:, cond, k:k + 1], bias[:, cond, k:k + 1]
                    if k % 2:
                        a = self.act.step(lambda e: e.activation(full, src, ACT.Identity, scale=gk, bias=bk), [t] + tmp.free)
                    else:
                        a = self.dve.step(lambda e: e.tensor_scalar(full, src, gk, bk, ALU.mult, ALU.add), [t] + tmp.free)
                    b = self.act.step(lambda e, hi=hi, full=full: e.activation(hi, full, ACT.Copy), [a])
                    c = self.dve.step(lambda e, lo=lo, full=full, hi=hi: e.tensor_tensor(lo, full, hi.bitcast(F32), ALU.subtract), [b])
                    bank.free, tmp.free = [a], [c]
                    out.append(c)
                out += bank.free
        return [self.act.now(), self.dve.now()]

    def load_rows_as_columns(self, rows, at):
        n, loads = 0, []
        slab = self.row_slab
        for src in rows:
            r = src.shape[0]
            loads.append(self.small.load(slab[n:n + r, :], src, after=self.slab_free))
            n += r
        bank = self.banks[7]
        t = self.pe.step(lambda e: e.transpose(bank.buf[:, 0:n], slab[0:n, :], self.ident[0:n, 0:n]),
                         loads + [self.cst_ready] + bank.free)
        c = self.dve.step(lambda e: e.tensor_copy(self.cols[:, at:at + n], bank.buf[:, 0:n]), [t])
        bank.free, self.slab_free = [c], [t]
        return at + n

    def rows(self, name, *index):
        a = self.ins[name]
        for i in index:
            a = a[i]
        if len(a.shape) == 2:
            a = a.rearrange("a b -> (a b)")
        return a.rearrange("(r c) -> r c", c=P)

    def setup(self):
        self.cst_ready = self.sp.load(self.cst[:, :], self.ins["constants"])
        self.x_ready = [self.sp.load(self.x[:, t, :], self.ins["x"][0, t * P:(t + 1) * P, :]) for t in range(XT)]
        base, self.at = self.at, self.high_end
        self.row_slab = self.place("row_slab", [P, P])
        self.at = base
        self.slab_free = []
        D = self.rows
        self.c = {"norm_mix": 0, "norm_mlp": 16}
        self.load_rows_as_columns([D("norm_mix_w", slice(0, DEPTH)), D("norm_mlp_w", slice(0, DEPTH))], 0)

    def setup_rest(self):
        base, self.at = self.at, self.high_end + P * 4
        self.mod_gain = [self.place(f"mod_gain{i}", [P, 2, 8]) for i in range(DEPTH)]
        self.mod_shift = [self.place(f"mod_shift{i}", [P, 2, 8]) for i in range(DEPTH)]
        self.cond = self.place("silu_cond", [P, KT, 2])
        self.mod_cols = self.place("mod_cols", [P, 2, 16])
        work = self.place("rope_work", [P, 6, XT, 8])
        pos_i = self.place("positions", [P, XT], I32)
        pos_f = self.place("positions_f", [P, XT])
        self.at = base
        pl = self.small.load(pos_i[:, :], self.ins["positions"][0].rearrange("(t p) -> p t", p=P), strided=True)
        D, c, at = self.rows, self.c, 32
        c["gla_b"], c["b_mqk"], c["conv_w"], c["conv_b"] = at, at + 8, at + 24, at + 88
        at = self.load_rows_as_columns(
            [D("gla_b_gf_2", 0), D("gla_b_gb_2", 0), D("b_in", 0, slice(COL_MQ, COL_MV)), D("b_in", 1, slice(COL_MQ, COL_MV)),
             self.ins["conv_w"].rearrange("l j (r c) -> (l j r) c", c=P), D("conv_b", slice(0, DEPTH))], at)
        c["b_gate"], c["norm_g"], c["q_norm"], c["kv_norm"], c["cond"], c["ada_b"] = at, at + 32, at + 48, at + 51, at + 53, at + 69
        at = self.load_rows_as_columns(
            [D("b_in", 0, slice(COL_GA, D_IN)), D("b_in", 1, slice(COL_GA, D_IN)), D("norm_g_2", slice(0, DEPTH)),
             D("mla_q_norm_2", 0), D("mla_kv_norm_2", 0), D("c_2", 0), D("c_ctx_2"), D("ada_b_2", slice(0, DEPTH))], at)
        assert at == c["ada_b"] + 48 and at <= 256
        f = self.dve.step(lambda e: e.tensor_copy(pos_f[:, :], pos_i[:, :]), [pl])
        ang, turn, k, r = (work[:, i, :, :] for i in range(4))
        inv = self.cst[:, C_INV:C_INV + 8]
        for t in range(XT):
            self.dve.step(lambda e, t=t: e.tensor_scalar(ang[:, t, :], inv, pos_f[:, t:t + 1], None, ALU.mult), [f, self.cst_ready])
        magic = 1.5 * 2.0 ** 23
        c1, c2 = 6.28125, float(np.float32(np.round((2 * np.pi - 6.28125) * 2 ** 22) / 2 ** 22))
        c3 = float(2 * np.pi - c1 - c2)
        for i, quarter in enumerate((0.25, 0.0)):
            self.dve.step(lambda e, quarter=quarter: e.tensor_scalar(turn, ang, 1 / (2 * np.pi), quarter, ALU.mult, ALU.add))
            self.dve.step(lambda e: e.tensor_scalar(k, turn, magic, None, ALU.add))
            self.dve.step(lambda e: e.tensor_scalar(k, k, -magic, None, ALU.add))
            self.dve.step(lambda e: e.scalar_tensor_tensor(r, k, -c1, ang, ALU.mult, ALU.add))
            self.dve.step(lambda e: e.scalar_tensor_tensor(r, k, -c2, r, ALU.mult, ALU.add))
            self.dve.step(lambda e: e.scalar_tensor_tensor(r, k, -c3, r, ALU.mult, ALU.add))
            self.dve.step(lambda e, quarter=quarter: e.tensor_scalar(r, r, quarter * 2 * np.pi, float(np.float32(3.1415925)), ALU.add, ALU.min))
            d = self.dve.step(lambda e: e.tensor_scalar(r, r, float(-np.float32(3.1415925)), None, ALU.max))
            s = self.act.step(lambda e, i=i: e.activation(work[:, 4 + i, :, :], r, ACT.Sin), [d])
            self.dve.pending = [s]
        cos, sin = work[:, 4, :, :], work[:, 5, :, :]
        for o in (0, 8):
            self.dve.step(lambda e, o=o: e.tensor_copy(self.rope[:, :, o:o + 8], cos), [s])
        self.dve.step(lambda e: e.tensor_scalar(self.rope[:, :, 16:24], sin, -1.0, None, ALU.mult))
        self.dve.step(lambda e: e.tensor_copy(self.rope[:, :, 24:32], sin))

    def layer(self, l):
        c, cols, cst, ins = self.c, self.cols, self.cst, self.ins
        pe, dve, act, pool = self.pe, self.dve, self.act, self.pool
        fence = self.fence()
        base = self.at = self.hc_at
        mqk = self.place("mlstm_qk", [P, 8, SEQ])
        mv = self.place("mlstm_v", [P, XT, MH, MHD + 1])
        mo = self.place("mlstm_out_gate", [P, XT, 512])
        qk_end = self.at
        y_att = Split(self.place("y_att_hi", [P, 4, SEQ], F32R), self.place("y_att_lo", [P, 4, SEQ], F32R))
        gates = self.place("gates", [P, 8, 16])
        mrow = self.place("running_max_row", [MH, SEQ])
        zrow = self.place("zero_row", [MH, SEQ])
        self.rope_tmp = self.place("rope_swapped", [P, P])
        att_at = self.at
        qT = self.place("att_qT", [P, 4, SEQ])
        kT = self.place("att_kT", [P, 4, SEQ])
        av = self.place("att_v", [P, XT, 512])
        conv_in = Ring([self.place(f"conv_in{i}", [P, CONV - 1 + SEQ]) for i in range(2)])
        conv_acc = self.place("conv_acc", [P, SEQ])
        tok = Ring([self.place(f"token_tile{i}", [P, 512]) for i in range(2)])
        bias_row = Ring([self.place(f"bias_row{i}", [P, 512]) for i in range(1)])
        tmp_at = self.at
        prob = Ring([self.place(f"prob{i}", [P, 512]) for i in range(2)])
        probT = Ring([self.place(f"probT{i}", [P, 512]) for i in range(2)])
        y_tok = Ring([self.place(f"y_tok{i}", [P, 512]) for i in range(1)])
        self.junk = self.nc.alloc_sbuf_tensor_at(f"junk_l{l}", [P, DM], F32, offset=(tmp_at + 31) // 32 * 32)
        self.diag = self.nc.alloc_sbuf_tensor_at(f"diag_l{l}", [P, 4, P], F32, offset=(tmp_at + 31) // 32 * 32 + 4096)
        self.junk2 = self.nc.alloc_sbuf_tensor_at(f"junk2_l{l}", [P, DM], F32, offset=base)
        tiny = self.tiny

        h_ready = self.norm_features([self.x[:, t, :] for t in range(XT)], DM, [(self.hx, t * P) for t in range(XT)],
                                     self.cols[:, c["norm_mix"] + 8 * l:c["norm_mix"] + 8 * l + 8], self.x_ready)
        if l == 0:
            self.setup_rest()
        marks_of_phase = self.fence()
        for s in conv_in.slots:
            s.free = [pool.step(lambda e, s=s: e.memset(s.buf[:, 0:CONV - 1], 0.0))]
        ones = [pool.step(lambda e: e.memset(mv[:, :, :, MHD:MHD + 1], 1.0)), pool.step(lambda e: e.memset(zrow[:, :], 0.0))]
        X = [(self.hx, t) for t in range(XT)]
        main, side = self.banks[0:4], self.banks[4:8]

        def bias_load(lo, n):
            b = bias_row.take()
            t = self.small.load(b.buf[:, 0:n], ins["b_in"][l, lo:lo + n].partition_broadcast(P), after=b.free + marks_of_phase)
            return b, t

        def u(name):
            return [(f"{name}.{l}.{i}", 4 * i, 4) for i in range(2)]

        done = {}
        for name, lo, dst in (("aq", COL_AQ, qT), ("ak", COL_AK, kT)):
            b, bt = bias_load(lo, 512)

            def evac(t, bank, made, dst=dst, b=b, bt=bt, name=name):
                z = tok.take()
                first = dve.step(lambda e: e.tensor_tensor(z.buf[:, :], bank, b.buf[:, :], ALU.add), [made, bt] + z.free)
                zh = z.buf[:, :].rearrange("p (h d) -> p h d", h=AH)
                swap = self.rope_tmp[:, 0:128].rearrange("p (h d) -> p h d", h=AH)
                table = self.rope[:, t, :]
                cc = table[:, 0:16].unsqueeze(1).broadcast_to([P, AH, 16])
                dve.step(lambda e: e.tensor_tensor(swap[:, :, 0:8], zh[:, :, 8:16], table[:, 16:24].unsqueeze(1).broadcast_to([P, AH, 8]), ALU.mult))
                dve.step(lambda e: e.tensor_tensor(swap[:, :, 8:16], zh[:, :, 0:8], table[:, 24:32].unsqueeze(1).broadcast_to([P, AH, 8]), ALU.mult))
                dve.step(lambda e: e.tensor_tensor(zh[:, :, 0:16], zh[:, :, 0:16], cc, ALU.mult))
                r = dve.step(lambda e: e.tensor_tensor(zh[:, :, 0:16], zh[:, :, 0:16], swap, ALU.add))
                sb = side[t]

                def turned():
                    def tr(e):
                        for g in range(4):
                            e.transpose(sb.buf[:, g * P:(g + 1) * P], z.buf[:, g * P:(g + 1) * P], self.ident)
                    tt = pe.step(tr, [r] + sb.free)
                    o = act.step(lambda e: e.activation(dst[:, :, t * P:(t + 1) * P], sb.buf[:, :].rearrange("p (g t) -> p g t", g=4), ACT.Copy), [tt])
                    sb.free, z.free = [o], [tt]
                    done[name, t] = o
                self.defer(turned)
                b.free = [first]
                return [first]
            for _ in self.to_tokens(u(name), X, 512, main, evac, h_ready):
                pass
        b, bt = bias_load(COL_AV, 512)

        def evac_v(t, bank, made):
            a = dve.step(lambda e: e.tensor_tensor(av[:, t, :], bank, b.buf[:, :], ALU.add), [made, bt])
            b.free = [a]
            done["av", t] = a
            return [a]
        for _ in self.to_tokens(u("av"), X, 512, main, evac_v, h_ready):
            pass

        def mlstm_inputs():
            for g in range(2):
                for _ in self.to_features(u(f"mqk{g}"), self.hx, SEQ, main, lambda m, bank, made, g=g: conv(g * 4 + m, bank, made)):
                    yield
            b, bt = bias_load(COL_MV, 512)

            def evac_mv(t, bank, made):
                a = dve.step(lambda e: e.tensor_tensor(mv[:, t, :, 0:MHD], bank.rearrange("p (h d) -> p h d", h=MH),
                                                       b.buf[:, :].rearrange("p (h d) -> p h d", h=MH), ALU.add), [made, bt] + ones)
                b.free = [a]
                done["mv", t] = a
                return [a]
            for _ in self.to_tokens(u("mv"), X, 512, main, evac_mv):
                yield
            b2, bt2 = bias_load(COL_MO, 512)

            def evac_mo(t, bank, made):
                a = dve.step(lambda e: e.tensor_tensor(mo[:, t, :], bank, b2.buf[:, :], ALU.add), [made, bt2])
                b2.free = [a]
                done["mo", t] = a
                return [a]
            for _ in self.to_tokens(u("mo"), X, 512, main, evac_mo):
                yield
            b3, bt3 = bias_load(COL_MI, 8)

            def evac_if(t, bank, made):
                a = dve.step(lambda e: e.tensor_tensor(gates[:, 0:2, 4 * t:4 * t + 4], bank.rearrange("p (g h) -> p g h", g=2),
                                                       b3.buf[:, 0:8].rearrange("p (g h) -> p g h", g=2), ALU.add), [made, bt3])
                b3.free = [a]
                done["if", t] = a
                return [a]
            for _ in self.to_tokens([(f"mif.{l}", 0, 8)], X, 8, main, evac_if):
                yield

        def conv(m, bank, made):
            s = conv_in.take()
            bcol = cols[:, c["b_mqk"] + 8 * l + m:c["b_mqk"] + 8 * l + m + 1]
            a = act.step(lambda e: e.activation(s.buf[:, CONV - 1:], bank, ACT.Identity, bias=bcol), [made] + s.free)
            w = lambda j: cols[:, c["conv_w"] + (l * CONV + j) * 8 + m:c["conv_w"] + (l * CONV + j) * 8 + m + 1]
            cb = cols[:, c["conv_b"] + 8 * l + m:c["conv_b"] + 8 * l + m + 1]
            d = dve.step(lambda e: e.tensor_scalar(conv_acc[:, :], s.buf[:, 0:SEQ], w(0), cb, ALU.mult, ALU.add), [a] + self.acc_free)
            for j in range(1, CONV):
                d = dve.step(lambda e, j=j: e.scalar_tensor_tensor(conv_acc[:, :], s.buf[:, j:j + SEQ], w(j), conv_acc[:, :], ALU.mult, ALU.add))
            s.free = [d]
            sg = act.step(lambda e: e.activation(mqk[:, m, :], conv_acc[:, :], ACT.Silu), [d])
            self.acc_free = [sg]
            done["mqk", m] = sg
            return [a]
        self.acc_free = []

        def attention():
            s_banks, t_bank, o_bank = Ring(side[0:2]), side[2], side[3]
            s_banks.slots = side[0:2]
            units = [(i, h) for i in range(XT) for h in range(AH)]
            state = {}

            def scores(i, h):
                n = (i + 1) * P
                bank = s_banks.take()
                hp = (h % 2) * AHD
                t = pe.step(lambda e: e.matmul(bank.buf[:, 0:n], qT[hp:hp + AHD, h // 2, i * P:(i + 1) * P], kT[hp:hp + AHD, h // 2, 0:n],
                                               start=True, stop=True), [done["aq", i], done["ak", i]] + bank.free)
                p = prob.take()
                mn, ls = tiny[:, 64 + h:65 + h], tiny[:, 72 + h:73 + h]
                d = dve.step(lambda e: e.tensor_tensor_reduce(out=p.buf[:, 0:n], in0=bank.buf[:, 0:n], in1=cst[:, C_ATT + 512 - n:C_ATT + 512],
                                                              scale=-AHD ** -0.5, scalar=3e38, op0=ALU.add, op1=ALU.min, accum_out=mn), [t] + p.free)
                bank.free = [d]
                a = act.step(lambda e: e.activation(p.buf[:, 0:n], p.buf[:, 0:n], ACT.Exp, bias=mn, scale=-1.0, accum_out=ls), [d])
                state[i, h] = (p, n, ls, a)

            def turn(i, h):
                p, n, ls, a = state[i, h]

                def tr(e):
                    for j in range(i + 1):
                        last = e.transpose(t_bank.buf[:, j * P:(j + 1) * P], p.buf[:, j * P:(j + 1) * P], self.ident)
                    return last
                t = pe.step(tr, [a] + t_bank.free)
                p.free = [t]
                q = probT.take()
                if h % 2:
                    cp = dve.step(lambda e: e.tensor_copy(q.buf[:, 0:n], t_bank.buf[:, 0:n]), [t] + q.free)
                else:
                    cp = act.step(lambda e: e.activation(q.buf[:, 0:n], t_bank.buf[:, 0:n], ACT.Copy), [t] + q.free)
                t_bank.free = [cp]
                state[i, h] = (q, ls, cp, a)

            def values(i, h):
                q, ls, cp, a = state[i, h]

                def pv(e):
                    for j in range(i + 1):
                        last = e.matmul(o_bank.buf[:, 0:AHD], q.buf[:, j * P:(j + 1) * P], av[:, j, h * AHD:(h + 1) * AHD],
                                        start=(j == 0), stop=(j == i))
                    return last
                t = pe.step(pv, [cp, done["av", i]] + o_bank.free)
                q.free = [t]
                if h == 0:
                    state["y", i] = y_tok.take()
                y = state["y", i]
                dve.step(lambda e: e.reciprocal(ls, ls), [a])
                d = dve.step(lambda e: e.tensor_scalar(y.buf[:, h * AHD:(h + 1) * AHD], o_bank.buf[:, 0:AHD], ls, None, ALU.mult), [t] + y.free)
                o_bank.free = [d]
                if h == AH - 1:
                    def tr(e):
                        for g in range(4):
                            last = e.transpose(t_bank.buf[:, g * P:(g + 1) * P], y.buf[:, g * P:(g + 1) * P], self.ident)
                        return last
                    tt = pe.step(tr, [d] + t_bank.free)
                    y.free = [tt]
                    t_bank.free = self.put_split(y_att, (slice(None), slice(0, 4), slice(i * P, (i + 1) * P)),
                                                 t_bank.buf[:, :].rearrange("p (g t) -> p g t", g=4), [tt])
                    done["y", i] = t_bank.free
            for s in range(len(units) + 2):
                if s < len(units):
                    scores(*units[s])
                    yield
                if 1 <= s <= len(units):
                    turn(*units[s - 1])
                    yield
                if s >= 2:
                    values(*units[s - 2])
                    yield

        def filler():
            yield from mlstm_inputs()
            yield from self.modulation(l, tok)
        interleave((attention(), 2), (filler(), 1))

        self.fence()
        self.at = att_at
        mix_a = self.place("mixed_att", [P, 8, SEQ])
        y_m = Split(self.place("y_mlstm_hi", [P, 4, SEQ], F32R), self.place("y_mlstm_lo", [P, 4, SEQ], F32R))
        E = Ring([self.place(f"decay{i}", [P, 512]) for i in range(2)])
        Pm = Ring([self.place("mlstm_prob", [P, 1280])])
        p_at = (0, 512, 896, 1152)
        nrow = self.place("mlstm_norm_row", [P, 512])
        bl = self.small.load(nrow[:, 0:512], ins["mlstm_norm_w"][l, :].partition_broadcast(P), after=self.fence())
        def mlstm():
            G = lambda j: gates[:, j, :]
            gr = [done["if", t] for t in range(XT)]
            act.step(lambda e: e.activation(G(2), G(1), ACT.Abs), gr)
            act.step(lambda e: e.activation(G(2), G(2), ACT.Exp, scale=-1.0))
            a = act.step(lambda e: e.activation(G(2), G(2), ACT.Ln, bias=1.0))
            d = dve.step(lambda e: e.scalar_tensor_tensor(G(3), G(1), 0.0, G(2), ALU.min, ALU.subtract), [a])
            dve.step(lambda e: e.memset(gates[:, 4, 0:4], 0.0))
            for t in range(1, XT):
                d = dve.step(lambda e, t=t: e.tensor_tensor(gates[:, 4, 4 * t:4 * t + 4], gates[:, 4, 4 * t - 4:4 * t], gates[:, 3, 4 * t - 4:4 * t], ALU.add))
            bk = side[2]

            def cum(e):
                e.matmul(bk.buf[:, 0:16], cst[:, C_UP:C_UP + P], G(3), start=True, stop=False)
                return e.matmul(bk.buf[:, 0:16], cst[:, C_ONES:C_ONES + P], G(4), start=False, stop=True)
            t = pe.step(cum, [d] + bk.free)
            yield
            dve.step(lambda e: e.tensor_copy(G(5), bk.buf[:, 0:16]), [t])
            d = dve.step(lambda e: e.tensor_tensor(G(6), G(0), G(5), ALU.subtract))
            bk.free = [d]
            bk2 = side[3]

            def rows_(e):
                for t in range(XT):
                    last = e.transpose(bk2.buf[0:MH, t * P:(t + 1) * P], gates[:, 6, 4 * t:4 * t + 4], self.ident)
                return last
            t = pe.step(rows_, [d] + bk2.free)
            yield
            m_row = dve.step(lambda e: e.tensor_tensor_scan(mrow[:, :], bk2.buf[0:MH, :], zrow[:, :], 0.0, ALU.max, ALU.max), [t])
            bk2.free = [m_row]

            def back(e):
                for t in range(XT):
                    last = e.transpose(bk.buf[:, 4 * t:4 * t + 4], mrow[:, t * P:(t + 1) * P], self.ident[0:MH, 0:MH])
                return last
            t = pe.step(back, [m_row] + bk.free)
            yield
            d = dve.step(lambda e: e.tensor_tensor(G(7), bk.buf[:, 0:16], G(5), ALU.add), [t])
            bk.free = [d]
            floor_ready = act.step(lambda e: e.activation(G(7), G(7), ACT.Exp, scale=-1.0), [d])
            m_bank, s_bank, o_banks = side[0], side[1], side[2:4]
            for h in range(MH):
                t = pe.step(lambda e, h=h: e.matmul(m_bank.buf[:, :], self.negsel[:, h, :], mrow[:, :], start=True, stop=True), [m_row] + m_bank.free)
                pm = Pm.take()
                last = None
                yield
                for j in range(XT):
                    n = (XT - j) * P
                    w = E.take()
                    d = dve.step(lambda e, j=j, n=n, w=w, h=h: e.tensor_scalar(w.buf[:, 0:n], m_bank.buf[:, j * P:], gates[:, 6, 4 * j + h:4 * j + h + 1], None, ALU.add), [t] + w.free)
                    d = dve.step(lambda e, w=w: e.tensor_tensor(w.buf[:, 0:P], w.buf[:, 0:P], cst[:, C_TRI:C_TRI + P], ALU.add))
                    a = act.step(lambda e, n=n, w=w: e.activation(w.buf[:, 0:n], w.buf[:, 0:n], ACT.Exp), [d])
                    s = pe.step(lambda e, j=j, n=n, h=h: e.matmul(s_bank.buf[:, 0:n], mqk[:, 4 + h, j * P:(j + 1) * P], mqk[:, h, j * P:], start=True, stop=True),
                                [done["mqk", h], done["mqk", 4 + h]] + s_bank.free)
                    last = dve.step(lambda e, j=j, n=n, w=w, pm=pm: e.scalar_tensor_tensor(pm.buf[:, p_at[j]:p_at[j] + n], s_bank.buf[:, 0:n], MHD ** -0.5, w.buf[:, 0:n], ALU.mult, ALU.mult),
                                    [s, a] + pm.free)
                    s_bank.free, w.free = [last], [last]
                    if j == XT - 1:
                        m_bank.free = [d]
                    yield
                for half in range(2):
                    ob = o_banks[half]

                    def pv(e):
                        for ii in range(2):
                            i = 2 * half + ii
                            for j in range(i + 1):
                                e.matmul(ob.buf[:, ii * 129:ii * 129 + 129], pm.buf[:, p_at[j] + (i - j) * P:p_at[j] + (i - j + 1) * P],
                                         mv[:, j, h, :], start=(j == 0), stop=(j == i))
                    t2 = pe.step(pv, [last] + [done["mv", j] for j in range(XT)] + ob.free)
                pm.free = [t2]
                yield
                for half in range(2):
                    ob = o_banks[half]
                    o2 = ob.buf[:, 0:258].rearrange("p (i d) -> p i d", i=2)
                    den = tiny[:, 96:98]
                    fl = gates[:, 7, :].rearrange("p (t h) -> p t h", h=MH)[:, 2 * half:2 * half + 2, h]
                    dve.step(lambda e: e.tensor_scalar(den, o2[:, :, MHD], -1.0, None, ALU.mult), [t2])
                    dve.step(lambda e: e.tensor_tensor(den, o2[:, :, MHD], den, ALU.max))
                    dve.step(lambda e: e.tensor_tensor(den, den, fl, ALU.max), [floor_ready])
                    dve.step(lambda e: e.reciprocal(den, den))
                    for ii in range(2):
                        d = dve.step(lambda e: e.tensor_scalar(mv[:, 2 * half + ii, h, 0:MHD], o2[:, ii, 0:MHD], den[:, ii:ii + 1], None, ALU.mult))
                    ob.free = [d]
                    yield
            done["hm"] = d

            rs = self.tiny[:, 100:116]
            for t in range(XT):
                w = E.take()
                d = dve.step(lambda e, t=t, w=w: e.tensor_tensor(w.buf[:, :].rearrange("p (h d) -> p h d", h=MH), mv[:, t, :, 0:MHD], mv[:, t, :, 0:MHD], ALU.mult), [done["hm"]] + w.free)
                d = dve.step(lambda e, t=t, w=w: e.tensor_reduce(rs[:, 4 * t:4 * t + 4], w.buf[:, :].rearrange("p (h d) -> p h d", h=MH), AX_X, ALU.add))
                w.free = [d]
            d = dve.step(lambda e: e.tensor_scalar(rs, rs, 1.0 / MHD, EPS, ALU.mult, ALU.add))
            a = act.step(lambda e: e.activation(rs, rs, ACT.Sqrt), [d])
            dve.step(lambda e: e.reciprocal(rs, rs), [a])
            sg = act.step(lambda e: e.activation(mo[:, :, :], mo[:, :, :], ACT.Sigmoid), [done["mo", t] for t in range(XT)])
            for t in range(XT):
                dve.step(lambda e, t=t: e.tensor_tensor(mo[:, t, :], mo[:, t, :], nrow[:, 0:512], ALU.mult), [sg, bl])
                for h in range(MH):
                    sl = slice(h * MHD, (h + 1) * MHD)
                    d = dve.step(lambda e, t=t, h=h, sl=sl: e.scalar_tensor_tensor(mv[:, t, h, 0:MHD], mv[:, t, h, 0:MHD], rs[:, 4 * t + h:4 * t + h + 1], mo[:, t, sl], ALU.mult, ALU.mult))
                sb = side[t]

                def tr(e, t=t, sb=sb):
                    for g in range(4):
                        last = e.transpose(sb.buf[:, g * P:(g + 1) * P], mv[:, t, g, 0:MHD], self.ident)
                    return last
                yield
                tt = pe.step(tr, [d] + sb.free)
                sb.free = self.put_split(y_m, (slice(None), slice(0, 4), slice(t * P, (t + 1) * P)),
                                         sb.buf[:, :].rearrange("p (g t) -> p g t", g=4), [tt])
                y_ready = sb.free
            done["y_m"] = y_ready

        def att_projection():
            for g in range(2):
                ga = {}

                def evac_g(m, bank, made, g=g):
                    bcol = cols[:, c["b_gate"] + 16 * l + 4 * g + m:c["b_gate"] + 16 * l + 4 * g + m + 1]
                    a = dve.step(lambda e: e.tensor_scalar(mix_a[:, 4 * g + m, :], bank, bcol, None, ALU.add), [made])
                    return [a]
                for _ in self.to_features(u(f"ga{g}"), self.hx, SEQ, main, evac_g):
                    yield
                a = act.step(lambda e, g=g: e.activation(mix_a[:, 4 * g:4 * g + 4, :], mix_a[:, 4 * g:4 * g + 4, :], ACT.Sigmoid), [dve.now()])

                def evac_p(m, bank, made, g=g, a=a):
                    return [dve.step(lambda e: e.tensor_tensor(mix_a[:, 4 * g + m, :], bank, mix_a[:, 4 * g + m, :], ALU.mult), [made, a])]
                for _ in self.to_features([(f"pa{g}.{l}", 0, 4)], y_att, SEQ, main, evac_p, done["y", 3]):
                    yield
            read = [pe.now()]
            for g in range(2):
                def evac_b(m, bank, made):
                    bcol = cols[:, c["b_gate"] + 16 * l + 8 + 4 * g + m:c["b_gate"] + 16 * l + 8 + 4 * g + m + 1]
                    return [dve.step(lambda e: e.tensor_scalar(gbt[:, 4 * g + m, :], bank, bcol, None, ALU.add), [made] + read)]
                for _ in self.to_features(u(f"gb{g}"), self.hx, SEQ, main, evac_b):
                    yield
        here, self.at = self.at, qk_end
        gbt = self.place("gate_b", [P, 8, SEQ])
        self.at = here
        interleave((mlstm(), 1), (att_projection(), 1))

        self.fence()
        self.at = base
        mixed = Split(self.place("mixed_hi", [P, 8, SEQ], F32R), self.place("mixed_lo", [P, 8, SEQ], F32R))
        assert self.at <= qk_end
        sgb = act.step(lambda e: e.activation(gbt[:, :, :], gbt[:, :, :], ACT.Sigmoid))
        for g in range(2):
            def evac_p(m, bank, made):
                k = 4 * g + m
                d0 = dve.step(lambda e: e.tensor_tensor(gbt[:, k, :], bank, gbt[:, k, :], ALU.mult), [made, sgb])
                d = dve.step(lambda e: e.tensor_tensor(gbt[:, k, :], gbt[:, k, :], mix_a[:, k, :], ALU.add))
                a = act.step(lambda e: e.activation(mixed.hi[:, k, :], gbt[:, k, :], ACT.Copy), [d])
                dve.step(lambda e: e.tensor_tensor(mixed.lo[:, k, :], gbt[:, k, :], mixed.hi[:, k, :].bitcast(F32), ALU.subtract), [a])
                return [d0]
            for _ in self.to_features([(f"pm{g}.{l}", 0, 4)], y_m, SEQ, self.banks[4 * g:4 * g + 4], evac_p):
                pass
        ready = [act.now(), dve.now()]
        for g in range(2):
            def evac_o(t, bank, made, g=g):
                sl = slice(g * 512, (g + 1) * 512)
                return [dve.step(lambda e: e.tensor_tensor(self.x[:, t, sl], bank, self.x[:, t, sl], ALU.add), [made])]
            for _ in self.to_tokens([(f"wo{g}.{l}.{i}", 4 * i, 4) for i in range(2)], [(mixed, t) for t in range(XT)], 512,
                                    self.banks[4 * g:4 * g + 4], evac_o, ready):
                pass

        self.fence()
        self.at = base
        up = [Split(self.place(f"hidden_hi{i}", [P, 8, SEQ], F32R), self.place(f"hidden_lo{i}", [P, 8, SEQ], F32R)) for i in range(2)]
        relu = Ring([self.place(f"relu{i}", [P, SEQ]) for i in range(2)])
        sq = Ring([self.place(f"relu_sq{i}", [P, SEQ]) for i in range(2)])
        self.junk = self.place("mlp_junk", [P, DM])
        self.junk2 = self.place("mlp_junk2", [P, DM])
        self.diag = self.place("mlp_diag", [P, 4, P])
        self.norm_features([self.x[:, t, :] for t in range(XT)], DM, [(self.hx, t * P) for t in range(XT)],
                           self.cols[:, c["norm_mlp"] + 8 * l:c["norm_mlp"] + 8 * l + 8], [dve.now()])
        h_ready = [act.now(), dve.now()]
        up_free, up_ready = [[], []], [None, None]

        def widen(q):
            U, free = up[q % 2], up_free[q % 2]
            for g in range(2):
                def evac_u(m, bank, made):
                    k = 4 * g + m
                    r, s = relu.take(), sq.take()
                    a = act.step(lambda e: e.activation(r.buf[:, :], bank, ACT.Relu), [made] + r.free)
                    b = act.step(lambda e: e.activation(U.hi[:, k, :], r.buf[:, :], ACT.Square), free)
                    dve.step(lambda e: e.tensor_tensor(s.buf[:, :], r.buf[:, :], r.buf[:, :], ALU.mult), [a] + s.free)
                    d = dve.step(lambda e: e.tensor_tensor(U.lo[:, k, :], s.buf[:, :], U.hi[:, k, :].bitcast(F32), ALU.subtract), [b] + free)
                    r.free, s.free = [b, d], [d]
                    return [a]
                for _ in self.to_features([(f"f1.{l}.{q}.{g}.{i}", 4 * i, 4) for i in range(2)], self.hx, SEQ, self.banks[0:4], evac_u, h_ready):
                    pass
            up_ready[q % 2] = [act.now(), dve.now()]

        def narrow(q):
            for g in range(2):
                def evac_d(t, bank, made):
                    sl = slice(g * 512, (g + 1) * 512)
                    return [dve.step(lambda e: e.tensor_tensor(self.x[:, t, sl], bank, self.x[:, t, sl], ALU.add), [made])]
                for _ in self.to_tokens([(f"f2.{l}.{q}.{g}.{i}", 4 * i, 4) for i in range(2)], [(up[q % 2], t) for t in range(XT)], 512,
                                        self.banks[4:8], evac_d, up_ready[q % 2]):
                    pass
            up_free[q % 2] = [pe.now()]
        for q in range(5):
            if q < 4:
                widen(q)
            if q > 0:
                narrow(q - 1)
        self.x_ready = [dve.now()]

    def layer_plan(self, l):
        w = {n: self.ins[n][l] for n in ("w_in", "w_proj_att", "w_proj_mlstm", "w_out", "w_ff1", "w_ff2")}

        units = self.units
        plan = []
        for n, c0 in (("aq", COL_AQ), ("ak", COL_AK), ("av", COL_AV), ("mqk0", COL_MQ), ("mqk1", COL_MQ + 512), ("mv", COL_MV), ("mo", COL_MO)):
            plan += units(f"{n}.{l}", w["w_in"], c0)
        plan += units(f"mif.{l}", w["w_in"], COL_MI, 8, per=8)
        for g in range(6):
            plan += units(f"ada{l}.{g}", self.ins["ada_w_2"][l], 512 * g, raw=True)
        for g in range(2):
            plan += units(f"ga{g}.{l}", w["w_in"], COL_GA + 512 * g)
            plan += units(f"pa{g}.{l}", w["w_proj_att"], 512 * g, kn=4)
        for g in range(2):
            plan += units(f"gb{g}.{l}", w["w_in"], COL_GB + 512 * g)
        for g in range(2):
            plan += units(f"pm{g}.{l}", w["w_proj_mlstm"], 512 * g, kn=4)
        for g in range(2):
            plan += units(f"wo{g}.{l}", w["w_out"], 512 * g)
        for q in range(5):
            for g in range(2 * (q < 4)):
                plan += units(f"f1.{l}.{q}.{g}", w["w_ff1"], q * 1024 + g * 512)
            for g in range(2 * (q > 0)):
                plan += units(f"f2.{l}.{q - 1}.{g}", w["w_ff2"], g * 512, k0=(q - 1) * 8)
        return plan

    def final_norm(self, name, dst_dram=None):
        marks = self.fence()
        row = self.place("final_gain_row", [P, DM])
        self.junk, self.junk2 = self.place("final_junk", [P, DM]), self.place("final_junk2", [P, DM])
        rl = self.small.load(row[:, :], self.ins[name].partition_broadcast(P), after=marks)
        r = self.tiny[:, 0:XT]
        ready = self.rstd([self.x[:, t, :] for t in range(XT)], DM, r, self.x_ready)
        for t in range(XT):
            self.x_ready = [self.dve.step(lambda e: e.scalar_tensor_tensor(self.x[:, t, :], self.x[:, t, :], r[:, t:t + 1], row[:, :], ALU.mult, ALU.mult), [ready, rl])]

    def modulation(self, i, rows):
        pe, dve, act, cols, c = self.pe, self.dve, self.act, self.cols, self.c
        cond, mod, gain, shift = self.cond, self.mod_cols, self.mod_gain[i], self.mod_shift[i]
        bank = self.banks[0]
        s = act.step(lambda e: e.activation(cond[:, :, :], cols[:, c["cond"]:c["cond"] + 16].rearrange("p (c k) -> p k c", c=2), ACT.Silu))
        for g in range(6):
            bank, b2 = self.banks[g % 2], self.banks[2 + g % 2]
            r, b = rows.take(), rows.take()
            rb, bb = r.buf[0:2, :], b.buf[0:2, :]
            bt = self.small.load(bb, self.ins["ada_b_2"][i, 512 * g:512 * g + 512].partition_broadcast(2), after=b.free)
            for u in range(2):
                w, slot, rdy = self.take(f"ada{i}.{g}.{u}")

                def issue(e):
                    for k in range(4):
                        e.matmul(bank.buf[0:2, :], cond[:, 4 * u + k, :], w[:, k, :], start=(u == 0 and k == 0), stop=(u == 1 and k == 3))
                t = pe.step(issue, rdy + [s] + (bank.free if u == 0 else []))
                self.raw_done(slot, t)
                yield
            d = dve.step(lambda e: e.tensor_tensor(rb, bank.buf[0:2, :], bb, ALU.add), [t, bt] + r.free)
            bank.free, b.free = [d], [d]
            if g < 4:
                yield

                def tr(e):
                    for m in range(4):
                        e.transpose(b2.buf[:, 2 * m:2 * m + 2], rb[:, m * P:(m + 1) * P], self.ident[0:2, 0:2])
                t = pe.step(tr, [d] + b2.free)
                d = dve.step(lambda e: e.tensor_copy(mod[:, :, 4 * g:4 * g + 4], b2.buf[:, 0:8].rearrange("p (m c) -> p c m", m=4)), [t])
                b2.free, r.free = [d], [t]
            else:
                r.free = [self.small.load(self.gate_rows[i][:, (g - 4) * 512:(g - 3) * 512], rb, after=[d])]
                self.gate_stored += r.free
        ng = cols[:, c["norm_g"] + 8 * i:c["norm_g"] + 8 * i + 8]
        dve.step(lambda e: e.tensor_copy(shift[:, :, :], mod[:, :, 0:8]))
        dve.step(lambda e: e.tensor_scalar(gain[:, :, :], mod[:, :, 8:16], 1.0, None, ALU.add))
        dve.step(lambda e: e.tensor_tensor(gain[:, :, :], gain[:, :, :], ng.unsqueeze(1).broadcast_to([P, 2, 8]), ALU.mult))

    def modulated_norm(self, i, ready):
        self.junk, self.junk2 = self.place("norm_junk", [P, DM]), self.place("norm_junk2", [P, DM])
        self.diag = self.place("norm_diag", [P, XT + CT, P])
        self.nrm_tmp = Ring([self.place(f"norm_tmp{j}", [P, 512]) for j in range(4)])
        return self.norm_features(
            [self.x[:, t, :] for t in range(XT)] + [self.ctx_res[:, t, :] for t in range(CT)], DM,
            [(self.hx, t * P) for t in range(XT)] + [(self.hc, t * P) for t in range(CT)],
            self.mod_gain[i], ready + self.x_ready, self.mod_shift[i])

    def mla(self):
        pe, dve, act, c, cols, cst = self.pe, self.dve, self.act, self.c, self.cols, self.cst
        T = XT + CT
        marks = self.fence()
        self.at = self.hc_at
        self.hc = Split(self.place("hc_hi", [P, KT, CTX], F32R), self.place("hc_lo", [P, KT, CTX], F32R))
        self.after_hc = self.at
        self.ctx_res = self.place("context_residual", [P, CT, DM])
        after_ctx = self.at
        cl = self.small.load(self.ctx_res[:, :, :], self.ins["ctx_2"][0].rearrange("(t p) d -> p t d", p=P), after=marks)
        gate_bc = [self.place("mod_gate_x", [P, DM]), self.place("mod_gate_ctx", [P, DM])]
        gl = [self.small.load(gate_bc[q][:, :], self.gate_rows[0][q, :].partition_broadcast(P), after=marks + self.gate_stored) for q in range(2)]
        gate = self.place("mla_gate", [P, T, DM])
        krot = self.place("mla_rope_key", [P, T, LROPE])
        self.rope_tmp = self.place("axial_swapped", [P, P])
        body = self.at
        ready = self.modulated_norm(0, [cl])
        self.fence()
        self.at = body
        lat = self.place("mla_latents", [P, T, LAT])
        srcs = [(self.hx, t) for t in range(XT)] + [(self.hc, t) for t in range(CT)]
        for n, lo, w in (("l0", 0, 512), ("l1", 512, 160), ("g0", LAT, 512), ("g1", LAT + 512, 512)):
            def evac(t, bank, made):
                if n[0] == "l":
                    return [act.step(lambda e: e.activation(lat[:, t, lo:lo + w], bank, ACT.Copy), [made])]
                return [act.step(lambda e: e.activation(gate[:, t, lo - LAT:lo - LAT + w], bank, ACT.Silu), [made])]
            for _ in self.to_tokens([(f"mla_{n}.{i}", 4 * i, 4) for i in range(2)], srcs, w, self.some_banks(T), evac, ready):
                pass
        r0 = QR + KVR
        dve.pending.append(act.now())
        for t in range(T):
            k = lat[:, t, r0:r0 + LROPE]
            if t < XT:
                self.axial(k.unsqueeze(1), krot[:, t, :].unsqueeze(1), t, 1)
            else:
                dve.step(lambda e: e.tensor_copy(krot[:, t, :], k))
        self.fence()
        lat_end = self.at
        self.at = self.hx_at
        cq = Split(self.place("cq_hi", [P, 3, 768], F32R), self.place("cq_lo", [P, 3, 768], F32R))
        ckv = Split(self.place("ckv_hi", [P, 2, 768], F32R), self.place("ckv_lo", [P, 2, 768], F32R))
        prob = Ring([self.place(f"mla_prob{j}", [P, 768]) for j in range(2)])
        probT = Ring([self.place(f"mla_probT{j}", [P, 768]) for j in range(2)])
        assert self.at <= self.after_hc, self.at - self.after_hc
        self.at = lat_end
        self.junk, self.junk2 = self.place("latent_junk", [P, QR]), self.place("latent_junk2", [P, QR])
        self.diag = self.place("latent_diag", [P, T, P])
        for lo, w, dst, gn in ((0, QR, cq, c["q_norm"]), (QR, KVR, ckv, c["kv_norm"])):
            self.norm_features([lat[:, t, lo:lo + w] for t in range(T)], w, [(dst, t * P) for t in range(T)],
                               cols[:, gn:gn + w // P], [])
            self.fence()
        self.at = body
        qT = self.place("mla_qT", [NOPE + LROPE, 4, 768])
        kT = self.place("mla_kT", [NOPE + LROPE, 4, 768])
        v = self.place("mla_v", [P, T, 4, LV])
        tok = Ring([self.place(f"mla_token_tile{j}", [P, 4, NOPE + LROPE]) for j in range(3)])
        scale = float((NOPE + LROPE) ** -0.5)
        tiny = self.tiny
        sizes = tiny[:, 128:256]
        stat = Ring([(sizes[:, 2 * j:2 * j + 1], sizes[:, 2 * j + 1:2 * j + 2]) for j in range(4)])
        proj_ready = [act.now(), dve.now()]
        last_use = []

        for g in range(4):
            heads = {}

            def turned(z, r, t, dst, what):
                b, = self.some_banks(1)

                def tr(e):
                    for h in range(4):
                        e.transpose(b.buf[0:96, h * P:(h + 1) * P], z.buf[:, h, :], self.ident)
                tt = pe.step(tr, [r] + b.free)
                o = act.step(lambda e: e.activation(dst[:, :, t * P:(t + 1) * P], b.buf[0:96, :].rearrange("p (h t) -> p h t", h=4), ACT.Copy), [tt] + last_use)
                b.free, z.free = [o], [tt]
                heads[what, t] = o

            def evac_q(t, bank, made):
                z = tok.take()
                a = act.step(lambda e: e.activation(z.buf[:, :, :], bank.rearrange("p (h d) -> p h d", h=4), ACT.Copy), [made] + z.free)
                r = a
                if t < XT:
                    dve.pending.append(a)
                    r = self.axial(z.buf[:, :, NOPE:], z.buf[:, :, NOPE:], t, 4)
                self.defer(lambda: turned(z, r, t, qT, "q"))
                return [a]

            def evac_kv(t, bank, made):
                z = tok.take()
                b4 = bank.rearrange("p (h d) -> p h d", h=4)
                a = act.step(lambda e: e.activation(z.buf[:, :, 0:NOPE], b4[:, :, 0:NOPE], ACT.Copy), [made] + z.free)
                d = dve.step(lambda e: e.tensor_copy(z.buf[:, :, NOPE:], krot[:, t, :].unsqueeze(1).broadcast_to([P, 4, LROPE])), z.free)
                d2 = dve.step(lambda e: e.tensor_copy(v[:, t, :, :], b4[:, :, NOPE:]), [a] + last_use)
                heads["v", t] = d2
                self.defer(lambda: turned(z, d2, t, kT, "k"))
                return [d2]
            for name, src, kn, w, ev in (("uq", cq, 3, 384, evac_q), ("ukv", ckv, 2, 512, evac_kv)):
                for _ in self.to_tokens([(f"{name}.{g}", 0, kn)], [(src, t) for t in range(T)], w, self.some_banks(T), ev, proj_ready):
                    pass
            self.flush()
            banks = self.banks
            pair = lambda b: self.ps[:, b:b + 2, :].rearrange("p b n -> p (b n)")
            s_turn = [0]
            state = {}

            def scores(u):
                h, t = units[u]
                b = 2 * (u % 2)
                s = pair(b)
                n, k0 = (768, 0) if t < XT else (CTX, SEQ)
                need = [heads["q", t]] + [heads["k", j] for j in range(k0 // P, T)] + banks[b].free + banks[b + 1].free

                def mm(e):
                    for lo in range(0, n, 512):
                        w = min(512, n - lo)
                        e.matmul(s[:, lo:lo + w], qT[:, h, t * P:(t + 1) * P], kT[:, h, k0 + lo:k0 + lo + w], start=True, stop=True)
                m = pe.step(mm, need)
                st = stat.take()
                mx, ls = st.buf
                dve.step(lambda e: e.tensor_reduce(mx, s[:, 0:n], AX_X, ALU.max), [m] + st.free)
                d = dve.step(lambda e: e.tensor_scalar(mx, mx, -scale, None, ALU.mult))
                p = prob.take()
                a = act.step(lambda e: e.activation(p.buf[:, 0:n], s[:, 0:n], ACT.Exp, bias=mx, scale=scale, accum_out=ls), [d] + p.free)
                banks[b].free = banks[b + 1].free = [a]
                state[u] = (p, n, k0, st, a)

            def turn(u):
                p, n, k0, st, a = state[u]
                s = pair(4)

                def tr(e):
                    for j in range(n // P):
                        e.transpose(s[:, j * P:(j + 1) * P], p.buf[:, j * P:(j + 1) * P], self.ident)
                t = pe.step(tr, [a] + banks[4].free + banks[5].free)
                p.free = [t]
                q = probT.take()
                w = min(n, 512)
                d = dve.step(lambda e: e.tensor_copy(q.buf[:, 0:w], s[:, 0:w]), [t] + q.free)
                copied = [d]
                if n > 512:
                    a2 = act.step(lambda e: e.activation(q.buf[:, 512:n], s[:, 512:n], ACT.Copy), [t] + q.free)
                    copied.append(a2)
                    banks[5].free = [a2]
                banks[4].free = [d]
                state[u] = (q, n, k0, st, a, copied)

            def values(u):
                h, t = units[u]
                q, n, k0, st, a, copied = state[u]
                ob = banks[6 + u % 2]

                def pv(e):
                    for j in range(n // P):
                        e.matmul(ob.buf[:, 0:LV], q.buf[:, j * P:(j + 1) * P], v[:, k0 // P + j, h, :], start=(j == 0), stop=(j == n // P - 1))
                m = pe.step(pv, copied + [heads["v", j] for j in range(k0 // P, T)] + ob.free)
                q.free = [m]
                ls = st.buf[1]
                dve.step(lambda e: e.reciprocal(ls, ls), [a])
                col = slice((4 * g + h) * LV, (4 * g + h + 1) * LV)
                d = dve.step(lambda e: e.scalar_tensor_tensor(gate[:, t, col], ob.buf[:, 0:LV], ls, gate[:, t, col], ALU.mult, ALU.mult), [m])
                ob.free, st.free = [d], [d]
            units = [(h, t) for h in range(4) for t in range(T)]
            for s in range(len(units) + 2):
                if s < len(units):
                    scores(s)
                if 1 <= s <= len(units):
                    turn(s - 1)
                if s >= 2:
                    values(s - 2)
            last_use = [pe.now()]

        self.fence()
        self.at = self.hx_at
        oT = Split(self.place("mla_oT_hi", [P, KT, 768], F32R), self.place("mla_oT_lo", [P, KT, 768], F32R))
        assert self.at <= self.after_hc
        ready = self.to_feature_major([gate[:, t, :] for t in range(T)], oT)
        self.fence()
        self.at = body
        gated = Ring([self.place(f"gated_out{j}", [P, 512]) for j in range(2)])
        for g in range(2):
            def evac_o(t, bank, made):
                sl = slice(g * 512, (g + 1) * 512)
                z = gated.take()
                res = self.x[:, t, sl] if t < XT else self.ctx_res[:, t - XT, sl]
                gb = gate_bc[0 if t < XT else 1]
                d = dve.step(lambda e: e.tensor_tensor(z.buf[:, :], bank, gb[:, sl], ALU.mult), [made] + gl + z.free)
                d2 = dve.step(lambda e: e.tensor_tensor(res, res, z.buf[:, :], ALU.add))
                z.free = [d2]
                return [d]
            for _ in self.to_tokens([(f"mla_o{g}.{i}", 4 * i, 4) for i in range(2)], [(oT, t) for t in range(T)], 512, self.some_banks(T), evac_o, ready):
                pass
        self.x_ready = [dve.now()]

    def axial(self, src, dst, t, heads):
        dve = self.dve
        at = C_AX + t * 64
        co = self.cst[:, at:at + 32].unsqueeze(1).broadcast_to([P, heads, 32])
        si = self.cst[:, at + 32:at + 64].rearrange("p (f c d) -> p f c d", f=2, c=2)
        tmp = self.rope_tmp[:, 0:heads * 32].rearrange("p (h d) -> p h d", h=heads)
        for f in range(2):
            for half in range(2):
                a, b = f * 16 + 8 * half, f * 16 + 8 * (1 - half)
                dve.step(lambda e: e.tensor_tensor(tmp[:, :, a:a + 8], src[:, :, b:b + 8], si[:, f, half, :].unsqueeze(1).broadcast_to([P, heads, 8]), ALU.mult))
        dve.step(lambda e: e.tensor_tensor(dst, src, co, ALU.mult))
        return dve.step(lambda e: e.tensor_tensor(dst, dst, tmp, ALU.add))

    def to_feature_major(self, tiles, dst):
        n = len(tiles)
        for k in range(KT):
            for lo in range(0, n, 4):
                m = min(4, n - lo)
                b, = self.some_banks(1)

                def tr(e):
                    for j in range(m):
                        e.transpose(b.buf[:, j * P:(j + 1) * P], tiles[lo + j][:, k * P:(k + 1) * P], self.ident)
                t = self.pe.step(tr, b.free)
                b.free = self.put_split(dst, (slice(None), k, slice(lo * P, (lo + m) * P)), b.buf[:, 0:m * P], [t])
        return [self.act.now(), self.dve.now()]

    def gla(self):
        pe, dve, act, pool, c, cols, cst = self.pe, self.dve, self.act, self.pool, self.c, self.cols, self.cst
        T = XT + CT
        marks = self.fence()
        self.at = self.after_hc
        self.place("context_residual_kept", [P, CT, DM])
        hc_at = self.hc_at
        self.hc = Split(self.nc.alloc_sbuf_tensor_at("gla_hc_hi", [P, KT, CTX], F32R, offset=hc_at),
                        self.nc.alloc_sbuf_tensor_at("gla_hc_lo", [P, KT, CTX], F32R, offset=hc_at + KT * CTX * 4))
        self.at = self.after_hc
        v = self.place("gla_v", [P, T, DM])
        body = self.at
        gate_bc = self.place("gla_mod_gate", [P, DM])
        gl = self.small.load(gate_bc[:, :], self.gate_rows[1][0, :].partition_broadcast(P), after=marks + self.gate_stored)
        q = self.place("gla_q", [P, GH, SEQ])
        kept = self.at
        ready = self.modulated_norm(1, [])
        self.at = kept
        k = self.place("gla_k", [P, GH, 768])
        cum = [self.place("gla_decay_fwd", [P, GH, T, GC + 1]), self.place("gla_decay_bwd", [P, GH, T, GC + 1])]
        end = self.at
        self.at = self.after_hc
        rtok = self.place("gla_rank_tok", [P, T, 32])
        rT = self.place("gla_rankT", [32, 768])
        wg = self.place("gla_gate_w", [32, 2, 512])
        lin = self.place("gla_gate_lin", [P, GH, 768])
        ones = self.place("gla_ones", [P, P])
        marks = self.fence()
        z = pool.step(lambda e: e.memset(wg[:, :, :], 0.0))
        z1 = pool.step(lambda e: e.memset(ones[:, :], 1.0))
        z2 = pool.step(lambda e: e.memset(cum[0][:, :, :, 0:1], 0.0))
        z3 = pool.step(lambda e: e.memset(cum[1][:, :, :, 0:1], 0.0))
        w1 = self.small.load(wg[0:GRANK, 0, :], self.ins["gla_w_gf_2"][0], after=[z])
        w2 = self.small.load(wg[GRANK:2 * GRANK, 1, :], self.ins["gla_w_gb_2"][0], after=[z])
        srcs = [(self.hx, t) for t in range(XT)] + [(self.hc, t) for t in range(CT)]
        for _ in self.to_tokens([("gla_r", 0, 8)], srcs, 32, self.some_banks(T),
                                lambda t, bank, made: [act.step(lambda e: e.activation(rtok[:, t, :], bank, ACT.Copy), [made])], ready):
            pass
        for lo in (0, 4):
            m = min(4, T - lo)
            b, = self.some_banks(1)

            def tr(e):
                for j in range(m):
                    e.transpose(b.buf[0:32, j * P:(j + 1) * P], rtok[:, lo + j, :], self.ident)
            t = pe.step(tr, [act.now()] + b.free)
            b.free = [act.step(lambda e: e.activation(rT[:, lo * P:(lo + m) * P], b.buf[0:32, 0:m * P], ACT.Copy), [t])]
        r_ready = act.now()
        lin_read = []
        for d_ in range(2):
            body4 = lambda m: cum[d_][:, m, :, 1:GC + 1]
            for m in range(GH):
                for lo, n in ((0, SEQ), (SEQ, CTX)):
                    b, = self.some_banks(1)
                    t = pe.step(lambda e: e.matmul(b.buf[:, 0:n], wg[:, d_, m * P:(m + 1) * P], rT[:, lo:lo + n], start=True, stop=True), [r_ready, w1, w2] + b.free)
                    bc = cols[:, c["gla_b"] + 4 * d_ + m:c["gla_b"] + 4 * d_ + m + 1]
                    b.free = [dve.step(lambda e: e.tensor_scalar(lin[:, m, lo:lo + n], b.buf[:, 0:n], bc, None, ALU.add), [t])]
            made = dve.now()
            for m in range(GH):
                src = lin[:, m, :].rearrange("p (t n) -> p t n", t=T)
                act.step(lambda e: e.activation(body4(m), src, ACT.Abs), [made])
                act.step(lambda e: e.activation(body4(m), body4(m), ACT.Exp, scale=-1.0))
            for m in range(GH):
                a = act.step(lambda e: e.activation(body4(m), body4(m), ACT.Ln, bias=1.0))
                src = lin[:, m, :].rearrange("p (t n) -> p t n", t=T)
                dve.step(lambda e: e.scalar_tensor_tensor(body4(m), src, 0.0, body4(m), ALU.min, ALU.subtract), [a])
                for ch in range(T):
                    dve.step(lambda e: e.tensor_tensor_scan(cum[d_][:, m, ch, 1:GC + 1], ones[:, :], cum[d_][:, m, ch, 1:GC + 1], 0.0, ALU.mult, ALU.add), [z1])

        def evac_k(m, cx, bank, made):
            n0 = 0 if cx == 0 else SEQ
            return [act.step(lambda e: e.activation(k[:, m, n0:n0 + bank.shape[1]], bank, ACT.Copy), [made])]
        self.to_both([(f"gla_k.{i}", 4 * i, 4) for i in range(2)], (self.hx, self.hc), self.some_banks(8), evac_k, ready)
        for _ in self.to_features([(f"gla_q.{i}", 4 * i, 4) for i in range(2)], self.hx, SEQ, self.some_banks(4),
                                  lambda m, bank, made: [act.step(lambda e: e.activation(q[:, m, :], bank, ACT.Copy, scale=GDK ** -0.5), [made])], ready):
            pass
        pe.pending += [dve.now(), act.now()]
        for g in range(2):
            for _ in self.to_tokens([(f"gla_v{g}.{i}", 4 * i, 4) for i in range(2)], srcs, 512, self.some_banks(T),
                                    lambda t, bank, made: [act.step(lambda e: e.activation(v[:, t, g * 512:(g + 1) * 512], bank, ACT.Copy), [made])], ready):
                pass
        self.fence()
        self.at = self.hc_at
        gate = self.place("gla_gate", [P, XT, DM])
        assert self.at <= self.after_hc
        self.at = end
        S = [self.place("gla_state_fwd", [P, GH, GDV]), self.place("gla_state_bwd", [P, GH, GDV])]
        Kd = [[self.place(f"gla_Kd{h}", [P, P])] for h in range(GH)]
        assert self.at <= self.high_end
        self.at = self.high_end
        tot = self.place("gla_total", [P, 2, GH * T])
        etot = self.place("gla_total_decay", [P, 2, GH * T])
        ref = self.place("gla_reference", [P, 2, GH * T, GC // GB])
        for d_ in range(2):
            dve.step(lambda e: e.tensor_scalar(tot[:, d_, :].rearrange("p (h t) -> p h t", h=GH), cum[d_][:, :, :, GC], 1.0 / GATE_NORM, None, ALU.mult))
            mids = cum[d_][:, :, :, 0:GC].rearrange("p h t (b n) -> p (h t) b n", b=GC // GB)[:, :, :, GB // 2]
            dve.step(lambda e: e.tensor_scalar(ref[:, d_, :, :], mids, (1.0 if d_ == 0 else -1.0) / GATE_NORM, None, ALU.mult))
        act.step(lambda e: e.activation(etot[:, :, :], tot[:, :, :], ACT.Exp), [dve.now()])
        dve.pending.append(act.now())
        masks = [cst[:, C_UP:C_UP + P].bitcast(I32), cst[:, C_LOW:C_LOW + P].bitcast(I32)]
        inv = 1.0 / GATE_NORM
        state_ready = {}
        Kd = [Ring(k_) for k_ in Kd]

        def decayed_keys(d_, h, ch, job):
            fwd, kd, cc = d_ == 0, Kd[h].take(), cum[d_][:, h, ch, :]
            tcol = tot[:, d_, h * T + ch:h * T + ch + 1]
            if fwd:
                a = act.step(lambda e: e.activation(kd.buf[:, :], cc[:, 1:P + 1], ACT.Exp, scale=-inv, bias=tcol), kd.free)
            else:
                a = act.step(lambda e: e.activation(kd.buf[:, :], cc[:, 0:P], ACT.Exp, scale=inv), kd.free)
            m_ = pool.step(lambda e: e.tensor_tensor(kd.buf[:, :], kd.buf[:, :], k[:, h, ch * P:(ch + 1) * P], ALU.mult), [a])
            yield
            b, = self.scan_banks(1)
            t = pe.step(lambda e: e.transpose(b.buf[:, 0:P], kd.buf[:, :], self.ident), [m_] + b.free)
            job["kd"], job["kd_made"] = kd, act.step(lambda e: e.activation(kd.buf[:, :], b.buf[:, 0:P], ACT.Copy), [t])
            b.free = [job["kd_made"]]
            yield

        def update_state(d_, h, ch, job, first, read):
            s_state, kd = S[d_][:, h, :], job["kd"]
            b, = self.scan_banks(1)
            t = pe.step(lambda e: e.matmul(b.buf[:, 0:GDV], kd.buf[:, :], v[:, ch, h * GDV:(h + 1) * GDV], start=True, stop=True), [job["kd_made"]] + b.free)
            kd.free = [t]
            if first:
                s2 = dve.step(lambda e: e.tensor_copy(s_state, b.buf[:, 0:GDV]), [t])
            else:
                et = etot[:, d_, h * T + ch:h * T + ch + 1]
                s2 = dve.step(lambda e: e.scalar_tensor_tensor(s_state, s_state, et, b.buf[:, 0:GDV], ALU.mult, ALU.add), [t] + read)
            b.free = state_ready[d_, h] = [s2]
            yield

        def context_states():
            for n in range(CT):
                for h in range(GH):
                    for d_ in range(2):
                        ch, job = XT + (n if d_ == 0 else CT - 1 - n), {}
                        yield from decayed_keys(d_, h, ch, job)
                        yield from update_state(d_, h, ch, job, n == 0, [])

        def gate_projection():
            for g in range(2):
                yield from self.to_tokens([(f"gla_g{g}.{i}", 4 * i, 4) for i in range(2)], srcs[0:XT], 512, self.banks[0:4],
                                          lambda t, bank, made: [dve.step(lambda e: e.tensor_copy(gate[:, t, g * 512:(g + 1) * 512], bank), [made])], ready)
        self.scan_turn = 0

        def scan_banks(n):
            self.scan_turn += n
            return [self.banks[4 + (self.scan_turn - n + i) % 4] for i in range(n)]
        self.scan_banks = scan_banks
        interleave((context_states(), 3), (gate_projection(), 1))
        self.scan_banks = self.some_banks

        self.fence()
        act.step(lambda e: e.activation(gate[:, :, :], gate[:, :, :], ACT.Silu))
        self.at = self.hx_at
        o = self.place("gla_o", [P, XT, DM])
        two = lambda n, spare: [Ring([self.place(f"{n}{h}", [P, P])[:, :], spare[:, h, :]]) for h in range(GH)]
        Kt = [Ring([self.place(f"gla_Kt{h}", [P, 4, P])]) for h in range(GH)]
        Qt = [Ring([self.place(f"gla_Qt{h}", [P, P])]) for h in range(GH)]
        spare = v[:, XT:T, :].rearrange("p t n -> p (t n)").rearrange("p (a h n) -> p a h n", a=4, h=GH)
        A, Qh = two("gla_A", spare[:, 0, :, :]), two("gla_Qh", spare[:, 1, :, :])
        for h in range(GH):
            Kd[h].slots.append(Slot(spare[:, 2, h, :]))
        assert self.at <= self.hc_at
        o_written = {}
        jobs = {}

        def prepare_chunk(h, n):
            d_, ch, last = order[n]
            fwd, job = d_ == 0, {}
            jobs[h, n] = job
            cc, sh = cum[d_][:, h, ch, :], 1 if d_ == 0 else 0
            tcol = tot[:, d_, h * T + ch:h * T + ch + 1]
            kk, qq = k[:, h, ch * P:(ch + 1) * P], q[:, h, ch * P:(ch + 1) * P]
            kt, qt, qh, at_ = Kt[h].take(), Qt[h].take(), Qh[h].take(), A[h].take()
            if n % len(x_chunks) < 2:
                at_.free = [pool.step(lambda e: e.memset(at_.buf, 0.0), at_.free)]
            rr = ref[:, d_, h * T + ch, :]

            def keys(e):
                for I in range(GC // GB):
                    e.activation(kt.buf[:, I, :], cc[:, sh:sh + P], ACT.Exp, scale=-inv if fwd else inv, bias=rr[:, I:I + 1])
            blocks = lambda ap: ap.rearrange("p (b n) -> p b n", b=GC // GB)
            mid = blocks(cc[:, 0:GC])[:, :, GB // 2:GB // 2 + 1].broadcast_to([P, GC // GB, GB])
            dd = dve.step(lambda e: e.tensor_tensor(blocks(qt.buf[:, :]), blocks(cc[:, sh:sh + P]), mid, ALU.subtract), qt.free)
            a = act.step(keys, kt.free)
            yield
            d1 = dve.step(lambda e: e.tensor_tensor(kt.buf[:, :, :], kt.buf[:, :, :], kk.unsqueeze(1).broadcast_to([P, 4, P]), ALU.mult), [a])
            a2 = act.step(lambda e: e.activation(qt.buf[:, :], qt.buf[:, :], ACT.Exp, scale=inv if fwd else -inv), [dd])
            d2 = dve.step(lambda e: e.tensor_tensor(qt.buf[:, :], qt.buf[:, :], qq, ALU.mult), [a2])
            if fwd:
                a3 = act.step(lambda e: e.activation(qh.buf, cc[:, 1:P + 1], ACT.Exp, scale=inv), qh.free)
            else:
                a3 = act.step(lambda e: e.activation(qh.buf, cc[:, 0:P], ACT.Exp, scale=-inv, bias=tcol), qh.free)
            d3 = pool.step(lambda e: e.tensor_tensor(qh.buf, qh.buf, qq, ALU.mult), [a3])
            yield
            if not last:
                yield from decayed_keys(d_, h, ch, job)
            b, = self.some_banks(1)

            def am(e):
                for I in range(4):
                    e.matmul(b.buf[:, I * GB:(I + 1) * GB], kt.buf[:, I, :], qt.buf[:, I * GB:(I + 1) * GB], start=True, stop=True)
            t = pe.step(am, [d1, d2] + b.free)
            kt.free, qt.free = [t], [t]
            d4 = dve.step(lambda e: e.copy_predicated(at_.buf, masks[d_], b.buf[:, 0:P]), [t] + at_.free)
            b.free = [d4]
            job.update(qh=qh, at=at_, ready=[d3, d4])
            yield

        def finish_chunk(h, n):
            d_, ch, last = order[n]
            job = jobs.pop((h, n))
            qh, at_, s_state = job["qh"], job["at"], S[d_][:, h, :]
            ob, = self.some_banks(1)

            def om(e):
                e.matmul(ob.buf[:, 0:GDV], qh.buf, s_state, start=True, stop=False)
                e.matmul(ob.buf[:, 0:GDV], at_.buf, v[:, ch, h * GDV:(h + 1) * GDV], start=False, stop=True)
            t = pe.step(om, job["ready"] + state_ready[d_, h] + ob.free)
            qh.free, at_.free = [t], [t]
            oc = o[:, ch, h * GDV:(h + 1) * GDV]
            if (ch, h) in o_written:
                ob.free = [dve.step(lambda e: e.tensor_tensor(oc, ob.buf[:, 0:GDV], oc, ALU.add), [t, o_written[ch, h]])]
            else:
                ob.free = [act.step(lambda e: e.activation(oc, ob.buf[:, 0:GDV], ACT.Copy), [t])]
            o_written[ch, h] = ob.free[0]
            yield
            if not last:
                yield from update_state(d_, h, ch, job, False, [t])
        x_chunks = list(range(XT))
        order = [(0, ch, ch == XT - 1) for ch in x_chunks] + [(1, ch, ch == 0) for ch in reversed(x_chunks)]

        def head(h):
            for _ in range(2 * h):
                yield
            yield from prepare_chunk(h, 0)
            for n in range(len(order)):
                live = [finish_chunk(h, n)] + ([prepare_chunk(h, n + 1)] if n + 1 < len(order) else [])
                while live:
                    live = [s for s in live if next(s, live) is not live]
                    yield
        interleave(*[(head(h), 1) for h in range(GH)])

        self.fence()
        self.at = end
        orow = self.place("gla_norm_row", [P, GDV])
        sq = self.place("gla_square", [P, DM])
        gated = Ring([self.place(f"gla_gated_out{j}", [P, 512]) for j in range(2)])
        rl = self.small.load(orow[:, :], self.ins["gla_o_norm_2"][0].partition_broadcast(P), after=self.fence())
        rs = self.tiny[:, 0:16]
        H = lambda ap: ap.rearrange("p (h d) -> p h d", h=GH)
        for t in range(XT):
            dve.step(lambda e: e.tensor_tensor(sq[:, :], o[:, t, :], o[:, t, :], ALU.mult))
            dve.step(lambda e: e.tensor_reduce(rs[:, 4 * t:4 * t + 4], H(sq[:, :]), AX_X, ALU.add))
        d = dve.step(lambda e: e.tensor_scalar(rs, rs, 1.0 / GDV, EPS, ALU.mult, ALU.add))
        a = act.step(lambda e: e.activation(rs, rs, ACT.Sqrt), [d])
        dve.step(lambda e: e.reciprocal(rs, rs), [a])
        for t in range(XT):
            dve.step(lambda e: e.tensor_tensor(H(gate[:, t, :]), H(gate[:, t, :]), orow[:, :].unsqueeze(1).broadcast_to([P, GH, GDV]), ALU.mult), [rl])
            for h in range(GH):
                sl = slice(h * GDV, (h + 1) * GDV)
                dve.step(lambda e: e.scalar_tensor_tensor(gate[:, t, sl], o[:, t, sl], rs[:, 4 * t + h:4 * t + h + 1], gate[:, t, sl], ALU.mult, ALU.mult))
        self.fence()
        self.hx = Split(self.nc.alloc_sbuf_tensor_at("gla_oT_hi", [P, KT, SEQ], F32R, offset=self.hx_at),
                        self.nc.alloc_sbuf_tensor_at("gla_oT_lo", [P, KT, SEQ], F32R, offset=self.hx_at + KT * SEQ * 4))
        ready = self.to_feature_major([gate[:, t, :] for t in range(XT)], self.hx)
        for g in range(2):
            def evac_o(t, bank, made):
                sl = slice(g * 512, (g + 1) * 512)
                z = gated.take()
                d = dve.step(lambda e: e.tensor_tensor(z.buf[:, :], bank, gate_bc[:, sl], ALU.mult), [made, gl] + z.free)
                z.free = [dve.step(lambda e: e.tensor_tensor(self.x[:, t, sl], self.x[:, t, sl], z.buf[:, :], ALU.add))]
                return [d]
            for _ in self.to_tokens([(f"gla_o{g}.{i}", 4 * i, 4) for i in range(2)], [(self.hx, t) for t in range(XT)], 512, self.some_banks(XT), evac_o, ready):
                pass
        self.x_ready = [dve.now()]
        self.at = self.hc_at

    def units(self, name, a, c0, n=512, k0=0, kn=8, per=4, raw=False):
        v = a.rearrange("(k p) n -> p k n", p=P)
        if kn <= per:
            return [(name, v[:, k0:k0 + kn, c0:c0 + n], kn, n, raw)]
        return [(f"{name}.{i}", v[:, k0 + i * per:k0 + (i + 1) * per, c0:c0 + n], per, n, raw) for i in range(kn // per)]

    def second_plan(self, mla=True, gla=True):
        ins, plan = self.ins, []
        if mla:
            w = ins["mla_w_in_2"][0]
            for n, c0, cn in (("l0", 0, 512), ("l1", 512, 160), ("g0", LAT, 512), ("g1", LAT + 512, 512)):
                plan += self.units(f"mla_{n}", w, c0, cn)
            for g in range(4):
                plan += self.units(f"uq.{g}", ins["mla_w_uq_2"][0], 384 * g, 384, kn=3)
                plan += self.units(f"ukv.{g}", ins["mla_w_ukv_2"][0], 512 * g, kn=2)
            for g in range(2):
                plan += self.units(f"mla_o{g}", ins["mla_w_out_2"][0], 512 * g)
        if gla:
            w = ins["gla_w_in_2"][0]
            plan += self.units("gla_r", w, 3072, 32, per=8)
            plan += self.units("gla_k", w, 512)
            plan += self.units("gla_q", w, 0)
            for n, c0 in (("v", 1024), ("g", 2048)):
                for g in range(2):
                    plan += self.units(f"gla_{n}{g}", w, c0 + 512 * g)
            for g in range(2):
                plan += self.units(f"gla_o{g}", ins["gla_w_out_2"][0], 512 * g)
        return plan


def build(nc, ins, out):
    with ExitStack() as ctx:
        p = Program(nc, ins, out, ctx)
        p.setup()
        plan = []
        for l in range(DEPTH):
            plan += p.layer_plan(l)
        plan += p.second_plan()
        p.plan_weights(plan)
        for l in range(DEPTH):
            p.layer(l)
        p.at = p.hc_at
        p.final_norm("final_norm_w")
        p.mla()
        p.gla()
        p.final_norm("final_g_2")
        xs = out.rearrange("(t p) d -> p t d", p=P)
        p.finish = (xs, p.x_ready)
        block = ctx.enter_context(nc.Block())

        @block.sync
        def _(e):
            emit(e, p.sp_queue)
            for s, v in p.finish[1]:
                e.wait_ge(s, v)
            e.dma_start(p.finish[0], p.x[:, :, :]).then_inc(p.out_sem, 16)
            e.wait_ge(p.out_sem, 16)

        @block.gpsimd
        def _(e):
            emit(e, p.pool.queue)

        @block.scalar
        def _(e):
            emit(e, p.act.queue)

        @block.vector
        def _(e):
            emit(e, p.dve.queue)

        @block.tensor
        def _(e):
            emit(e, p.pe.queue)
        return p


_INS = ['x', 'positions', 'norm_mix_w', 'w_in', 'b_in', 'conv_w', 'conv_b', 'mlstm_norm_w', 'w_proj_att',
        'w_proj_mlstm', 'w_out', 'norm_mlp_w', 'w_ff1', 'w_ff2', 'final_norm_w', 'c_2', 'ctx_2', 'c_ctx_2', 'ada_w_2',
        'ada_b_2', 'norm_g_2', 'final_g_2', 'mla_w_in_2', 'mla_q_norm_2', 'mla_w_uq_2', 'mla_kv_norm_2',
        'mla_w_ukv_2', 'mla_w_out_2', 'gla_w_in_2', 'gla_w_gf_2', 'gla_b_gf_2', 'gla_w_gb_2', 'gla_b_gb_2',
        'gla_o_norm_2', 'gla_w_out_2']


def kernel(**inputs):
    import numpy as _np
    import concourse.bacc as _bacc
    from concourse import mybir as _mybir
    from concourse.bass_utils import run_bass_kernel_spmd as _run

    nc = _bacc.Bacc("TRN2", target_bir_lowering=False, num_devices=1)
    arrays, ins = {}, {}
    for name in _INS:
        arrays[f"in_{name}"] = _np.ascontiguousarray(inputs[name])
    arrays["in_constants"] = constants()
    for name, a in arrays.items():
        ins[name[3:]] = nc.dram_tensor(name, a.shape, _mybir.dt.from_np(a.dtype), kind="ExternalInput").ap()
    out = nc.dram_tensor("out_x", (SEQ, DM), _mybir.dt.float32, kind="ExternalOutput").ap()
    build(nc, ins, out)
    r = _run(nc, [arrays], core_ids=[0])
    return r.results[0]["out_x"].reshape(1, SEQ, DM)
```

```python
from contextlib import ExitStack

import numpy as np

import concourse.bass as bass
from concourse import mybir

P = 128
F32 = mybir.dt.float32
F32R = mybir.dt.float32r
I32 = mybir.dt.int32
ALU = mybir.AluOpType
ACT = mybir.ActivationFunctionType
AX_X = mybir.AxisListType.X

SEQ, CTX, DM = 512, 256, 1024
XT, CT, KT = SEQ // P, CTX // P, DM // P
DEPTH = 2
EPS = 1e-6
NEG = -1e30

AH, AHD = 8, 64
MH, MHD = 4, 128
ROPE_HALF = 8
CONV = 4
COL_AQ, COL_AK, COL_AV, COL_MQ, COL_MV, COL_MO, COL_MI, COL_GA, COL_GB, D_IN = (
    0, 512, 1024, 1536, 2560, 3072, 3584, 3592, 4616, 5640)
D_FF = 4096
PATTERNS = ((128, 1), (512, 4), (2048, 16))
ROPE_THETA = 500000.0

LH, NOPE, LROPE, LV = 16, 64, 32, 64
QR, KVR = 384, 256
LAT = QR + KVR + LROPE
GH, GDK, GDV, GRANK = 4, 128, 256, 16
GC = 128
GB = 32
GATE_NORM = 16.0

UNIT = 2048

C_ID, C_ATT, C_TRI, C_UP, C_ONES, C_NSEL, C_SEL2, C_AX, C_INV, C_LOW, C_END = (
    0, 128, 640, 768, 896, 1024, 1536, 1792, 2048, 2056, 2184)


def constants():
    c = np.zeros((P, C_END), np.float32)
    p = np.arange(P)
    c[:, C_ID:C_ID + P] = np.eye(P)
    d = p[:, None] + 3 * P - np.arange(4 * P)[None, :]
    n = sum(((d >= 0) & (d <= w) & (d % s == 0)).astype(np.float64) for w, s in PATTERNS)
    c[:, C_ATT:C_ATT + 512] = np.where(n > 0, np.log(np.maximum(n, 1)) * AHD ** 0.5, NEG)
    c[:, C_TRI:C_TRI + P] = np.where(p[:, None] <= p[None, :], 0.0, NEG)
    c[:, C_UP:C_UP + P] = p[:, None] <= p[None, :]
    c[:, C_LOW:C_LOW + P] = p[:, None] >= p[None, :]
    c[:, C_ONES:C_ONES + P] = 1.0
    for h in range(MH):
        c[h, C_NSEL + h * P:C_NSEL + (h + 1) * P] = -1.0
    for r in range(2):
        c[r, C_SEL2 + r * P:C_SEL2 + (r + 1) * P] = 1.0
    inv = (10000.0 ** (-np.arange(8, dtype=np.float32) / 8)).astype(np.float32)
    tok = np.arange(SEQ)
    for t in range(XT):
        at = C_AX + t * 64
        for half, pos in enumerate((tok // 64, tok % 64)):
            ang = (pos[t * P:(t + 1) * P, None].astype(np.float32) * inv).astype(np.float32)
            co, si = np.cos(ang), np.sin(ang)
            c[:, at + half * 16:at + half * 16 + 16] = np.concatenate([co, co], 1)
            c[:, at + 32 + half * 16:at + 48 + half * 16] = np.concatenate([-si, si], 1)
    c[:, C_INV:C_INV + 8] = (np.float32(ROPE_THETA) ** (-np.arange(0, 16, 2, dtype=np.float32) / 16))
    return c


def _queued(call):
    def queue(self, *args, **kwargs):
        self.calls.append((call, args, kwargs))
    return queue


class Calls:

    def __init__(self):
        self.calls = []

    matmul = _queued(lambda e, a, k: e.matmul(*a, **k))
    transpose = _queued(lambda e, a, k: e.transpose(*a, **k))
    activation = _queued(lambda e, a, k: e.activation(*a, **k))
    tensor_tensor = _queued(lambda e, a, k: e.tensor_tensor(*a, **k))
    tensor_scalar = _queued(lambda e, a, k: e.tensor_scalar(*a, **k))
    scalar_tensor_tensor = _queued(lambda e, a, k: e.scalar_tensor_tensor(*a, **k))
    tensor_tensor_reduce = _queued(lambda e, a, k: e.tensor_tensor_reduce(*a, **k))
    tensor_tensor_scan = _queued(lambda e, a, k: e.tensor_tensor_scan(*a, **k))
    tensor_reduce = _queued(lambda e, a, k: e.tensor_reduce(*a, **k))
    tensor_copy = _queued(lambda e, a, k: e.tensor_copy(*a, **k))
    copy_predicated = _queued(lambda e, a, k: e.copy_predicated(*a, **k))
    reciprocal = _queued(lambda e, a, k: e.reciprocal(*a, **k))
    dma_start = _queued(lambda e, a, k: e.dma_start(*a, **k))
    memset = _queued(lambda e, a, k: e.memset(*a, **k))


def emit(e, queue):
    reached = {}
    for waits, calls, sem, increment in queue:
        for w, value in waits:
            if value > reached.get(w.name, 0):
                e.wait_ge(w, value)
                reached[w.name] = value
        for call, args, kwargs in calls:
            last = call(e, args, kwargs)
        last.then_inc(sem, increment)


class Engine:

    def __init__(self, done, in_order=False):
        self.done, self.in_order = done, in_order
        self.count, self.queue, self.pending = 0, [], []

    def now(self):
        return (self.done, self.count)

    def step(self, issue, after=()):
        waits = list(after) + self.pending
        self.pending = []
        if not self.in_order:
            waits.append(self.now())
        most = {}
        for sem, value in waits:
            if value > most.get(sem.name, (sem, 0))[1]:
                most[sem.name] = (sem, value)
        self.count += 1
        step = Calls()
        issue(step)
        self.queue.append((list(most.values()), step.calls, self.done, 1))
        return (self.done, self.count)


class Loads:

    def __init__(self, sems, queue):
        self.sems, self.counts, self.n, self.queue = sems, [0] * len(sems), 0, queue

    def load(self, out, in_, after=(), strided=False):
        i = self.n % len(self.sems)
        self.n += 1
        waits = list(after)
        if self.counts[i]:
            waits.append((self.sems[i], self.counts[i]))
        self.counts[i] += 16
        step = Calls()
        step.dma_start(out, in_, allow_slow_non_contiguous=strided)
        self.queue.append((waits, step.calls, self.sems[i], 16))
        return (self.sems[i], self.counts[i])


class Slot:

    def __init__(self, buf):
        self.buf, self.free = buf, []


class Ring:
    def __init__(self, bufs):
        self.slots, self.n = [Slot(b) for b in bufs], 0

    def take(self):
        self.n += 1
        return self.slots[(self.n - 1) % len(self.slots)]


class Split:

    def __init__(self, hi, lo):
        self.hi, self.lo = hi, lo


def needed(ready, k):
    return ready[k] if isinstance(ready, dict) else list(ready)


def woven(*streams):
    live = list(streams)
    while live:
        for entry in list(live):
            for _ in range(entry[1]):
                if next(entry[0], live) is live:
                    live.remove(entry)
                    break
                yield


def interleave(*streams):
    for _ in woven(*streams):
        pass


class Program:
    def __init__(self, nc, ins, out, ctx):
        self.nc, self.ins, self.out, self.ctx = nc, ins, out, ctx
        sem = lambda n: ctx.enter_context(nc.semaphore(n))
        self.pe = Engine(sem("pe_done"), in_order=True)
        self.dve = Engine(sem("dve_done"))
        self.act = Engine(sem("act_done"))
        self.pool = Engine(sem("pool_done"))
        self.sp_queue = []
        self.sp = Loads([sem(f"sp_load{i}") for i in range(4)], self.sp_queue)
        self.small = Loads([sem(f"small_load{i}") for i in range(8)], self.pool.queue)
        self.gate_rows = nc.dram_tensor("mod_gate_rows", (DEPTH, 2, DM), F32, kind="Internal").ap()
        self.high = 0
        self.high_end = 229344 - 2048
        self.at = 16512
        self.names = self.bank_turn = 0
        self.ps = ctx.enter_context(nc.psum_tensor("ps", [P, 8, 512], F32))
        self.gate_stored, self.stored = [], []
        self.banks = [Slot(self.ps[:, i, :]) for i in range(8)]
        self.fixed()

    def place(self, name, shape, dt=F32):
        size = int(np.prod(shape[1:])) * 4
        self.at = (self.at + 31) // 32 * 32
        t = self.nc.alloc_sbuf_tensor_at(f"{name}_{self.names}", list(shape), dt, offset=self.at)
        self.names += 1
        self.at += size
        assert self.at <= 229344, (name, self.at)
        self.high = max(self.high, self.at)
        return t

    def fixed(self):
        self.cst = self.place("constant_columns", [P, C_END])
        self.cols = self.place("feature_columns", [P, 256])
        self.rope = self.place("rope_tables", [P, XT, 32])
        self.tiny = self.place("tiny", [P, 256])
        self.x = self.place("x_residual", [P, XT, DM])
        self.stage = Ring([self.place(f"w_stage{i}", [P, UNIT]) for i in range(2)])
        self.w_split = Ring([Split(self.place(f"w_hi{i}", [P, UNIT], F32R), self.place(f"w_lo{i}", [P, UNIT], F32R))
                             for i in range(2)])
        self.at = (self.at + 31) // 32 * 32
        self.hx_at = self.at
        self.hx = Split(self.place("hx_hi", [P, KT, SEQ], F32R), self.place("hx_lo", [P, KT, SEQ], F32R))
        self.hc_at = self.at
        self.negsel = self.cst[0:MH, C_NSEL:C_NSEL + MH * P].rearrange("p (h n) -> p h n", h=MH)
        self.ident = self.cst[:, C_ID:C_ID + P]
        self.area = None

    def fence(self):
        marks = [e.now() for e in (self.pe, self.dve, self.act, self.pool)] + self.gate_stored
        marks = [m for m in marks if m[1]]
        for e in (self.pe, self.dve, self.act, self.pool):
            e.pending = list(marks)
        return marks

    def plan_weights(self, plan):
        self.plan, self.loaded, self.prepared, self.taken = plan, 0, 0, 0
        self.staged, self.ready, self.released, self.deferred = {}, {}, set(), []

    def refill(self):
        while self.loaded < len(self.plan) and (self.loaded < 2 or self.loaded - 2 in self.released):
            name, src, k, n, raw = self.plan[self.loaded]
            slot = self.stage.take()
            dst = slot.buf[:, 0:k * n].rearrange("p (k n) -> p k n", k=k)
            self.staged[self.loaded] = (slot, dst, self.sp.load(dst, src, after=slot.free))
            self.loaded += 1

    def prepare(self):
        self.refill()
        i = self.prepared
        name, src, k, n, raw = self.plan[i]
        slot, staged, landed = self.staged.pop(i)
        if raw:
            self.ready[i] = (staged, slot, [landed])
        else:
            w = self.w_split.take()
            hi = w.buf.hi[:, 0:k * n].rearrange("p (k n) -> p k n", k=k)
            lo = w.buf.lo[:, 0:k * n].rearrange("p (k n) -> p k n", k=k)
            a = self.act.step(lambda e: e.activation(hi, staged, ACT.Copy), [landed] + w.free)
            b = self.dve.step(lambda e: e.tensor_tensor(lo, staged, hi.bitcast(F32), ALU.subtract), [a, landed] + w.free)
            slot.free = [a, b]
            self.released.add(i)
            self.ready[i] = (Split(hi, lo), w, [a, b])
        self.prepared += 1
        self.refill()

    def take(self, name):
        i = self.taken
        assert self.plan[i][0] == name, (self.plan[i][0], name)
        while self.prepared <= i:
            self.prepare()
        self.taken += 1
        return self.ready.pop(i)

    def prepare_ahead(self):
        if self.prepared == self.taken < len(self.plan) and not self.plan[self.taken][4]:
            self.prepare()

    def defer(self, task):
        self.deferred.append(task)

    def flush(self):
        tasks, self.deferred = self.deferred, []
        for task in tasks:
            task()

    def raw_done(self, slot, ticket):
        slot.free = [ticket]
        self.released.add(self.taken - 1)
        self.refill()

    @staticmethod
    def mm3(e, out, a, b, start, stop):
        e.matmul(out, a[0], b[0], start=start, stop=False)
        e.matmul(out, a[0], b[1], start=False, stop=False)
        return e.matmul(out, a[1], b[0], start=False, stop=stop)

    def to_tokens(self, halves, srcs, nc_, banks, evac, ready=()):
        last = None
        for u, (uname, k0, kn) in enumerate(halves):
            w, slot, rdy = self.take(uname)
            for j, (src, t, *own) in enumerate(srcs):
                bank = banks[j]

                def issue(e, src=src, t=t, bank=bank, w=w, k0=k0, kn=kn, u=u):
                    for k in range(kn):
                        l = self.mm3(e, bank.buf[:, 0:nc_],
                                     (src.hi[:, k0 + k, t * P:(t + 1) * P], src.lo[:, k0 + k, t * P:(t + 1) * P]),
                                     (w.hi[:, k, :], w.lo[:, k, :]),
                                     u == 0 and k == 0, u == len(halves) - 1 and k == kn - 1)
                    return l
                last = self.pe.step(issue, rdy + (bank.free if u == 0 else []) + needed(ready, k0 + kn - 1) + sum(own, []))
                if j == 0:
                    self.prepare_ahead()
                tasks, self.deferred = self.deferred, []
                if u == len(halves) - 1:
                    bank.free = evac(j, bank.buf[:, 0:nc_], last)
                for task in tasks:
                    task()
                yield
            slot.free = [last]

    def to_features(self, halves, src, ntok, banks, evac, ready=(), m_tiles=4, feat=P):
        last = None
        for u, (uname, k0, kn) in enumerate(halves):
            w, slot, rdy = self.take(uname)
            for m in range(m_tiles):
                bank = banks[m]

                def issue(e, m=m, bank=bank, w=w, k0=k0, kn=kn, u=u):
                    for k in range(kn):
                        l = self.mm3(e, bank.buf[0:feat, 0:ntok],
                                     (w.hi[:, k, m * feat:(m + 1) * feat], w.lo[:, k, m * feat:(m + 1) * feat]),
                                     (src.hi[:, k0 + k, 0:ntok], src.lo[:, k0 + k, 0:ntok]),
                                     u == 0 and k == 0, u == len(halves) - 1 and k == kn - 1)
                    return l
                last = self.pe.step(issue, rdy + (bank.free if u == 0 else []) + needed(ready, k0 + kn - 1))
                if m == 0:
                    self.prepare_ahead()
                self.flush()
                if u == len(halves) - 1:
                    bank.free = evac(m, bank.buf[0:feat, 0:ntok], last)
                yield
            slot.free = [last]

    def put_split(self, dst, at, src, after, scale=1.0):
        hi, lo = dst.hi[at], dst.lo[at]
        a = self.act.step(lambda e: e.activation(hi, src, ACT.Identity, scale=scale), after)
        b = self.dve.step(lambda e: e.scalar_tensor_tensor(lo, src, scale, hi.bitcast(F32), ALU.mult, ALU.subtract), [a])
        return [a, b]

    def some_banks(self, n):
        self.bank_turn += n
        return [self.banks[(self.bank_turn - n + i) % 8] for i in range(n)]

    def to_both(self, halves, src, banks, evac, ready=(), m_tiles=4, feat=P):
        for u, (uname, k0, kn) in enumerate(halves):
            w, slot, rdy = self.take(uname)
            for m in range(m_tiles):
                for c, n in ((0, SEQ), (1, CTX)):
                    bank = banks[2 * m + c]

                    def issue(e):
                        for k in range(kn):
                            self.mm3(e, bank.buf[0:feat, 0:n],
                                     (w.hi[:, k, m * feat:(m + 1) * feat], w.lo[:, k, m * feat:(m + 1) * feat]),
                                     (src[c].hi[:, k0 + k, 0:n], src[c].lo[:, k0 + k, 0:n]),
                                     u == 0 and k == 0, u == len(halves) - 1 and k == kn - 1)
                    last = self.pe.step(issue, rdy + (bank.free if u == 0 else []) + needed(ready, k0 + kn - 1))
                    if m == c == 0:
                        self.prepare_ahead()
                    if u == len(halves) - 1:
                        bank.free = evac(m, c, bank.buf[0:feat, 0:n], last)
                    yield
            slot.free = [last]

    def square(self, i, src, after):
        self.act.step(lambda e: e.activation(self.junk[:, 0:src.shape[1]], src, ACT.Square, accum_out=self.tiny[:, i:i + 1]), after)

    def squares(self, srcs, after, at=0):
        for i, s in enumerate(srcs):
            if i % 2:
                self.dve.step(lambda e: e.tensor_tensor_reduce(out=self.junk2[:, 0:s.shape[1]], in0=s, in1=s, scale=1.0, scalar=0.0,
                                                               op0=ALU.mult, op1=ALU.add, accum_out=self.tiny[:, at + i:at + i + 1]), after)
            else:
                self.square(at + i, s, after)

    def rstd(self, n, width, at=0):
        r = self.tiny[:, at:at + n]
        a = self.dve.step(lambda e: e.tensor_scalar(r, r, 1.0 / width, EPS, ALU.mult, ALU.add), [self.act.now()])
        b = self.act.step(lambda e: e.activation(r, r, ACT.Sqrt), [a])
        return self.dve.step(lambda e: e.reciprocal(r, r), [b])

    def norm_features(self, tiles, width, dst, gain, bias=None):
        made = {}
        for _ in self.norm_stream(tiles, width, dst, gain, made, bias):
            pass
        return made

    def norm_stream(self, tiles, width, dst, gain, made, bias=None, at=0, banks=None):
        nt, kt, banks = len(tiles), width // P, banks or self.banks
        r = self.tiny[:, at:at + nt]
        ready = self.rstd(nt, width, at)
        for i in range(nt):
            last = self.dve.step(lambda e, i=i: e.tensor_scalar(self.diag[:, i, :], self.ident, r[:, i:i + 1], None, ALU.mult), [ready])
        yield
        groups = []
        for lo in range(0, nt, 4):
            groups.append(list(range(lo, min(lo + 4, nt))))
        splits = []
        n = 0
        for k in range(kt):
            for g in groups:
                bank = banks[n % len(banks)]
                n += 1

                def issue(e, k=k, g=g, bank=bank):
                    for j, i in enumerate(g):
                        l = e.matmul(bank.buf[:, j * P:(j + 1) * P], tiles[i][:, k * P:(k + 1) * P],
                                     self.diag[:, i, :], start=True, stop=True)
                    return l
                t = self.pe.step(issue, [last] + bank.free)
                src = bank.buf[:, 0:len(g) * P]
                d, tok = dst[g[0]]
                at = (slice(None), k, slice(tok, tok + len(g) * P))
                if bias is None:
                    bank.free = self.put_split(d, at, src, [t], gain[:, k:k + 1])
                else:
                    cond = 0 if g[0] < XT else 1
                    tmp = self.nrm_tmp.take()
                    full = tmp.buf[:, 0:len(g) * P]
                    hi, lo = d.hi[at], d.lo[at]
                    gk, bk = gain[:, cond, k:k + 1], bias[:, cond, k:k + 1]
                    if k % 2:
                        a = self.act.step(lambda e: e.activation(full, src, ACT.Identity, scale=gk, bias=bk), [t] + tmp.free)
                    else:
                        a = self.dve.step(lambda e: e.tensor_scalar(full, src, gk, bk, ALU.mult, ALU.add), [t] + tmp.free)
                    bank.free = [a]

                    def split(hi=hi, lo=lo, full=full, a=a, tmp=tmp, k=k):
                        b = self.act.step(lambda e: e.activation(hi, full, ACT.Copy), [a])
                        tmp.free = [self.dve.step(lambda e: e.tensor_tensor(lo, full, hi.bitcast(F32), ALU.subtract), [b])]
                        made[k] = [self.act.now(), self.dve.now()]
                    splits.append(split)
                    if len(splits) > 1:
                        splits.pop(0)()
            if bias is None:
                made[k] = [self.act.now(), self.dve.now()]
            yield
        for split in splits:
            split()

    def load_rows(self, slab, rows):
        n, loads = 0, []
        for src in rows:
            r = src.shape[0]
            loads.append(self.small.load(slab[n:n + r, :], src))
            n += r
        return slab, n, loads

    def to_columns(self, loaded, at):
        slab, n, loads = loaded
        bank = self.banks[7]
        t = self.pe.step(lambda e: e.transpose(bank.buf[:, 0:n], slab[0:n, :], self.ident[0:n, 0:n]),
                         loads + [self.cst_ready] + bank.free)
        c = self.dve.step(lambda e: e.tensor_copy(self.cols[:, at:at + n], bank.buf[:, 0:n]), [t])
        bank.free = [c]
        return at + n

    def rows(self, name, *index):
        a = self.ins[name]
        for i in index:
            a = a[i]
        if len(a.shape) == 2:
            a = a.rearrange("a b -> (a b)")
        return a.rearrange("(r c) -> r c", c=P)

    def setup(self):
        self.cst_ready = self.sp.load(self.cst[:, 0:C_ATT], self.ins["constants"][:, 0:C_ATT])
        self.x_ready = [self.sp.load(self.x[:, t, :], self.ins["x"][0, t * P:(t + 1) * P, :]) for t in range(XT)]
        cst_rest = self.sp.load(self.cst[:, C_ATT:], self.ins["constants"][:, C_ATT:])
        base, self.at = self.at, self.high_end
        slab = [self.place("row_slab0", [P, P])]
        self.mod_gain = [self.place(f"mod_gain{i}", [P, 2, 8]) for i in range(DEPTH)]
        self.mod_shift = [self.place(f"mod_shift{i}", [P, 2, 8]) for i in range(DEPTH)]
        self.cond = self.place("silu_cond", [P, KT, 2])
        self.mod_cols = self.place("mod_cols", [P, 2, 16])
        self.rope_work = self.place("rope_work", [P, 6, XT, 8])
        pos_i = self.place("positions", [P, XT], I32)
        self.pos_f = self.place("positions_f", [P, XT])
        self.at = base + 2 * DM * 4
        slab += [self.place(f"row_slab{i}", [P, P]) for i in (1, 2)]
        self.at = base
        D, c = self.rows, {"norm_mix": 0, "norm_mlp": 16}
        self.c = c
        norm_rows = self.load_rows(slab[0], [D("norm_mix_w", slice(0, DEPTH)), D("norm_mlp_w", slice(0, DEPTH))])
        self.positions = (pos_i, self.small.load(pos_i[:, :], self.ins["positions"][0].rearrange("(t p) -> p t", p=P), strided=True), cst_rest)
        self.more_rows = [
            self.load_rows(slab[1], [D("gla_b_gf_2", 0), D("gla_b_gb_2", 0), D("b_in", 0, slice(COL_MQ, COL_MV)), D("b_in", 1, slice(COL_MQ, COL_MV)),
                                     self.ins["conv_w"].rearrange("l j (r c) -> (l j r) c", c=P), D("conv_b", slice(0, DEPTH))]),
            self.load_rows(slab[2], [D("b_in", 0, slice(COL_GA, D_IN)), D("b_in", 1, slice(COL_GA, D_IN)), D("norm_g_2", slice(0, DEPTH)),
                                     D("mla_q_norm_2", 0), D("mla_kv_norm_2", 0), D("c_2", 0), D("c_ctx_2"), D("gla_o_norm_2", 0)])]
        self.to_columns(norm_rows, 0)

    def setup_rest(self):
        c, work, pos_f = self.c, self.rope_work, self.pos_f
        pos_i, pl, cst_rest = self.positions
        at = 32
        c["gla_b"], c["b_mqk"], c["conv_w"], c["conv_b"] = at, at + 8, at + 24, at + 88
        at = self.to_columns(self.more_rows[0], at)
        c["b_gate"], c["norm_g"], c["q_norm"], c["kv_norm"], c["cond"] = at, at + 32, at + 48, at + 51, at + 53
        at = self.to_columns(self.more_rows[1], at)
        c["o_norm"] = c["cond"] + 16
        assert at == c["o_norm"] + GDV // P and at <= 256
        f = self.dve.step(lambda e: e.tensor_copy(pos_f[:, :], pos_i[:, :]), [pl])
        ang, turn, k, r = (work[:, i, :, :] for i in range(4))
        inv = self.cst[:, C_INV:C_INV + 8]
        for t in range(XT):
            self.dve.step(lambda e, t=t: e.tensor_scalar(ang[:, t, :], inv, pos_f[:, t:t + 1], None, ALU.mult), [f, cst_rest])
        magic = 1.5 * 2.0 ** 23
        c1, c2 = 6.28125, float(np.float32(np.round((2 * np.pi - 6.28125) * 2 ** 22) / 2 ** 22))
        c3 = float(2 * np.pi - c1 - c2)
        for i, quarter in enumerate((0.25, 0.0)):
            self.dve.step(lambda e, quarter=quarter: e.tensor_scalar(turn, ang, 1 / (2 * np.pi), quarter, ALU.mult, ALU.add))
            self.dve.step(lambda e: e.tensor_scalar(k, turn, magic, None, ALU.add))
            self.dve.step(lambda e: e.tensor_scalar(k, k, -magic, None, ALU.add))
            self.dve.step(lambda e: e.scalar_tensor_tensor(r, k, -c1, ang, ALU.mult, ALU.add))
            self.dve.step(lambda e: e.scalar_tensor_tensor(r, k, -c2, r, ALU.mult, ALU.add))
            self.dve.step(lambda e: e.scalar_tensor_tensor(r, k, -c3, r, ALU.mult, ALU.add))
            self.dve.step(lambda e, quarter=quarter: e.tensor_scalar(r, r, quarter * 2 * np.pi, float(np.float32(3.1415925)), ALU.add, ALU.min))
            d = self.dve.step(lambda e: e.tensor_scalar(r, r, float(-np.float32(3.1415925)), None, ALU.max))
            s = self.act.step(lambda e, i=i: e.activation(work[:, 4 + i, :, :], r, ACT.Sin), [d])
            self.dve.pending = [s]
        cos, sin = work[:, 4, :, :], work[:, 5, :, :]
        for o in (0, 8):
            self.dve.step(lambda e, o=o: e.tensor_copy(self.rope[:, :, o:o + 8], cos), [s])
        self.dve.step(lambda e: e.tensor_scalar(self.rope[:, :, 16:24], sin, -1.0, None, ALU.mult))
        self.dve.step(lambda e: e.tensor_copy(self.rope[:, :, 24:32], sin))

    def layer(self, l):
        c, cols, cst, ins = self.c, self.cols, self.cst, self.ins
        pe, dve, act, pool = self.pe, self.dve, self.act, self.pool
        fence = self.fence()
        base = self.at = self.hc_at
        mqk = self.place("mlstm_qk", [P, 8, SEQ])
        mv = self.place("mlstm_v", [P, XT, MH, MHD + 1])
        mo = self.place("mlstm_out_gate", [P, XT, 512])
        qk_end = self.at
        y_att = Split(self.place("y_att_hi", [P, 4, SEQ], F32R), self.place("y_att_lo", [P, 4, SEQ], F32R))
        gates = self.place("gates", [P, 8, 16])
        mrow = self.place("running_max_row", [MH, SEQ])
        zrow = self.place("zero_row", [MH, SEQ])
        self.rope_tmp = self.place("rope_swapped", [P, P])
        att_at = self.at
        qT = self.place("att_qT", [P, 4, SEQ])
        kT = self.place("att_kT", [P, 4, SEQ])
        av = self.place("att_v", [P, XT, 512])
        conv_in = Ring([self.place(f"conv_in{i}", [P, CONV - 1 + SEQ]) for i in range(2)])
        conv_term = self.place("conv_term", [P, SEQ])
        tok = Ring([self.place(f"token_tile{i}", [P, 512]) for i in range(2)])
        bias_row = Ring([self.place(f"bias_row{i}", [P, 512]) for i in range(1)])
        tmp_at = self.at
        prob = Ring([self.place(f"prob{i}", [P, 512]) for i in range(2)])
        probT = Ring([self.place(f"probT{i}", [P, 512]) for i in range(2)])
        y_tok = Ring([self.place(f"y_tok{i}", [P, 512]) for i in range(1)])
        self.junk = self.nc.alloc_sbuf_tensor_at(f"junk_l{l}", [P, DM], F32, offset=(tmp_at + 31) // 32 * 32)
        self.diag = self.nc.alloc_sbuf_tensor_at(f"diag_l{l}", [P, 4, P], F32, offset=(tmp_at + 31) // 32 * 32 + 4096)
        self.junk2 = self.nc.alloc_sbuf_tensor_at(f"junk2_l{l}", [P, DM], F32, offset=base)
        tiny = self.tiny

        if l == 0:
            self.squares([self.x[:, t, :] for t in range(XT)], self.x_ready)
        h_ready = self.norm_features([self.x[:, t, :] for t in range(XT)], DM, [(self.hx, t * P) for t in range(XT)],
                                     self.cols[:, c["norm_mix"] + 8 * l:c["norm_mix"] + 8 * l + 8])
        if l == 0:
            self.prepare()
            self.setup_rest()
        marks_of_phase = self.fence()
        pe.pending = []
        for s in conv_in.slots:
            s.free = [pool.step(lambda e, s=s: e.memset(s.buf[:, 0:CONV - 1], 0.0))]
        ones = [pool.step(lambda e: e.memset(mv[:, :, :, MHD:MHD + 1], 1.0)), pool.step(lambda e: e.memset(zrow[:, :], 0.0))]
        X = [(self.hx, t) for t in range(XT)]
        main, side = self.banks[0:4], self.banks[4:8]

        def bias_load(lo, n):
            b = bias_row.take()
            t = self.small.load(b.buf[:, 0:n], ins["b_in"][l, lo:lo + n].partition_broadcast(P), after=b.free + marks_of_phase)
            return b, t

        def u(name):
            return [(f"{name}.{l}.{i}", 4 * i, 4) for i in range(2)]

        done = {}
        for name, lo, dst in (("aq", COL_AQ, qT), ("ak", COL_AK, kT)):
            b, bt = bias_load(lo, 512)

            def evac(t, bank, made, dst=dst, b=b, bt=bt, name=name):
                z = tok.take()
                first = dve.step(lambda e: e.tensor_tensor(z.buf[:, :], bank, b.buf[:, :], ALU.add), [made, bt] + z.free)
                zh = z.buf[:, :].rearrange("p (h d) -> p h d", h=AH)
                swap = self.rope_tmp[:, 0:128].rearrange("p (h d) -> p h d", h=AH)
                table = self.rope[:, t, :]
                cc = table[:, 0:16].unsqueeze(1).broadcast_to([P, AH, 16])
                dve.step(lambda e: e.tensor_tensor(swap[:, :, 0:8], zh[:, :, 8:16], table[:, 16:24].unsqueeze(1).broadcast_to([P, AH, 8]), ALU.mult))
                dve.step(lambda e: e.tensor_tensor(swap[:, :, 8:16], zh[:, :, 0:8], table[:, 24:32].unsqueeze(1).broadcast_to([P, AH, 8]), ALU.mult))
                dve.step(lambda e: e.tensor_tensor(zh[:, :, 0:16], zh[:, :, 0:16], cc, ALU.mult))
                r = dve.step(lambda e: e.tensor_tensor(zh[:, :, 0:16], zh[:, :, 0:16], swap, ALU.add))
                sb = side[t]

                def turned():
                    def tr(e):
                        for g in range(4):
                            e.transpose(sb.buf[:, g * P:(g + 1) * P], z.buf[:, g * P:(g + 1) * P], self.ident)
                    tt = pe.step(tr, [r] + sb.free)
                    o = act.step(lambda e: e.activation(dst[:, :, t * P:(t + 1) * P], sb.buf[:, :].rearrange("p (g t) -> p g t", g=4), ACT.Copy), [tt])
                    sb.free, z.free = [o], [tt]
                    done[name, t] = o
                self.defer(turned)
                b.free = [first]
                return [first]
            for _ in self.to_tokens(u(name), X, 512, main, evac, h_ready):
                pass
        b, bt = bias_load(COL_AV, 512)

        def evac_v(t, bank, made):
            a = dve.step(lambda e: e.tensor_tensor(av[:, t, :], bank, b.buf[:, :], ALU.add), [made, bt])
            b.free = [a]
            done["av", t] = a
            return [a]
        for _ in self.to_tokens(u("av"), X, 512, main, evac_v, h_ready):
            pass

        def mlstm_inputs():
            for g in range(2):
                for _ in self.to_features(u(f"mqk{g}"), self.hx, SEQ, main, lambda m, bank, made, g=g: conv(g * 4 + m, bank, made)):
                    yield
            b, bt = bias_load(COL_MV, 512)

            def evac_mv(t, bank, made):
                a = dve.step(lambda e: e.tensor_tensor(mv[:, t, :, 0:MHD], bank.rearrange("p (h d) -> p h d", h=MH),
                                                       b.buf[:, :].rearrange("p (h d) -> p h d", h=MH), ALU.add), [made, bt] + ones)
                b.free = [a]
                done["mv", t] = a
                return [a]
            for _ in self.to_tokens(u("mv"), X, 512, main, evac_mv):
                yield
            b2, bt2 = bias_load(COL_MO, 512)

            def evac_mo(t, bank, made):
                a = dve.step(lambda e: e.tensor_tensor(mo[:, t, :], bank, b2.buf[:, :], ALU.add), [made, bt2])
                b2.free = [a]
                done["mo", t] = a
                return [a]
            for _ in self.to_tokens(u("mo"), X, 512, main, evac_mo):
                yield
            b3, bt3 = bias_load(COL_MI, 8)

            def evac_if(m, bank, made):
                z = tok.take()
                a = act.step(lambda e: e.activation(z.buf[0:2 * MH, :], bank, ACT.Copy), [made] + z.free)
                done["if raw"] = (z, a)
                return [a]
            for _ in self.to_features([(f"mif.{l}", 0, 8)], self.hx, SEQ, main, evac_if, (), 1, 2 * MH):
                yield
            (z, a), b = done["if raw"], main[1]

            def tr(e):
                for t in range(XT):
                    e.transpose(b.buf[:, 2 * MH * t:2 * MH * (t + 1)], z.buf[0:2 * MH, t * P:(t + 1) * P], self.ident[0:2 * MH, 0:2 * MH])
            t = pe.step(tr, [a] + b.free)
            bias = b3.buf[:, 0:2 * MH].rearrange("p (g h) -> p g h", g=2).unsqueeze(1).broadcast_to([P, XT, 2, MH])
            done["if"] = dve.step(lambda e: e.tensor_tensor(gates[:, 0:2, :].rearrange("p g (t h) -> p t g h", t=XT),
                                                            b.buf[:, 0:2 * MH * XT].rearrange("p (t g h) -> p t g h", t=XT, g=2), bias, ALU.add), [t, bt3])
            z.free, b.free, b3.free = [t], [done["if"]], [done["if"]]
            yield

        def conv(m, bank, made):
            s = conv_in.take()
            bcol = cols[:, c["b_mqk"] + 8 * l + m:c["b_mqk"] + 8 * l + m + 1]
            a = act.step(lambda e: e.activation(s.buf[:, CONV - 1:], bank, ACT.Identity, bias=bcol), [made] + s.free)
            w = lambda j: cols[:, c["conv_w"] + (l * CONV + j) * 8 + m:c["conv_w"] + (l * CONV + j) * 8 + m + 1]
            cb = cols[:, c["conv_b"] + 8 * l + m:c["conv_b"] + 8 * l + m + 1]
            acc = mqk[:, m, :]
            first = act.step(lambda e: e.activation(acc, s.buf[:, 0:SEQ], ACT.Identity, bias=cb, scale=w(0)))
            pool.step(lambda e: e.tensor_scalar(conv_term[:, :], s.buf[:, 1:1 + SEQ], w(1), None, ALU.mult), [a])
            d = pool.step(lambda e: e.tensor_tensor(acc, acc, conv_term[:, :], ALU.add), [first])

            def last_taps():
                for j in range(2, CONV):
                    done["conv"] = dve.step(lambda e: e.scalar_tensor_tensor(acc, s.buf[:, j:j + SEQ], w(j), acc, ALU.mult, ALU.add), [d])
                s.free = [done["conv"]]
            self.defer(last_taps)
            return [a]

        def attention():
            s_banks, t_bank, o_bank = Ring(side[0:2]), side[2], side[3]
            s_banks.slots = side[0:2]
            units = [(i, h) for i in range(XT) for h in range(AH)]
            state = {}

            def scores(i, h):
                n = (i + 1) * P
                bank = s_banks.take()
                hp = (h % 2) * AHD
                t = pe.step(lambda e: e.matmul(bank.buf[:, 0:n], qT[hp:hp + AHD, h // 2, i * P:(i + 1) * P], kT[hp:hp + AHD, h // 2, 0:n],
                                               start=True, stop=True), [done["aq", i], done["ak", i]] + bank.free)
                p = prob.take()
                mn, ls = tiny[:, 64 + h:65 + h], tiny[:, 72 + h:73 + h]
                d = dve.step(lambda e: e.tensor_tensor_reduce(out=p.buf[:, 0:n], in0=bank.buf[:, 0:n], in1=cst[:, C_ATT + 512 - n:C_ATT + 512],
                                                              scale=-AHD ** -0.5, scalar=3e38, op0=ALU.add, op1=ALU.min, accum_out=mn), [t] + p.free)
                bank.free = [d]
                a = act.step(lambda e: e.activation(p.buf[:, 0:n], p.buf[:, 0:n], ACT.Exp, bias=mn, scale=-1.0, accum_out=ls), [d])
                state[i, h] = (p, n, ls, a)

            def turn(i, h):
                p, n, ls, a = state[i, h]

                def tr(e):
                    for j in range(i + 1):
                        last = e.transpose(t_bank.buf[:, j * P:(j + 1) * P], p.buf[:, j * P:(j + 1) * P], self.ident)
                    return last
                t = pe.step(tr, [a] + t_bank.free)
                p.free = [t]
                q = probT.take()
                if h % 2:
                    cp = dve.step(lambda e: e.tensor_copy(q.buf[:, 0:n], t_bank.buf[:, 0:n]), [t] + q.free)
                else:
                    cp = act.step(lambda e: e.activation(q.buf[:, 0:n], t_bank.buf[:, 0:n], ACT.Copy), [t] + q.free)
                t_bank.free = [cp]
                state[i, h] = (q, ls, cp, a)

            def values(i, h):
                q, ls, cp, a = state[i, h]

                def pv(e):
                    for j in range(i + 1):
                        last = e.matmul(o_bank.buf[:, 0:AHD], q.buf[:, j * P:(j + 1) * P], av[:, j, h * AHD:(h + 1) * AHD],
                                        start=(j == 0), stop=(j == i))
                    return last
                t = pe.step(pv, [cp, done["av", i]] + o_bank.free)
                q.free = [t]
                if h == 0:
                    state["y", i] = y_tok.take()
                y = state["y", i]
                dve.step(lambda e: e.reciprocal(ls, ls), [a])
                d = dve.step(lambda e: e.tensor_scalar(y.buf[:, h * AHD:(h + 1) * AHD], o_bank.buf[:, 0:AHD], ls, None, ALU.mult), [t] + y.free)
                o_bank.free = [d]
                if h == AH - 1:
                    def tr(e):
                        for g in range(4):
                            last = e.transpose(t_bank.buf[:, g * P:(g + 1) * P], y.buf[:, g * P:(g + 1) * P], self.ident)
                        return last
                    tt = pe.step(tr, [d] + t_bank.free)
                    y.free = [tt]
                    t_bank.free = self.put_split(y_att, (slice(None), slice(0, 4), slice(i * P, (i + 1) * P)),
                                                 t_bank.buf[:, :].rearrange("p (g t) -> p g t", g=4), [tt])
                    done["y", i] = t_bank.free
            for s in range(len(units) + 2):
                if s < len(units):
                    scores(*units[s])
                    yield
                if 1 <= s <= len(units):
                    turn(*units[s - 1])
                    yield
                if s >= 2:
                    values(*units[s - 2])
                    yield

        def mlstm_gates():
            G = lambda j: gates[:, j, :]
            gr = [done["if"]]
            act.step(lambda e: e.activation(G(2), G(1), ACT.Abs), gr)
            act.step(lambda e: e.activation(G(2), G(2), ACT.Exp, scale=-1.0))
            a = act.step(lambda e: e.activation(G(2), G(2), ACT.Ln, bias=1.0))
            d = dve.step(lambda e: e.scalar_tensor_tensor(G(3), G(1), 0.0, G(2), ALU.min, ALU.subtract), [a])
            dve.step(lambda e: e.memset(gates[:, 4, 0:4], 0.0))
            for t in range(1, XT):
                d = dve.step(lambda e, t=t: e.tensor_tensor(gates[:, 4, 4 * t:4 * t + 4], gates[:, 4, 4 * t - 4:4 * t], gates[:, 3, 4 * t - 4:4 * t], ALU.add))
            bk = main[2]

            def cum(e):
                e.matmul(bk.buf[:, 0:16], cst[:, C_UP:C_UP + P], G(3), start=True, stop=False)
                return e.matmul(bk.buf[:, 0:16], cst[:, C_ONES:C_ONES + P], G(4), start=False, stop=True)
            t = pe.step(cum, [d] + bk.free)
            yield
            dve.step(lambda e: e.tensor_copy(G(5), bk.buf[:, 0:16]), [t])
            d = dve.step(lambda e: e.tensor_tensor(G(6), G(0), G(5), ALU.subtract))
            bk.free = [d]
            bk2 = main[3]

            def rows_(e):
                for t in range(XT):
                    last = e.transpose(bk2.buf[0:MH, t * P:(t + 1) * P], gates[:, 6, 4 * t:4 * t + 4], self.ident)
                return last
            t = pe.step(rows_, [d] + bk2.free)
            yield
            m_row = dve.step(lambda e: e.tensor_tensor_scan(mrow[:, :], bk2.buf[0:MH, :], zrow[:, :], 0.0, ALU.max, ALU.max), [t])
            bk2.free = [m_row]

            def back(e):
                for t in range(XT):
                    last = e.transpose(bk.buf[:, 4 * t:4 * t + 4], mrow[:, t * P:(t + 1) * P], self.ident[0:MH, 0:MH])
                return last
            t = pe.step(back, [m_row] + bk.free)
            yield
            d = dve.step(lambda e: e.tensor_tensor(G(7), bk.buf[:, 0:16], G(5), ALU.add), [t])
            bk.free = [d]
            floor_ready = act.step(lambda e: e.activation(G(7), G(7), ACT.Exp, scale=-1.0), [d])
            done["m_row"], done["floor"] = m_row, floor_ready
            yield

        def filler():
            yield from mlstm_inputs()
            self.flush()
            for part in (slice(0, 4), slice(4, 8)):
                silu = act.step(lambda e: e.activation(mqk[:, part, :], mqk[:, part, :], ACT.Silu), [done["conv"]])
                for m in range(8)[part]:
                    done["mqk", m] = silu
            yield from woven((self.modulation(l, tok), 2), (mlstm_gates(), 1))
        interleave((attention(), 2), (filler(), 1))

        self.fence()
        self.at = att_at
        mix_a = self.place("mixed_att", [P, 8, SEQ])
        y_m = Split(self.place("y_mlstm_hi", [P, 4, SEQ], F32R), self.place("y_mlstm_lo", [P, 4, SEQ], F32R))
        E = Ring([self.place(f"decay{i}", [P, 512]) for i in range(2)])
        pm_at = (self.at + 31) // 32 * 32
        Pm = Ring([self.place("mlstm_prob", [P, 1280])])
        p_at = (0, 512, 896, 1152)
        nrow = self.place("mlstm_norm_row", [P, 512])
        bl = self.small.load(nrow[:, 0:512], ins["mlstm_norm_w"][l, :].partition_broadcast(P), after=self.fence())
        pe.pending = []

        def mlstm():
            G = lambda j: gates[:, j, :]
            m_row, floor_ready = done["m_row"], done["floor"]
            sg = act.step(lambda e: e.activation(mo[:, :, :], mo[:, :, :], ACT.Sigmoid), [done["mo", t] for t in range(XT)])
            for t in range(XT):
                gated_gain = pool.step(lambda e, t=t: e.tensor_tensor(mo[:, t, :], mo[:, t, :], nrow[:, 0:512], ALU.mult), [sg, bl])
            m_bank, s_bank, o_banks = side[0], side[1], side[2:4]
            rs = self.tiny[:, 100:100 + XT * MH]
            for h in range(MH):
                t = pe.step(lambda e, h=h: e.matmul(m_bank.buf[:, :], self.negsel[:, h, :], mrow[:, :], start=True, stop=True), [m_row] + m_bank.free)
                pm = Pm.take()
                last = None
                yield
                for j in range(XT):
                    n = (XT - j) * P
                    w = E.take()
                    d = dve.step(lambda e, j=j, n=n, w=w, h=h: e.tensor_scalar(w.buf[:, 0:n], m_bank.buf[:, j * P:], gates[:, 6, 4 * j + h:4 * j + h + 1], None, ALU.add), [t] + w.free)
                    d = dve.step(lambda e, w=w: e.tensor_tensor(w.buf[:, 0:P], w.buf[:, 0:P], cst[:, C_TRI:C_TRI + P], ALU.add))
                    a = act.step(lambda e, n=n, w=w: e.activation(w.buf[:, 0:n], w.buf[:, 0:n], ACT.Exp), [d])
                    s = pe.step(lambda e, j=j, n=n, h=h: e.matmul(s_bank.buf[:, 0:n], mqk[:, 4 + h, j * P:(j + 1) * P], mqk[:, h, j * P:], start=True, stop=True),
                                [done["mqk", h], done["mqk", 4 + h]] + s_bank.free)
                    last = dve.step(lambda e, j=j, n=n, w=w, pm=pm: e.scalar_tensor_tensor(pm.buf[:, p_at[j]:p_at[j] + n], s_bank.buf[:, 0:n], MHD ** -0.5, w.buf[:, 0:n], ALU.mult, ALU.mult),
                                    [s, a] + pm.free)
                    s_bank.free, w.free = [last], [last]
                    if j == XT - 1:
                        m_bank.free = [d]
                    yield
                for half in range(2):
                    ob = o_banks[half]

                    def pv(e):
                        for ii in range(2):
                            i = 2 * half + ii
                            for j in range(i + 1):
                                e.matmul(ob.buf[:, ii * 129:ii * 129 + 129], pm.buf[:, p_at[j] + (i - j) * P:p_at[j] + (i - j + 1) * P],
                                         mv[:, j, h, :], start=(j == 0), stop=(j == i))
                    t2 = pe.step(pv, [last] + [done["mv", j] for j in range(XT)] + ob.free)
                pm.free = [t2]
                yield
                for half in range(2):
                    ob = o_banks[half]
                    o2 = ob.buf[:, 0:258].rearrange("p (i d) -> p i d", i=2)
                    den = tiny[:, 96:98]
                    fl = gates[:, 7, :].rearrange("p (t h) -> p t h", h=MH)[:, 2 * half:2 * half + 2, h]
                    dve.step(lambda e: e.tensor_scalar(den, o2[:, :, MHD], -1.0, None, ALU.mult), [t2])
                    dve.step(lambda e: e.tensor_tensor(den, o2[:, :, MHD], den, ALU.max))
                    dve.step(lambda e: e.tensor_tensor(den, den, fl, ALU.max), [floor_ready])
                    dve.step(lambda e: e.reciprocal(den, den))
                    for ii in range(2):
                        i = 2 * half + ii
                        hv = mv[:, i, h, 0:MHD]
                        dve.step(lambda e: e.tensor_scalar(hv, o2[:, ii, 0:MHD], den[:, ii:ii + 1], None, ALU.mult))
                        d = dve.step(lambda e: e.tensor_tensor_reduce(out=ob.buf[:, 384:384 + MHD], in0=hv, in1=hv, scale=1.0, scalar=0.0, op0=ALU.mult,
                                                                      op1=ALU.add, accum_out=rs[:, MH * i + h:MH * i + h + 1]))
                    ob.free = [d]
                    yield
            done["hm"] = d

            d = dve.step(lambda e: e.tensor_scalar(rs, rs, 1.0 / MHD, EPS, ALU.mult, ALU.add))
            a = act.step(lambda e: e.activation(rs, rs, ACT.Sqrt), [d])
            dve.step(lambda e: e.reciprocal(rs, rs), [a])
            for t in range(XT):
                for h in range(MH):
                    sl = slice(h * MHD, (h + 1) * MHD)
                    d = dve.step(lambda e, t=t, h=h, sl=sl: e.scalar_tensor_tensor(mv[:, t, h, 0:MHD], mv[:, t, h, 0:MHD], rs[:, 4 * t + h:4 * t + h + 1], mo[:, t, sl], ALU.mult, ALU.mult), [gated_gain])
                sb = side[t]

                def tr(e, t=t, sb=sb):
                    for g in range(4):
                        last = e.transpose(sb.buf[:, g * P:(g + 1) * P], mv[:, t, g, 0:MHD], self.ident)
                    return last
                yield
                tt = pe.step(tr, [d] + sb.free)
                sb.free = self.put_split(y_m, (slice(None), slice(0, 4), slice(t * P, (t + 1) * P)),
                                         sb.buf[:, :].rearrange("p (g t) -> p g t", g=4), [tt])
                y_ready = sb.free
            done["y_m"] = y_ready

        def att_projection():
            for g in range(2):
                ga = {}

                def evac_g(m, bank, made, g=g):
                    bcol = cols[:, c["b_gate"] + 16 * l + 4 * g + m:c["b_gate"] + 16 * l + 4 * g + m + 1]
                    a = dve.step(lambda e: e.tensor_scalar(mix_a[:, 4 * g + m, :], bank, bcol, None, ALU.add), [made])
                    return [a]
                for _ in self.to_features(u(f"ga{g}"), self.hx, SEQ, main, evac_g):
                    yield
                a = act.step(lambda e, g=g: e.activation(mix_a[:, 4 * g:4 * g + 4, :], mix_a[:, 4 * g:4 * g + 4, :], ACT.Sigmoid), [dve.now()])

                def evac_p(m, bank, made, g=g, a=a):
                    return [dve.step(lambda e: e.tensor_tensor(mix_a[:, 4 * g + m, :], bank, mix_a[:, 4 * g + m, :], ALU.mult), [made, a])]
                for _ in self.to_features([(f"pa{g}.{l}", 0, 4)], y_att, SEQ, main, evac_p, done["y", 3]):
                    yield
            read = [pe.now()]
            for g in range(2):
                def evac_b(m, bank, made):
                    bcol = cols[:, c["b_gate"] + 16 * l + 8 + 4 * g + m:c["b_gate"] + 16 * l + 8 + 4 * g + m + 1]
                    return [dve.step(lambda e: e.tensor_scalar(gbt[:, 4 * g + m, :], bank, bcol, None, ALU.add), [made] + read)]
                for _ in self.to_features(u(f"gb{g}"), self.hx, SEQ, main, evac_b):
                    yield
        here, self.at = self.at, qk_end
        gbt = self.place("gate_b", [P, 8, SEQ])
        self.at = here
        interleave((mlstm(), 1), (att_projection(), 1))

        self.fence()
        self.at = base
        mixed = Split(self.place("mixed_hi", [P, 8, SEQ], F32R), self.place("mixed_lo", [P, 8, SEQ], F32R))
        assert self.at <= qk_end
        sgb = [act.step(lambda e: e.activation(gbt[:, 4 * g:4 * g + 4, :], gbt[:, 4 * g:4 * g + 4, :], ACT.Sigmoid)) for g in range(2)]
        ready = {}
        for g in range(2):
            def evac_p(m, bank, made):
                k = 4 * g + m
                d0 = dve.step(lambda e: e.tensor_tensor(gbt[:, k, :], bank, gbt[:, k, :], ALU.mult), [made, sgb[k // 4]])
                d = dve.step(lambda e: e.tensor_tensor(gbt[:, k, :], gbt[:, k, :], mix_a[:, k, :], ALU.add))
                a = act.step(lambda e: e.activation(mixed.hi[:, k, :], gbt[:, k, :], ACT.Copy), [d])
                ready[k] = [a, dve.step(lambda e: e.tensor_tensor(mixed.lo[:, k, :], gbt[:, k, :], mixed.hi[:, k, :].bitcast(F32), ALU.subtract), [a])]
                return [d0]
            for _ in self.to_features([(f"pm{g}.{l}", 0, 4)], y_m, SEQ, self.banks[4 * g:4 * g + 4], evac_p):
                pass
        self.junk = self.nc.alloc_sbuf_tensor_at(f"out_junk_l{l}", [P, DM], F32, offset=pm_at)
        for g in range(2):
            def evac_o(t, bank, made, g=g):
                sl = slice(g * 512, (g + 1) * 512)
                d = dve.step(lambda e: e.tensor_tensor(self.x[:, t, sl], bank, self.x[:, t, sl], ALU.add), [made])
                if g == 1:
                    self.square(t, self.x[:, t, :], [d])
                return [d]
            for _ in self.to_tokens([(f"wo{g}.{l}.{i}", 4 * i, 4) for i in range(2)], [(mixed, t) for t in range(XT)], 512,
                                    self.banks[4 * g:4 * g + 4], evac_o, ready):
                pass

        mlp_marks = self.fence()
        self.at = base
        up = [Split(self.place(f"hidden_hi{i}", [P, 8, SEQ], F32R), self.place(f"hidden_lo{i}", [P, 8, SEQ], F32R)) for i in range(2)]
        relu = Ring([self.place(f"relu{i}", [P, SEQ]) for i in range(2)])
        sq = Ring([self.place(f"relu_sq{i}", [P, SEQ]) for i in range(2)])
        self.junk = self.place("mlp_junk", [P, DM])
        self.diag = self.place("mlp_diag", [P, 4, P])
        mlp_end = self.at
        h_ready = self.norm_features([self.x[:, t, :] for t in range(XT)], DM, [(self.hx, t * P) for t in range(XT)],
                                     self.cols[:, c["norm_mlp"] + 8 * l:c["norm_mlp"] + 8 * l + 8])
        up_free, up_ready = [[], []], [None, None]
        if l == DEPTH - 1:
            self.load_context(mlp_marks)
            assert mlp_end <= self.top

        def widen(q):
            U, free = up[q % 2], up_free[q % 2]
            for g in range(2):
                def evac_u(m, bank, made):
                    k = 4 * g + m
                    r, s = relu.take(), sq.take()
                    a = act.step(lambda e: e.activation(r.buf[:, :], bank, ACT.Relu), [made] + r.free)
                    b = act.step(lambda e: e.activation(U.hi[:, k, :], r.buf[:, :], ACT.Square), free)
                    dve.step(lambda e: e.tensor_tensor(s.buf[:, :], r.buf[:, :], r.buf[:, :], ALU.mult), [a] + s.free)
                    d = dve.step(lambda e: e.tensor_tensor(U.lo[:, k, :], s.buf[:, :], U.hi[:, k, :].bitcast(F32), ALU.subtract), [b] + free)
                    r.free, s.free = [b, d], [d]
                    return [a]
                for _ in self.to_features([(f"f1.{l}.{q}.{g}.{i}", 4 * i, 4) for i in range(2)], self.hx, SEQ, self.banks[0:4], evac_u, h_ready):
                    pass
            up_ready[q % 2] = [act.now(), dve.now()]

        def narrow(q):
            for g in range(2):
                def evac_d(t, bank, made):
                    sl = slice(g * 512, (g + 1) * 512)
                    d = dve.step(lambda e: e.tensor_tensor(self.x[:, t, sl], bank, self.x[:, t, sl], ALU.add), [made])
                    if q == 3 and g == 1:
                        self.square(t, self.x[:, t, :], [d])
                    return [d]
                for _ in self.to_tokens([(f"f2.{l}.{q}.{g}.{i}", 4 * i, 4) for i in range(2)], [(up[q % 2], t) for t in range(XT)], 512,
                                        self.banks[4:8], evac_d, up_ready[q % 2]):
                    pass
            up_free[q % 2] = [pe.now()]
        for q in range(5):
            if q < 4:
                widen(q)
            if q > 0:
                narrow(q - 1)

    def layer_plan(self, l):
        w = {n: self.ins[n][l] for n in ("w_in", "w_proj_att", "w_proj_mlstm", "w_out", "w_ff1", "w_ff2")}

        units = self.units
        plan = []
        for n, c0 in (("aq", COL_AQ), ("ak", COL_AK), ("av", COL_AV), ("mqk0", COL_MQ), ("mqk1", COL_MQ + 512), ("mv", COL_MV), ("mo", COL_MO)):
            plan += units(f"{n}.{l}", w["w_in"], c0)
        plan += units(f"mif.{l}", w["w_in"], COL_MI, 8, per=8)
        for g in range(6):
            plan += units(f"ada{l}.{g}", self.ins["ada_w_2"][l], 512 * g, raw=True)
        for g in range(2):
            plan += units(f"ga{g}.{l}", w["w_in"], COL_GA + 512 * g)
            plan += units(f"pa{g}.{l}", w["w_proj_att"], 512 * g, kn=4)
        for g in range(2):
            plan += units(f"gb{g}.{l}", w["w_in"], COL_GB + 512 * g)
        for g in range(2):
            plan += units(f"pm{g}.{l}", w["w_proj_mlstm"], 512 * g, kn=4)
        for g in range(2):
            plan += units(f"wo{g}.{l}", w["w_out"], 512 * g)
        for q in range(5):
            for g in range(2 * (q < 4)):
                plan += units(f"f1.{l}.{q}.{g}", w["w_ff1"], q * 1024 + g * 512)
            for g in range(2 * (q > 0)):
                plan += units(f"f2.{l}.{q - 1}.{g}", w["w_ff2"], g * 512, k0=(q - 1) * 8)
        return plan

    def load_context(self, marks):
        self.top = self.high_end - (CT + 1) * DM * 4
        base, self.at = self.at, self.top
        self.norm_row = self.place("between_gain_row", [P, DM])
        self.ctx_res = self.place("context_residual", [P, CT, DM])
        self.at = base
        self.ctx_ready = self.small.load(self.ctx_res[:, :, :], self.ins["ctx_2"][0].rearrange("(t p) d -> p t d", p=P), after=marks)
        self.row_ready = self.small.load(self.norm_row[:, :], self.ins["final_norm_w"].partition_broadcast(P), after=marks)

    def norm_between(self):
        self.fence()
        self.at = self.hc_at
        self.junk = self.place("between_junk", [P, DM])
        r = self.tiny[:, 0:XT]
        for t in range(CT):
            self.square(XT + t, self.ctx_res[:, t, :], [self.ctx_ready])
        ready = self.rstd(XT, DM)
        for t in range(XT):
            d = self.dve.step(lambda e: e.scalar_tensor_tensor(self.x[:, t, :], self.x[:, t, :], r[:, t:t + 1], self.norm_row[:, :], ALU.mult, ALU.mult), [ready, self.row_ready])
            self.square(t, self.x[:, t, :], [d])

    def modulation(self, i, rows):
        pe, dve, act, cols, c = self.pe, self.dve, self.act, self.cols, self.c
        cond, mod, gain, shift = self.cond, self.mod_cols, self.mod_gain[i], self.mod_shift[i]
        s = act.step(lambda e: e.activation(cond[:, :, :], cols[:, c["cond"]:c["cond"] + 16].rearrange("p (c k) -> p k c", c=2), ACT.Silu))
        for g in range(6):
            bank, b2 = self.banks[g % 2], self.banks[1 - g % 2]
            r, b = rows.take(), rows.take()
            rb, bb = r.buf[0:2, :], b.buf[0:2, :]
            bt = self.small.load(bb, self.ins["ada_b_2"][i, 512 * g:512 * g + 512].partition_broadcast(2), after=b.free)
            for u in range(2):
                w, slot, rdy = self.take(f"ada{i}.{g}.{u}")

                def issue(e):
                    for k in range(4):
                        e.matmul(bank.buf[0:2, :], cond[:, 4 * u + k, :], w[:, k, :], start=(u == 0 and k == 0), stop=(u == 1 and k == 3))
                t = pe.step(issue, rdy + [s] + (bank.free if u == 0 else []))
                self.raw_done(slot, t)
                self.prepare_ahead()
                yield
            d = dve.step(lambda e: e.tensor_tensor(rb, bank.buf[0:2, :], bb, ALU.add), [t, bt] + r.free)
            bank.free, b.free = [d], [d]
            if g < 4:
                yield

                def tr(e):
                    for m in range(4):
                        e.transpose(b2.buf[:, 2 * m:2 * m + 2], rb[:, m * P:(m + 1) * P], self.ident[0:2, 0:2])
                t = pe.step(tr, [d] + b2.free)
                d = dve.step(lambda e: e.tensor_copy(mod[:, :, 4 * g:4 * g + 4], b2.buf[:, 0:8].rearrange("p (m c) -> p c m", m=4)), [t])
                b2.free, r.free = [d], [t]
            else:
                r.free = [self.small.load(self.gate_rows[i][:, (g - 4) * 512:(g - 3) * 512], rb, after=[d])]
                self.gate_stored += r.free
        ng = cols[:, c["norm_g"] + 8 * i:c["norm_g"] + 8 * i + 8]
        dve.step(lambda e: e.tensor_copy(shift[:, :, :], mod[:, :, 0:8]))
        dve.step(lambda e: e.tensor_scalar(gain[:, :, :], mod[:, :, 8:16], 1.0, None, ALU.add))
        dve.step(lambda e: e.tensor_tensor(gain[:, :, :], gain[:, :, :], ng.unsqueeze(1).broadcast_to([P, 2, 8]), ALU.mult))

    def modulated_norm(self, i):
        self.diag = self.place("norm_diag", [P, XT + CT, P])
        self.nrm_tmp = Ring([self.place(f"norm_tmp{j}", [P, 512]) for j in range(4)])
        return self.norm_features(
            [self.x[:, t, :] for t in range(XT)] + [self.ctx_res[:, t, :] for t in range(CT)], DM,
            [(self.hx, t * P) for t in range(XT)] + [(self.hc, t * P) for t in range(CT)],
            self.mod_gain[i], self.mod_shift[i])

    def mla(self):
        pe, dve, act, c, cols, cst = self.pe, self.dve, self.act, self.c, self.cols, self.cst
        T = XT + CT
        marks = self.fence()
        self.at = self.hc_at
        self.hc = Split(self.place("hc_hi", [P, KT, CTX], F32R), self.place("hc_lo", [P, KT, CTX], F32R))
        self.after_hc = self.at
        gate = self.place("mla_gate", [P, T, DM])
        krot = self.place("mla_rope_key", [P, T, LROPE])
        self.rope_tmp = self.place("axial_swapped", [P, P])
        body = self.at
        ready = self.modulated_norm(0)
        self.fence()
        pe.pending = []
        self.at = body
        lat = self.place("mla_latents", [P, T, LAT])
        self.diag = self.place("latent_diag", [P, T, P])
        self.top += DM * 4
        assert self.at <= self.top - 2 * (QR + KVR) // P * 768 * 4
        self.at = self.top - 2 * (QR + KVR) // P * 768 * 4
        cq = Split(self.place("cq_hi", [P, 3, 768], F32R), self.place("cq_lo", [P, 3, 768], F32R))
        ckv = Split(self.place("ckv_hi", [P, 2, 768], F32R), self.place("ckv_lo", [P, 2, 768], F32R))
        srcs = [(self.hx, t) for t in range(XT)] + [(self.hc, t) for t in range(CT)]
        product = lambda n, w, banks, evac: self.to_tokens([(f"mla_{n}.{i}", 4 * i, 4) for i in range(2)], srcs, w, banks, evac, ready)
        lat_made = []
        for n, lo, w in (("l0", 0, 512), ("l1", 512, 160)):
            def evac(t, bank, made):
                lat_made.append(act.step(lambda e: e.activation(lat[:, t, lo:lo + w], bank, ACT.Copy), [made]))
                return [lat_made[-1]]
            for _ in product(n, w, self.some_banks(T), evac):
                pass
        cq_ready, ckv_ready = {}, {}

        def latent_norms():
            tiles = [[lat[:, t, lo:hi] for t in range(T)] for lo, hi in ((0, QR), (QR, QR + KVR))]
            b6, b7 = self.banks[6:8]
            self.junk, self.junk2 = b6.buf, b7.buf
            self.squares(tiles[0], [lat_made[-1]] + b6.free + b7.free)
            yield
            yield from self.norm_stream(tiles[0], QR, [(cq, t * P) for t in range(T)], cols[:, c["q_norm"]:c["q_norm"] + QR // P], cq_ready, banks=self.banks[6:8])
            self.squares(tiles[1], [pe.now()] + b6.free + b7.free, 8)
            dve.pending.append(pe.now())
            yield
            yield from self.norm_stream(tiles[1], KVR, [(ckv, t * P) for t in range(T)], cols[:, c["kv_norm"]:c["kv_norm"] + KVR // P], ckv_ready, None, 8, self.banks[6:8])
            r0 = QR + KVR
            for t in range(T):
                key = lat[:, t, r0:r0 + LROPE]
                if t < XT:
                    self.axial(key.unsqueeze(1), krot[:, t, :].unsqueeze(1), t, 1)
                else:
                    dve.step(lambda e: e.tensor_copy(krot[:, t, :], key))
                yield

        def gate_product():
            for n, lo in (("g0", 0), ("g1", 512)):
                yield from product(n, 512, self.banks[0:T], lambda t, bank, made: [act.step(lambda e: e.activation(gate[:, t, lo:lo + 512], bank, ACT.Silu), [made])])
        interleave((gate_product(), 1), (latent_norms(), 1))
        fence = self.fence()
        self.at = self.hx_at
        qT = self.place("mla_qT", [NOPE + LROPE, 4, 768])
        kT = self.place("mla_kT", [NOPE + LROPE, 4, 768])
        assert self.at <= self.hc_at
        self.at = self.hc_at
        prob = Ring([self.place(f"mla_prob{j}", [P, 768]) for j in range(2)])
        probT = Ring([self.place(f"mla_probT{j}", [P, 768]) for j in range(2)])
        assert self.at <= self.after_hc
        self.at = body
        v = self.place("mla_v", [P, T, 4, LV])
        tok = Ring([self.place(f"mla_token_tile{j}", [P, 4, NOPE + LROPE]) for j in range(3)])
        gate_bc = [self.place("mod_gate_x", [P, DM]), self.place("mod_gate_ctx", [P, DM])]
        gl = [self.small.load(gate_bc[q][:, :], self.gate_rows[0][q, :].partition_broadcast(P), after=fence + self.gate_stored) for q in range(2)]
        body = self.at
        scale = float((NOPE + LROPE) ** -0.5)
        tiny = self.tiny
        sizes = tiny[:, 128:256]
        stat = Ring([(sizes[:, 2 * j:2 * j + 1], sizes[:, 2 * j + 1:2 * j + 2]) for j in range(4)])
        last_use = []

        for g in range(4):
            heads = {}

            def turned(z, r, t, dst, what):
                b, = self.some_banks(1)

                def tr(e):
                    for h in range(4):
                        e.transpose(b.buf[0:96, h * P:(h + 1) * P], z.buf[:, h, :], self.ident)
                tt = pe.step(tr, [r] + b.free)
                o = act.step(lambda e: e.activation(dst[:, :, t * P:(t + 1) * P], b.buf[0:96, :].rearrange("p (h t) -> p h t", h=4), ACT.Copy), [tt] + last_use)
                b.free, z.free = [o], [tt]
                heads[what, t] = o

            def evac_q(t, bank, made):
                z = tok.take()
                a = act.step(lambda e: e.activation(z.buf[:, :, :], bank.rearrange("p (h d) -> p h d", h=4), ACT.Copy), [made] + z.free)
                r = a
                if t < XT:
                    dve.pending.append(a)
                    r = self.axial(z.buf[:, :, NOPE:], z.buf[:, :, NOPE:], t, 4)
                self.defer(lambda: turned(z, r, t, qT, "q"))
                return [a]

            def evac_kv(t, bank, made):
                z = tok.take()
                b4 = bank.rearrange("p (h d) -> p h d", h=4)
                a = act.step(lambda e: e.activation(z.buf[:, :, 0:NOPE], b4[:, :, 0:NOPE], ACT.Copy), [made] + z.free)
                d = dve.step(lambda e: e.tensor_copy(z.buf[:, :, NOPE:], krot[:, t, :].unsqueeze(1).broadcast_to([P, 4, LROPE])), z.free)
                d2 = dve.step(lambda e: e.tensor_copy(v[:, t, :, :], b4[:, :, NOPE:]), [a] + last_use)
                heads["v", t] = d2
                self.defer(lambda: turned(z, d2, t, kT, "k"))
                return [d2]
            for name, src, kn, w, ev, made in (("uq", cq, 3, 384, evac_q, cq_ready), ("ukv", ckv, 2, 512, evac_kv, ckv_ready)):
                for _ in self.to_tokens([(f"{name}.{g}", 0, kn)], [(src, t) for t in range(T)], w, self.some_banks(T), ev, made):
                    pass
            self.flush()
            banks = self.banks
            pair = lambda b: self.ps[:, b:b + 2, :].rearrange("p b n -> p (b n)")
            s_turn = [0]
            state = {}

            def scores(u):
                h, t = units[u]
                b = 2 * (u % 2)
                s = pair(b)
                n, k0 = (768, 0) if t < XT else (CTX, SEQ)
                need = [heads["q", t]] + [heads["k", j] for j in range(k0 // P, T)] + banks[b].free + banks[b + 1].free

                def mm(e):
                    for lo in range(0, n, 512):
                        w = min(512, n - lo)
                        e.matmul(s[:, lo:lo + w], qT[:, h, t * P:(t + 1) * P], kT[:, h, k0 + lo:k0 + lo + w], start=True, stop=True)
                m = pe.step(mm, need)
                st = stat.take()
                mx, ls = st.buf
                dve.step(lambda e: e.tensor_reduce(mx, s[:, 0:n], AX_X, ALU.max), [m] + st.free)
                d = dve.step(lambda e: e.tensor_scalar(mx, mx, -scale, None, ALU.mult))
                p = prob.take()
                a = act.step(lambda e: e.activation(p.buf[:, 0:n], s[:, 0:n], ACT.Exp, bias=mx, scale=scale, accum_out=ls), [d] + p.free)
                banks[b].free = banks[b + 1].free = [a]
                state[u] = (p, n, k0, st, a)

            def turn(u):
                p, n, k0, st, a = state[u]
                s = pair(4)

                def tr(e):
                    for j in range(n // P):
                        e.transpose(s[:, j * P:(j + 1) * P], p.buf[:, j * P:(j + 1) * P], self.ident)
                t = pe.step(tr, [a] + banks[4].free + banks[5].free)
                p.free = [t]
                q = probT.take()
                w = min(n, 512)
                d = dve.step(lambda e: e.tensor_copy(q.buf[:, 0:w], s[:, 0:w]), [t] + q.free)
                copied = [d]
                if n > 512:
                    a2 = act.step(lambda e: e.activation(q.buf[:, 512:n], s[:, 512:n], ACT.Copy), [t] + q.free)
                    copied.append(a2)
                    banks[5].free = [a2]
                banks[4].free = [d]
                state[u] = (q, n, k0, st, a, copied)

            def values(u):
                h, t = units[u]
                q, n, k0, st, a, copied = state[u]
                ob = banks[6 + u % 2]

                def pv(e):
                    for j in range(n // P):
                        e.matmul(ob.buf[:, 0:LV], q.buf[:, j * P:(j + 1) * P], v[:, k0 // P + j, h, :], start=(j == 0), stop=(j == n // P - 1))
                m = pe.step(pv, copied + [heads["v", j] for j in range(k0 // P, T)] + ob.free)
                q.free = [m]
                ls = st.buf[1]
                dve.step(lambda e: e.reciprocal(ls, ls), [a])
                col = slice((4 * g + h) * LV, (4 * g + h + 1) * LV)
                d = dve.step(lambda e: e.scalar_tensor_tensor(gate[:, t, col], ob.buf[:, 0:LV], ls, gate[:, t, col], ALU.mult, ALU.mult), [m])
                ob.free, st.free = [d], [d]
            units = [(h, t) for h in range(4) for t in range(T)]
            for s in range(len(units) + 2):
                if s < len(units):
                    scores(s)
                if 1 <= s <= len(units):
                    turn(s - 1)
                if s >= 2:
                    values(s - 2)
            last_use = [pe.now()]

        self.fence()
        self.at = self.hx_at
        oT = Split(self.place("mla_oT_hi", [P, KT, 768], F32R), self.place("mla_oT_lo", [P, KT, 768], F32R))
        assert self.at <= self.after_hc
        ready = self.to_feature_major([gate[:, t, :] for t in range(T)], oT)
        self.fence()
        pe.pending = []
        self.at = body
        gated = Ring([self.place(f"gated_out{j}", [P, 512]) for j in range(2)])
        self.junk = self.place("mla_out_junk", [P, DM])
        for g in range(2):
            def evac_o(t, bank, made):
                sl = slice(g * 512, (g + 1) * 512)
                z = gated.take()
                whole = self.x[:, t, :] if t < XT else self.ctx_res[:, t - XT, :]
                res = whole[:, sl]
                gb = gate_bc[0 if t < XT else 1]
                d = dve.step(lambda e: e.tensor_tensor(z.buf[:, :], bank, gb[:, sl], ALU.mult), [made] + gl + z.free)
                d2 = dve.step(lambda e: e.tensor_tensor(res, res, z.buf[:, :], ALU.add))
                z.free = [d2]
                if g == 1:
                    self.square(t, whole, [d2])
                return [d]
            for _ in self.to_tokens([(f"mla_o{g}.{i}", 4 * i, 4) for i in range(2)], [(oT, t) for t in range(T)], 512, self.some_banks(T), evac_o, ready):
                pass

    def axial(self, src, dst, t, heads):
        dve = self.dve
        at = C_AX + t * 64
        co = self.cst[:, at:at + 32].unsqueeze(1).broadcast_to([P, heads, 32])
        si = self.cst[:, at + 32:at + 64].rearrange("p (f c d) -> p f c d", f=2, c=2)
        tmp = self.rope_tmp[:, 0:heads * 32].rearrange("p (h d) -> p h d", h=heads)
        for f in range(2):
            for half in range(2):
                a, b = f * 16 + 8 * half, f * 16 + 8 * (1 - half)
                dve.step(lambda e: e.tensor_tensor(tmp[:, :, a:a + 8], src[:, :, b:b + 8], si[:, f, half, :].unsqueeze(1).broadcast_to([P, heads, 8]), ALU.mult))
        dve.step(lambda e: e.tensor_tensor(dst, src, co, ALU.mult))
        return dve.step(lambda e: e.tensor_tensor(dst, dst, tmp, ALU.add))

    def to_feature_major(self, tiles, dst):
        n, made = len(tiles), {}
        for k in range(KT):
            for lo in range(0, n, 4):
                m = min(4, n - lo)
                b, = self.some_banks(1)

                def tr(e):
                    for j in range(m):
                        e.transpose(b.buf[:, j * P:(j + 1) * P], tiles[lo + j][:, k * P:(k + 1) * P], self.ident)
                t = self.pe.step(tr, b.free)
                b.free = self.put_split(dst, (slice(None), k, slice(lo * P, (lo + m) * P)), b.buf[:, 0:m * P], [t])
            made[k] = [self.act.now(), self.dve.now()]
        return made

    def gla(self):
        pe, dve, act, pool, c, cols, cst = self.pe, self.dve, self.act, self.pool, self.c, self.cols, self.cst
        T = XT + CT
        marks = self.fence()
        hc_at = self.hc_at
        self.hc = Split(self.nc.alloc_sbuf_tensor_at("gla_hc_hi", [P, KT, CTX], F32R, offset=hc_at),
                        self.nc.alloc_sbuf_tensor_at("gla_hc_lo", [P, KT, CTX], F32R, offset=hc_at + KT * CTX * 4))
        self.at = self.after_hc
        v = self.place("gla_v", [P, T, DM])
        body = self.at
        gate_bc = self.place("gla_mod_gate", [P, DM])
        gl = self.small.load(gate_bc[:, :], self.gate_rows[1][0, :].partition_broadcast(P), after=marks + self.gate_stored)
        q = self.place("gla_q", [P, GH, SEQ])
        kept = self.at
        ready = self.modulated_norm(1)
        assert self.at <= self.top
        self.at = kept
        k = self.place("gla_k", [P, GH, 768])
        cum = [self.place("gla_decay_fwd", [P, GH, T, GC + 1]), self.place("gla_decay_bwd", [P, GH, T, GC + 1])]
        end = self.at
        self.at = self.after_hc
        lin = self.place("gla_gate_lin", [P, 2, GH, 768])
        self.at = end
        rT = self.place("gla_rankT", [2 * GRANK, 768])
        wg = self.place("gla_gate_w", [2 * GRANK, 2, GH * GDK])
        ones = self.place("gla_ones", [P, P])
        marks = self.fence()
        pe.pending = []
        z = pool.step(lambda e: e.memset(wg[:, :, :], 0.0))
        z1 = pool.step(lambda e: e.memset(ones[:, :], 1.0))
        for d_ in range(2):
            pool.step(lambda e: e.memset(cum[d_][:, :, :, 0:1], 0.0))
        w1 = self.small.load(wg[0:GRANK, 0, :], self.ins["gla_w_gf_2"][0], after=[z])
        w2 = self.small.load(wg[GRANK:2 * GRANK, 1, :], self.ins["gla_w_gb_2"][0], after=[z])
        srcs = [(self.hx, t) for t in range(XT)] + [(self.hc, t) for t in range(CT)]
        span = lambda cx, w: slice(0, w) if cx == 0 else slice(SEQ, SEQ + w)
        for _ in self.to_both([(f"gla_r.{i}", 4 * i, 4) for i in range(2)], (self.hx, self.hc), self.some_banks(2),
                              lambda m, cx, bank, made: [act.step(lambda e: e.activation(rT[:, span(cx, bank.shape[1])], bank, ACT.Copy), [made])],
                              ready, 1, 2 * GRANK):
            pass
        r_ready = act.now()
        for d_ in range(2):
            for m in range(GH):
                for cx, n in ((0, SEQ), (1, CTX)):
                    b, = self.some_banks(1)
                    t = pe.step(lambda e: e.matmul(b.buf[:, 0:n], wg[:, d_, m * P:(m + 1) * P], rT[:, span(cx, n)], start=True, stop=True), [r_ready, w1, w2] + b.free)
                    bc = cols[:, c["gla_b"] + 4 * d_ + m:c["gla_b"] + 4 * d_ + m + 1]
                    if m % 2:
                        b.free = [dve.step(lambda e: e.tensor_scalar(lin[:, d_, m, span(cx, n)], b.buf[:, 0:n], bc, None, ALU.add), [t])]
                    else:
                        b.free = [act.step(lambda e: e.activation(lin[:, d_, m, span(cx, n)], b.buf[:, 0:n], ACT.Identity, bias=bc), [t])]
        lin_made = [act.now(), dve.now()]

        def decays():
            for d_ in range(2):
                body4 = lambda m: cum[d_][:, m, :, 1:GC + 1]
                src = lambda m: lin[:, d_, m, :].rearrange("p (t n) -> p t n", t=T)
                for pair in ((0, 1), (2, 3)):
                    for m in pair:
                        act.step(lambda e: e.activation(body4(m), src(m), ACT.Abs), lin_made)
                        act.step(lambda e: e.activation(body4(m), body4(m), ACT.Exp, scale=-1.0))
                        yield
                    for m in pair:
                        a = act.step(lambda e: e.activation(body4(m), body4(m), ACT.Ln, bias=1.0))
                        dve.step(lambda e: e.scalar_tensor_tensor(body4(m), src(m), 0.0, body4(m), ALU.min, ALU.subtract), [a] + lin_made)
                        for ch in range(T):
                            dve.step(lambda e: e.tensor_tensor_scan(cum[d_][:, m, ch, 1:GC + 1], ones[:, :], cum[d_][:, m, ch, 1:GC + 1], 0.0, ALU.mult, ALU.add), [z1])
                        yield

        def keys_and_queries():
            yield from self.to_both([(f"gla_k.{i}", 4 * i, 4) for i in range(2)], (self.hx, self.hc), self.some_banks(8),
                                    lambda m, cx, bank, made: [act.step(lambda e: e.activation(k[:, m, span(cx, bank.shape[1])], bank, ACT.Copy), [made])], ready)
            yield from self.to_features([(f"gla_q.{i}", 4 * i, 4) for i in range(2)], self.hx, SEQ, self.some_banks(4),
                                        lambda m, bank, made: [act.step(lambda e: e.activation(q[:, m, :], bank, ACT.Copy, scale=GDK ** -0.5), [made])], ready)
        interleave((keys_and_queries(), 1), (decays(), 1))
        pe.pending += [dve.now(), act.now()]
        for g in range(2):
            for _ in self.to_tokens([(f"gla_v{g}.{i}", 4 * i, 4) for i in range(2)], srcs, 512, self.some_banks(T),
                                    lambda t, bank, made: [act.step(lambda e: e.activation(v[:, t, g * 512:(g + 1) * 512], bank, ACT.Copy), [made])], ready):
                pass
        self.fence()
        self.at = self.hc_at
        gate = self.place("gla_gate", [P, XT, DM])
        assert self.at <= self.after_hc
        self.at = end
        S = [self.place("gla_state_fwd", [P, GH, GDV]), self.place("gla_state_bwd", [P, GH, GDV])]
        Kd = [[self.place(f"gla_Kd{h}", [P, P])] for h in range(GH)]
        assert self.at <= self.high_end
        self.at = self.high_end
        tot = self.place("gla_total", [P, 2, GH * T])
        etot = self.place("gla_total_decay", [P, 2, GH * T])
        ref = self.place("gla_reference", [P, 2, GH * T, GC // GB])
        for d_ in range(2):
            dve.step(lambda e: e.tensor_scalar(tot[:, d_, :].rearrange("p (h t) -> p h t", h=GH), cum[d_][:, :, :, GC], 1.0 / GATE_NORM, None, ALU.mult))
            mids = cum[d_][:, :, :, 0:GC].rearrange("p h t (b n) -> p (h t) b n", b=GC // GB)[:, :, :, GB // 2]
            dve.step(lambda e: e.tensor_scalar(ref[:, d_, :, :], mids, (1.0 if d_ == 0 else -1.0) / GATE_NORM, None, ALU.mult))
        act.step(lambda e: e.activation(etot[:, :, :], tot[:, :, :], ACT.Exp), [dve.now()])
        dve.pending.append(act.now())
        masks = [cst[:, C_UP:C_UP + P].bitcast(I32), cst[:, C_LOW:C_LOW + P].bitcast(I32)]
        inv = 1.0 / GATE_NORM
        state_ready = {}
        Kd = [Ring(k_) for k_ in Kd]

        def decayed_keys(d_, h, ch, job):
            fwd, kd, cc = d_ == 0, Kd[h].take(), cum[d_][:, h, ch, :]
            tcol = tot[:, d_, h * T + ch:h * T + ch + 1]
            if fwd:
                a = act.step(lambda e: e.activation(kd.buf[:, :], cc[:, 1:P + 1], ACT.Exp, scale=-inv, bias=tcol), kd.free)
            else:
                a = act.step(lambda e: e.activation(kd.buf[:, :], cc[:, 0:P], ACT.Exp, scale=inv), kd.free)
            m_ = pool.step(lambda e: e.tensor_tensor(kd.buf[:, :], kd.buf[:, :], k[:, h, ch * P:(ch + 1) * P], ALU.mult), [a])
            yield
            b, = self.scan_banks(1)
            t = pe.step(lambda e: e.transpose(b.buf[:, 0:P], kd.buf[:, :], self.ident), [m_] + b.free)
            job["kd"], job["kd_made"] = kd, act.step(lambda e: e.activation(kd.buf[:, :], b.buf[:, 0:P], ACT.Copy), [t])
            b.free = [job["kd_made"]]
            yield

        def update_state(d_, h, ch, job, first, read):
            s_state, kd = S[d_][:, h, :], job["kd"]
            b, = self.scan_banks(1)
            t = pe.step(lambda e: e.matmul(b.buf[:, 0:GDV], kd.buf[:, :], v[:, ch, h * GDV:(h + 1) * GDV], start=True, stop=True), [job["kd_made"]] + b.free)
            kd.free = [t]
            if first:
                s2 = dve.step(lambda e: e.tensor_copy(s_state, b.buf[:, 0:GDV]), [t])
            else:
                et = etot[:, d_, h * T + ch:h * T + ch + 1]
                s2 = dve.step(lambda e: e.scalar_tensor_tensor(s_state, s_state, et, b.buf[:, 0:GDV], ALU.mult, ALU.add), [t] + read)
            b.free = state_ready[d_, h] = [s2]
            yield

        def context_states():
            for n in range(CT):
                for h in range(GH):
                    for d_ in range(2):
                        ch, job = XT + (n if d_ == 0 else CT - 1 - n), {}
                        yield from decayed_keys(d_, h, ch, job)
                        yield from update_state(d_, h, ch, job, n == 0, [])

        def gate_projection():
            for g in range(2):
                yield from self.to_tokens([(f"gla_g{g}.{i}", 4 * i, 4) for i in range(2)], srcs[0:XT], 512, self.banks[0:4],
                                          lambda t, bank, made: [dve.step(lambda e: e.tensor_copy(gate[:, t, g * 512:(g + 1) * 512], bank), [made])], ready)
        self.scan_turn = 0

        def scan_banks(n):
            self.scan_turn += n
            return [self.banks[4 + (self.scan_turn - n + i) % 4] for i in range(n)]
        self.scan_banks = scan_banks
        interleave((context_states(), 3), (gate_projection(), 1))
        self.scan_banks = self.some_banks

        self.fence()
        self.at = self.hx_at
        o = self.place("gla_o", [P, XT, DM])
        two = lambda n, spare: [Ring([self.place(f"{n}{h}", [P, P])[:, :], spare[:, h, :]]) for h in range(GH)]
        Kt = [Ring([self.place(f"gla_Kt{h}", [P, 4, P])]) for h in range(GH)]
        Qt = [Ring([self.place(f"gla_Qt{h}", [P, P])]) for h in range(GH)]
        spare = v[:, XT:T, :].rearrange("p t n -> p (t n)").rearrange("p (a h n) -> p a h n", a=4, h=GH)
        A, Qh = two("gla_A", spare[:, 0, :, :]), two("gla_Qh", spare[:, 1, :, :])
        for h in range(GH):
            Kd[h].slots.append(Slot(spare[:, 2, h, :]))
        assert self.at <= self.hc_at
        o_written = {}
        jobs = {}

        def prepare_chunk(h, n):
            d_, ch, last = order[n]
            fwd, job = d_ == 0, {}
            jobs[h, n] = job
            cc, sh = cum[d_][:, h, ch, :], 1 if d_ == 0 else 0
            tcol = tot[:, d_, h * T + ch:h * T + ch + 1]
            kk, qq = k[:, h, ch * P:(ch + 1) * P], q[:, h, ch * P:(ch + 1) * P]
            kt, qt, qh, at_ = Kt[h].take(), Qt[h].take(), Qh[h].take(), A[h].take()
            if n % len(x_chunks) < 2:
                at_.free = [pool.step(lambda e: e.memset(at_.buf, 0.0), at_.free)]
            rr = ref[:, d_, h * T + ch, :]

            def keys(e):
                for I in range(GC // GB):
                    e.activation(kt.buf[:, I, :], cc[:, sh:sh + P], ACT.Exp, scale=-inv if fwd else inv, bias=rr[:, I:I + 1])
            blocks = lambda ap: ap.rearrange("p (b n) -> p b n", b=GC // GB)
            mid = blocks(cc[:, 0:GC])[:, :, GB // 2:GB // 2 + 1].broadcast_to([P, GC // GB, GB])
            dd = dve.step(lambda e: e.tensor_tensor(blocks(qt.buf[:, :]), blocks(cc[:, sh:sh + P]), mid, ALU.subtract), qt.free)
            a = act.step(keys, kt.free)
            yield
            d1 = dve.step(lambda e: e.tensor_tensor(kt.buf[:, :, :], kt.buf[:, :, :], kk.unsqueeze(1).broadcast_to([P, 4, P]), ALU.mult), [a])
            a2 = act.step(lambda e: e.activation(qt.buf[:, :], qt.buf[:, :], ACT.Exp, scale=inv if fwd else -inv), [dd])
            d2 = dve.step(lambda e: e.tensor_tensor(qt.buf[:, :], qt.buf[:, :], qq, ALU.mult), [a2])
            if fwd:
                a3 = act.step(lambda e: e.activation(qh.buf, cc[:, 1:P + 1], ACT.Exp, scale=inv), qh.free)
            else:
                a3 = act.step(lambda e: e.activation(qh.buf, cc[:, 0:P], ACT.Exp, scale=-inv, bias=tcol), qh.free)
            d3 = pool.step(lambda e: e.tensor_tensor(qh.buf, qh.buf, qq, ALU.mult), [a3])
            yield
            if not last:
                yield from decayed_keys(d_, h, ch, job)
            b, = self.some_banks(1)

            def am(e):
                for I in range(4):
                    e.matmul(b.buf[:, I * GB:(I + 1) * GB], kt.buf[:, I, :], qt.buf[:, I * GB:(I + 1) * GB], start=True, stop=True)
            t = pe.step(am, [d1, d2] + b.free)
            kt.free, qt.free = [t], [t]
            d4 = dve.step(lambda e: e.copy_predicated(at_.buf, masks[d_], b.buf[:, 0:P]), [t] + at_.free)
            b.free = [d4]
            job.update(qh=qh, at=at_, ready=[d3, d4])
            yield

        def finish_chunk(h, n):
            d_, ch, last = order[n]
            job = jobs.pop((h, n))
            qh, at_, s_state = job["qh"], job["at"], S[d_][:, h, :]
            ob, = self.some_banks(1)

            def om(e):
                e.matmul(ob.buf[:, 0:GDV], qh.buf, s_state, start=True, stop=False)
                e.matmul(ob.buf[:, 0:GDV], at_.buf, v[:, ch, h * GDV:(h + 1) * GDV], start=False, stop=True)
            t = pe.step(om, job["ready"] + state_ready[d_, h] + ob.free)
            qh.free, at_.free = [t], [t]
            oc = o[:, ch, h * GDV:(h + 1) * GDV]
            if (ch, h) in o_written:
                dve.step(lambda e: e.tensor_tensor(oc, ob.buf[:, 0:GDV], oc, ALU.add), [t, o_written[ch, h]])
                ob.free = [dve.step(lambda e: e.tensor_tensor_reduce(out=ob.buf[:, GDV:2 * GDV], in0=oc, in1=oc, scale=1.0, scalar=0.0, op0=ALU.mult,
                                                                     op1=ALU.add, accum_out=self.tiny[:, GH * ch + h:GH * ch + h + 1]))]
            else:
                ob.free = [act.step(lambda e: e.activation(oc, ob.buf[:, 0:GDV], ACT.Copy), [t])]
            o_written[ch, h] = ob.free[0]
            yield
            if not last:
                yield from update_state(d_, h, ch, job, False, [t])
        x_chunks = list(range(XT))
        order = [(0, ch, ch == XT - 1) for ch in x_chunks] + [(1, ch, ch == 0) for ch in reversed(x_chunks)]

        def head(h):
            for _ in range(2 * h):
                yield
            yield from prepare_chunk(h, 0)
            for n in range(len(order)):
                live = [finish_chunk(h, n)] + ([prepare_chunk(h, n + 1)] if n + 1 < len(order) else [])
                while live:
                    live = [s for s in live if next(s, live) is not live]
                    yield
        interleave(*[(head(h), 1) for h in range(GH)])

        self.fence()
        self.at = end
        row = self.place("final_gain_row", [P, DM])
        self.junk = self.place("final_junk", [P, DM])
        gated = Ring([self.place(f"gla_gated_out{j}", [P, 512]) for j in range(2)])
        row_ready = self.small.load(row[:, :], self.ins["final_g_2"].partition_broadcast(P), after=[pe.now(), dve.now(), act.now()])
        oT = Split(self.nc.alloc_sbuf_tensor_at("gla_oT_hi", [P, KT, SEQ], F32R, offset=self.after_hc),
                   self.nc.alloc_sbuf_tensor_at("gla_oT_lo", [P, KT, SEQ], F32R, offset=kept))
        rs = self.tiny[:, 0:XT * GH]
        d = dve.step(lambda e: e.tensor_scalar(rs, rs, 1.0 / GDV, EPS, ALU.mult, ALU.add))
        a = act.step(lambda e: e.activation(rs, rs, ACT.Sqrt), [d])
        r_ready = dve.step(lambda e: e.reciprocal(rs, rs), [a])
        tiles = [(oT, t, []) for t in range(XT)]

        def evac_o(g, t, bank, made):
            sl = slice(g * 512, (g + 1) * 512)
            z = gated.take()
            d = dve.step(lambda e: e.tensor_tensor(z.buf[:, :], bank, gate_bc[:, sl], ALU.mult), [made, gl] + z.free)
            d2 = dve.step(lambda e: e.tensor_tensor(self.x[:, t, sl], self.x[:, t, sl], z.buf[:, :], ALU.add))
            z.free = [d2]
            if g == 1:
                self.square(t, self.x[:, t, :], [d2])
                squared.append(act.now())
                if t > 0:
                    finish_tile(t - 1)
            return [d]

        def finish_tile(t):
            r = self.tiny[:, t:t + 1]
            d = dve.step(lambda e: e.tensor_scalar(r, r, 1.0 / DM, EPS, ALU.mult, ALU.add), [squared[t]])
            a = act.step(lambda e: e.activation(r, r, ACT.Sqrt), [d])
            dve.step(lambda e: e.reciprocal(r, r), [a])
            d = dve.step(lambda e: e.scalar_tensor_tensor(self.x[:, t, :], self.x[:, t, :], r, row[:, :], ALU.mult, ALU.mult), [row_ready])
            self.stored.append(self.sp.load(self.out[t * P:(t + 1) * P, :], self.x[:, t, :], after=[d]))
        squared = []
        products = [self.to_tokens([(f"gla_o{g}.{i}", 4 * i, 4) for i in range(2)], tiles, 512, self.banks[4 * g:4 * g + 4],
                                   lambda t, bank, made, g=g: evac_o(g, t, bank, made)) for g in range(2)]
        silu = [act.step(lambda e: e.activation(gate[:, 0, :], gate[:, 0, :], ACT.Silu))]
        for t in range(XT):
            if t + 1 < XT:
                silu.append(act.step(lambda e: e.activation(gate[:, t + 1, :], gate[:, t + 1, :], ACT.Silu)))
            for h in range(GH):
                sl = slice(h * GDV, (h + 1) * GDV)
                d = dve.step(lambda e: e.scalar_tensor_tensor(gate[:, t, sl], o[:, t, sl], rs[:, 4 * t + h:4 * t + h + 1], gate[:, t, sl], ALU.mult, ALU.mult), [silu[t], r_ready])
            for odd in range(2):
                b = self.banks[4 + (2 * t + odd) % 4]

                def tr(e):
                    for j in range(4):
                        k_ = 2 * j + odd
                        e.transpose(b.buf[:, j * P:(j + 1) * P], gate[:, t, k_ * P:(k_ + 1) * P], self.ident)
                tt = pe.step(tr, [d] + b.free)
                gain = cols[:, c["o_norm"] + odd:c["o_norm"] + odd + 1]
                b.free = self.put_split(oT, (slice(None), slice(odd, KT, 2), slice(t * P, (t + 1) * P)), b.buf[:, :].rearrange("p (k t) -> p k t", k=4), [tt], gain)
            tiles[t][2].extend(b.free)
            if t > 0:
                next(products[0])
        for g in range(2):
            for _ in products[g]:
                pass
        finish_tile(XT - 1)

    def units(self, name, a, c0, n=512, k0=0, kn=8, per=4, raw=False):
        v = a.rearrange("(k p) n -> p k n", p=P)
        if kn <= per:
            return [(name, v[:, k0:k0 + kn, c0:c0 + n], kn, n, raw)]
        return [(f"{name}.{i}", v[:, k0 + i * per:k0 + (i + 1) * per, c0:c0 + n], per, n, raw) for i in range(kn // per)]

    def second_plan(self, mla=True, gla=True):
        ins, plan = self.ins, []
        if mla:
            w = ins["mla_w_in_2"][0]
            for n, c0, cn in (("l0", 0, 512), ("l1", 512, 160), ("g0", LAT, 512), ("g1", LAT + 512, 512)):
                plan += self.units(f"mla_{n}", w, c0, cn)
            for g in range(4):
                plan += self.units(f"uq.{g}", ins["mla_w_uq_2"][0], 384 * g, 384, kn=3)
                plan += self.units(f"ukv.{g}", ins["mla_w_ukv_2"][0], 512 * g, kn=2)
            for g in range(2):
                plan += self.units(f"mla_o{g}", ins["mla_w_out_2"][0], 512 * g)
        if gla:
            w = ins["gla_w_in_2"][0]
            plan += self.units("gla_r", w, 3072, 32)
            plan += self.units("gla_k", w, 512)
            plan += self.units("gla_q", w, 0)
            for n, c0 in (("v", 1024), ("g", 2048)):
                for g in range(2):
                    plan += self.units(f"gla_{n}{g}", w, c0 + 512 * g)
            for g in range(2):
                plan += self.units(f"gla_o{g}", ins["gla_w_out_2"][0], 512 * g)
        return plan


def build(nc, ins, out):
    with ExitStack() as ctx:
        p = Program(nc, ins, out, ctx)
        p.setup()
        plan = []
        for l in range(DEPTH):
            plan += p.layer_plan(l)
        plan += p.second_plan()
        p.plan_weights(plan)
        for l in range(DEPTH):
            p.layer(l)
        p.norm_between()
        p.mla()
        p.gla()
        block = ctx.enter_context(nc.Block())

        @block.sync
        def _(e):
            emit(e, p.sp_queue)
            for sem, count in p.stored:
                e.wait_ge(sem, count)

        @block.gpsimd
        def _(e):
            emit(e, p.pool.queue)

        @block.scalar
        def _(e):
            emit(e, p.act.queue)

        @block.vector
        def _(e):
            emit(e, p.dve.queue)

        @block.tensor
        def _(e):
            emit(e, p.pe.queue)


_INS = ['x', 'positions', 'norm_mix_w', 'w_in', 'b_in', 'conv_w', 'conv_b', 'mlstm_norm_w', 'w_proj_att',
        'w_proj_mlstm', 'w_out', 'norm_mlp_w', 'w_ff1', 'w_ff2', 'final_norm_w', 'c_2', 'ctx_2', 'c_ctx_2', 'ada_w_2',
        'ada_b_2', 'norm_g_2', 'final_g_2', 'mla_w_in_2', 'mla_q_norm_2', 'mla_w_uq_2', 'mla_kv_norm_2',
        'mla_w_ukv_2', 'mla_w_out_2', 'gla_w_in_2', 'gla_w_gf_2', 'gla_b_gf_2', 'gla_w_gb_2', 'gla_b_gb_2',
        'gla_o_norm_2', 'gla_w_out_2']


def kernel(**inputs):
    import numpy as _np
    import concourse.bacc as _bacc
    from concourse import mybir as _mybir
    from concourse.bass_utils import run_bass_kernel_spmd as _run

    nc = _bacc.Bacc("TRN2", target_bir_lowering=False, num_devices=1)
    arrays, ins = {}, {}
    for name in _INS:
        arrays[f"in_{name}"] = _np.ascontiguousarray(inputs[name])
    arrays["in_constants"] = constants()
    for name, a in arrays.items():
        ins[name[3:]] = nc.dram_tensor(name, a.shape, _mybir.dt.from_np(a.dtype), kind="ExternalInput").ap()
    out = nc.dram_tensor("out_x", (SEQ, DM), _mybir.dt.float32, kind="ExternalOutput").ap()
    build(nc, ins, out)
    r = _run(nc, [arrays], core_ids=[0])
    return r.results[0]["out_x"].reshape(1, SEQ, DM)
```
